# Optimizing a Trainium2 kernel written in Bass

```python
import math
import jax, jax.numpy as jnp
from jax import lax
import numpy as np

"""Hybrid bidirectional encoder trunk (Hymba-style parallel head groups, post-LN DeepNorm).

Each layer:
  proj = x @ w_in  -> columns split among three head groups:
    A: windowed GQA (|t-s|<=128) with per-head sink logit + ALiBi   (8 q heads, 2 kv heads)
    B: 2-D neighbourhood attention on a (ROWS x 64) grid, window min(8,ROWS) x 16,
       learned per-head 2-D relative position bias                    (4 heads)
    M: cross-attention into 256 memory tokens (k/v from mem)          (4 heads)
  group outputs -> per-group RMSNorm with gain -> concat -> w_out
  x <- LayerNorm(alpha*x + mix(x))
  x <- LayerNorm(alpha*x + MoE(x))   (router shared over all layers, group-limited top-2)
Inputs : x_prompt (BATCH,SEQ,D), x_sample (DEC_BATCH,DEC_SEQ,D),
         mem_prompt (BATCH,256,D), mem_sample (DEC_BATCH,256,D), weights.
Outputs: (y_prompt (BATCH,SEQ,D), y_sample (DEC_BATCH,DEC_SEQ,D)).
"""

D_MODEL = 1024
BATCH = 1
SEQ = 512
DEPTH = 1
DEC_BATCH = 1
DEC_SEQ = 512
PAST_LEN = 128

HEAD_DIM = 64
A_HEADS = 8
A_KV_HEADS = 2
WINDOW = 128
BLOCK = 128
B_HEADS = 4
GRID_W = 64
NA_ROWS = 8
NA_COLS = 16
M_HEADS = 4
MEM_LEN = 256
N_EXPERTS = 16
N_GROUPS = 4
TOP_K = 2
D_EXPERT = 512
LN_EPS = 1e-5

A_Q_W = A_HEADS * HEAD_DIM
A_KV_W = A_KV_HEADS * HEAD_DIM
B_W = B_HEADS * HEAD_DIM
M_W = M_HEADS * HEAD_DIM
MIX_W = A_Q_W + B_W + M_W
IN_W = A_Q_W + 2 * A_KV_W + 3 * B_W + M_W
DEEPNORM_ALPHA = (2 * DEPTH) ** 0.25
DEEPNORM_BETA = (8 * DEPTH) ** -0.25
ATTN_SCALE = HEAD_DIM ** -0.5

kernel_name = "hymba_style_hybrid_encoder"

def layer_norm(x, g, b):
    xf = x.astype(jnp.float32)
    mu = jnp.mean(xf, -1, keepdims=True)
    xc = xf - mu
    var = jnp.mean(xc * xc, -1, keepdims=True)
    return (xc * lax.rsqrt(var + LN_EPS) * g.astype(jnp.float32) + b.astype(jnp.float32)).astype(x.dtype)

def group_rms(o, g):
    of = o.astype(jnp.float32)
    return (of * lax.rsqrt(jnp.mean(of * of, -1, keepdims=True) + LN_EPS) * g.astype(jnp.float32)).astype(o.dtype)

def alibi_slopes(n):
    return jnp.exp2(-8.0 * jnp.arange(1, n + 1, dtype=jnp.float32) / n)

def window_attention(q, k, v, sink):
    B, S = q.shape[0], q.shape[1]
    nb = S // BLOCK
    G = A_HEADS // A_KV_HEADS
    qb = q.reshape(B, nb, BLOCK, A_KV_HEADS, G, HEAD_DIM)
    pad = ((0, 0), (BLOCK, BLOCK), (0, 0), (0, 0))

    def bands(t):
        tp = jnp.pad(t, pad).reshape(B, nb + 2, BLOCK, A_KV_HEADS, HEAD_DIM)
        return jnp.concatenate([tp[:, :-2], tp[:, 1:-1], tp[:, 2:]], axis=2)

    kb, vb = bands(k), bands(v)
    s = jnp.einsum('bnqhgd,bnkhd->bnhgqk', qb, kb, preferred_element_type=jnp.float32) * ATTN_SCALE
    a = jnp.arange(BLOCK)
    j = jnp.arange(3 * BLOCK)
    dist = a[:, None] + BLOCK - j[None, :]
    kpos = jnp.arange(nb)[:, None] * BLOCK - BLOCK + j[None, :]
    valid = (jnp.abs(dist) <= WINDOW)[None] & ((kpos >= 0) & (kpos < S))[:, None, :]
    slopes = alibi_slopes(A_HEADS).reshape(A_KV_HEADS, G)[:, :, None, None]
    s = s - slopes * jnp.abs(dist).astype(jnp.float32)
    s = jnp.where(valid[None, :, None, None], s, -jnp.inf)
    sk = sink.astype(jnp.float32).reshape(A_KV_HEADS, G)[:, :, None, None]
    m = jnp.maximum(jnp.max(s, -1, keepdims=True), sk)
    p = jnp.exp(s - m)
    p = p / (jnp.sum(p, -1, keepdims=True) + jnp.exp(sk - m))
    o = jnp.einsum('bnhgqk,bnkhd->bnqhgd', p.astype(v.dtype), vb)
    return o.reshape(B, S, A_Q_W)

def neighborhood_attention(q, k, v, rpb):
    B, S = q.shape[0], q.shape[1]
    rows = S // GRID_W
    kh = min(NA_ROWS, rows)
    qg = q.reshape(B, rows, GRID_W, B_HEADS, HEAD_DIM)
    kg = k.reshape(B, rows, GRID_W, B_HEADS, HEAD_DIM)
    vg = v.reshape(B, rows, GRID_W, B_HEADS, HEAD_DIM)
    r = jnp.arange(rows)
    c = jnp.arange(GRID_W)
    row_start = jnp.clip(r - kh // 2, 0, rows - kh)
    col_idx = jnp.clip(c - NA_COLS // 2, 0, GRID_W - NA_COLS)[:, None] + jnp.arange(NA_COLS)[None]
    dc_idx = col_idx - c[:, None] + NA_COLS - 1
    rpb_f = rpb.astype(jnp.float32)

    def one_row(ri):
        rs = row_start[ri]
        qr = lax.dynamic_index_in_dim(qg, ri, axis=1, keepdims=False)
        kr = lax.dynamic_slice_in_dim(kg, rs, kh, axis=1)[:, :, col_idx]
        vr = lax.dynamic_slice_in_dim(vg, rs, kh, axis=1)[:, :, col_idx]
        dr_idx = rs + jnp.arange(kh) - ri + NA_ROWS - 1
        bias = rpb_f[:, dr_idx[:, None, None], dc_idx[None]]
        s = jnp.einsum('bchd,bicjhd->bhicj', qr, kr, preferred_element_type=jnp.float32) * ATTN_SCALE + bias
        p = jax.nn.softmax(s, axis=(2, 4))
        return jnp.einsum('bhicj,bicjhd->bchd', p.astype(vr.dtype), vr)

    o = lax.map(one_row, r)
    return o.transpose(1, 0, 2, 3, 4).reshape(B, S, B_W)

def memory_attention(q, mk, mv):
    B, S = q.shape[0], q.shape[1]
    s = jnp.einsum('bshd,bmhd->bhsm', q, mk, preferred_element_type=jnp.float32) * ATTN_SCALE
    p = jax.nn.softmax(s, axis=-1)
    o = jnp.einsum('bhsm,bmhd->bshd', p.astype(mv.dtype), mv)
    return o.reshape(B, S, M_W)

def grouped_moe(x, w_router, router_bias, w_gate, w_up, w_down):
    B, S, D = x.shape
    xf = x.reshape(B * S, D)
    scores = jax.nn.sigmoid(jnp.dot(xf, w_router, preferred_element_type=jnp.float32))
    sel = scores + router_bias.astype(jnp.float32)
    eg = N_EXPERTS // N_GROUPS
    grp_score = jnp.sum(lax.top_k(sel.reshape(-1, N_GROUPS, eg), TOP_K)[0], -1)
    gmask = jnp.argmax(grp_score, -1)[:, None] == jnp.arange(N_GROUPS)[None]
    emask = jnp.repeat(gmask, eg, axis=1)
    _, idx = lax.top_k(jnp.where(emask, sel, -jnp.inf), TOP_K)
    w = jnp.take_along_axis(scores, idx, -1)
    w = w / jnp.sum(w, -1, keepdims=True)
    combine = jnp.einsum('nk,nke->ne', w, jax.nn.one_hot(idx, N_EXPERTS, dtype=jnp.float32))
    y = jnp.zeros((B * S, D), jnp.float32)
    for e in range(N_EXPERTS):
        h = jax.nn.silu(jnp.dot(xf, w_gate[e])) * jnp.dot(xf, w_up[e])
        y = y + combine[:, e:e + 1] * jnp.dot(h, w_down[e], preferred_element_type=jnp.float32)
    return y.astype(x.dtype).reshape(B, S, D)

def encoder_layer(x, mem, w_in, w_mem_kv, sink, rpb, grp_g, w_out, ln1_g, ln1_b,
                  w_router, router_bias, w_gate, w_up, w_down, ln2_g, ln2_b):
    B, S, _ = x.shape
    proj = jnp.dot(x, w_in)
    o1 = A_Q_W
    o2 = o1 + A_KV_W
    o3 = o2 + A_KV_W
    o4 = o3 + B_W
    o5 = o4 + B_W
    o6 = o5 + B_W
    qa, ka, va, qb, kb, vb, qm = jnp.split(proj, [o1, o2, o3, o4, o5, o6], axis=-1)
    mkv = jnp.dot(mem, w_mem_kv)
    mk, mv = jnp.split(mkv, 2, axis=-1)
    Mn = mem.shape[1]
    oa = window_attention(qa.reshape(B, S, A_HEADS, HEAD_DIM),
                          ka.reshape(B, S, A_KV_HEADS, HEAD_DIM),
                          va.reshape(B, S, A_KV_HEADS, HEAD_DIM), sink)
    ob = neighborhood_attention(qb.reshape(B, S, B_HEADS, HEAD_DIM),
                                kb.reshape(B, S, B_HEADS, HEAD_DIM),
                                vb.reshape(B, S, B_HEADS, HEAD_DIM), rpb)
    om = memory_attention(qm.reshape(B, S, M_HEADS, HEAD_DIM),
                          mk.reshape(B, Mn, M_HEADS, HEAD_DIM),
                          mv.reshape(B, Mn, M_HEADS, HEAD_DIM))
    mixed = jnp.concatenate([group_rms(oa, grp_g[:A_Q_W]),
                             group_rms(ob, grp_g[A_Q_W:A_Q_W + B_W]),
                             group_rms(om, grp_g[A_Q_W + B_W:])], axis=-1)
    x = layer_norm(DEEPNORM_ALPHA * x + jnp.dot(mixed, w_out), ln1_g, ln1_b)
    x = layer_norm(DEEPNORM_ALPHA * x + grouped_moe(x, w_router, router_bias, w_gate, w_up, w_down), ln2_g, ln2_b)
    return x

def setup_inputs(seed: int = 0) -> dict:
    key = jax.random.key(seed)
    ks = jax.random.split(key, 20)
    f32 = jnp.float32
    sd = D_MODEL ** -0.5
    nrm = lambda k, shp: jax.random.normal(k, shp, f32)
    col_scale = np.ones((IN_W,), np.float32)
    col_scale[A_Q_W + A_KV_W:A_Q_W + 2 * A_KV_W] = DEEPNORM_BETA
    vb0 = A_Q_W + 2 * A_KV_W + 2 * B_W
    col_scale[vb0:vb0 + B_W] = DEEPNORM_BETA
    mem_scale = np.concatenate([np.ones((M_W,), np.float32), np.full((M_W,), DEEPNORM_BETA, np.float32)])
    return {
        "x_prompt": nrm(ks[0], (BATCH, SEQ, D_MODEL)),
        "x_sample": nrm(ks[1], (DEC_BATCH, DEC_SEQ, D_MODEL)),
        "mem_prompt": nrm(ks[2], (BATCH, MEM_LEN, D_MODEL)),
        "mem_sample": nrm(ks[3], (DEC_BATCH, MEM_LEN, D_MODEL)),
        "w_in": nrm(ks[4], (DEPTH, D_MODEL, IN_W)) * sd * jnp.asarray(col_scale),
        "w_mem_kv": nrm(ks[5], (DEPTH, D_MODEL, 2 * M_W)) * sd * jnp.asarray(mem_scale),
        "sink_logits": nrm(ks[6], (DEPTH, A_HEADS)) * 0.5,
        "rpb": nrm(ks[7], (DEPTH, B_HEADS, 2 * NA_ROWS - 1, 2 * NA_COLS - 1)) * 0.02,
        "grp_norm_g": 1.0 + 0.02 * nrm(ks[8], (DEPTH, MIX_W)),
        "w_out": nrm(ks[9], (DEPTH, MIX_W, D_MODEL)) * (MIX_W ** -0.5) * DEEPNORM_BETA,
        "ln1_g": 1.0 + 0.02 * nrm(ks[10], (DEPTH, D_MODEL)),
        "ln1_b": 0.02 * nrm(ks[11], (DEPTH, D_MODEL)),
        "w_router": nrm(ks[12], (D_MODEL, N_EXPERTS)) * sd,
        "router_bias": 0.01 * nrm(ks[13], (N_EXPERTS,)),
        "w_gate": nrm(ks[14], (DEPTH, N_EXPERTS, D_MODEL, D_EXPERT)) * sd,
        "w_up": nrm(ks[15], (DEPTH, N_EXPERTS, D_MODEL, D_EXPERT)) * sd * DEEPNORM_BETA,
        "w_down": nrm(ks[16], (DEPTH, N_EXPERTS, D_EXPERT, D_MODEL)) * (D_EXPERT ** -0.5) * DEEPNORM_BETA,
        "ln2_g": 1.0 + 0.02 * nrm(ks[17], (DEPTH, D_MODEL)),
        "ln2_b": 0.02 * nrm(ks[18], (DEPTH, D_MODEL)),
    }

def reference(x_prompt, x_sample, mem_prompt, mem_sample, w_in, w_mem_kv, sink_logits, rpb,
              grp_norm_g, w_out, ln1_g, ln1_b, w_router, router_bias, w_gate, w_up, w_down,
              ln2_g, ln2_b):
    def trunk(x, mem):
        for l in range(DEPTH):
            x = encoder_layer(x, mem, w_in[l], w_mem_kv[l], sink_logits[l], rpb[l], grp_norm_g[l],
                              w_out[l], ln1_g[l], ln1_b[l], w_router, router_bias,
                              w_gate[l], w_up[l], w_down[l], ln2_g[l], ln2_b[l])
        return x

    y_prompt = trunk(x_prompt, mem_prompt)
    y_sample = trunk(x_sample, mem_sample)
    return (y_prompt, y_sample)


_drawn_inputs = setup_inputs


def setup_inputs(seed=0):
    import zlib

    import numpy as np

    out = dict(_drawn_inputs(seed))
    spreads = {}
    factors = {'rpb': 5.489, 'grp_norm_g': 3.693, 'ln2_g': 2.877, 'ln2_b': 2.903}
    for name, (base, spread) in spreads.items():
        noise = np.random.default_rng([zlib.crc32(name.encode()), seed]).standard_normal(out[name].shape)
        drawn = base * np.exp(spread * noise) if base else spread * noise
        out[name] = __import__('jax').numpy.asarray(drawn.astype(out[name].dtype))
    for name, factor in factors.items():
        out[name] = (out[name] * factor).astype(out[name].dtype)
    return out
```

```python
from contextlib import ExitStack

import concourse.bass as bass
from concourse import mybir

F32 = mybir.dt.float32
F32R = mybir.dt.float32r
BF16 = mybir.dt.bfloat16
I32 = mybir.dt.int32
ALU = mybir.AluOpType
ACT = mybir.ActivationFunctionType
AX = mybir.AxisListType

P = 128
D = 1024
KD = D // P
S = 512
NSEQ = 2
NT = S // P
TT = NSEQ * NT
HD = 64
A_HEADS, B_HEADS, M_HEADS = 8, 4, 4
WINDOW = 128
GRID_W, ROWS, NA_ROWS, NA_COLS = 64, 8, 8, 16
BW = 32
WIN0 = (0, 8, 24, 32)
MEM = 256
NE, NG, EG = 16, 4, 4
FE = 512
KF = FE // P
EPS = 1e-5
ALPHA = 2.0 ** 0.25
SCALE = HD ** -0.5
MASKED = -1.0e30
SLOTS = 32
A_Q, A_KV, B_W, M_W = 512, 128, 256, 256
IN_W = A_Q + 2 * A_KV + 3 * B_W + M_W
QA0, KA0, VA0 = 0, A_Q, A_Q + A_KV
QB0 = VA0 + A_KV
KB0, VB0 = QB0 + B_W, QB0 + 2 * B_W
QM0 = QB0 + 3 * B_W
UNITS = KD + KF
RAW = 6
POOL_LO = (1, 4, 7, 10)
DVE_LO = tuple(w for w in range(UNITS) if w not in POOL_LO)


def key_range(n):
    k0 = max(0, (n - 1) * P)
    return k0, min(S, (n + 2) * P) - k0


def chunk_order():
    c = [("mk", 0), ("mk", 1), ("mv", 0), ("mv", 1), ("qm", 0), ("qm", 1)]
    c += [("qa", g) for g in range(4)] + [("ka", 0), ("va", 0)]
    c += [("qb", 0), ("qb", 1), ("kb", 0), ("kb", 1), ("vb", 0), ("vb", 1)]
    return c + [("wo", g) for g in range(8)]


CHUNKS = chunk_order()
NCH = len(CHUNKS)
UNIT_LIST = ([("M", n, h) for n in range(NT) for h in range(M_HEADS)]
             + [("A", n, h) for n in range(NT) for h in range(A_HEADS)]
             + [("B", n, h) for n in range(NT) for h in range(B_HEADS)])
NU = len(UNIT_LIST)
GROUPS = [(k, n) for k in "MAB" for n in range(NT)]
HEADS = {"M": M_HEADS, "A": A_HEADS, "B": B_HEADS}
OCOL = {"A": 0, "B": A_Q, "M": A_Q + B_W}


def schedule():
    ev, tu = [], 0
    for s in range(NSEQ):
        for kind, tiles in (("x", NT), ("m", MEM // P)):
            for t in range(tiles):
                for b in range(2):
                    ev.append((kind, s, t, b, tu))
                    tu += 1
        nxt = 0
        for _ in range(6):
            ev.append(("C", s, nxt, s * NCH + nxt))
            nxt += 1
        for i in range(NU + 2):
            if i < NU:
                ev.append(("S", s, i, s * NU + i))
            if 1 <= i <= NU:
                ev.append(("T", s, i - 1, s * NU + i - 1, tu))
                tu += 1
            if i >= 2:
                ev.append(("PV", s, i - 2, s * NU + i - 2))
            if nxt < 12 and i < 16 and i * 6 // 14 + 7 > nxt:
                ev.append(("C", s, nxt, s * NCH + nxt))
                nxt += 1
            elif 16 <= i < 48 and nxt < 18 and (i - 14) // 4 + 12 > nxt:
                ev.append(("C", s, nxt, s * NCH + nxt))
                nxt += 1
        for n in range(NT):
            for b in range(2):
                ev.append(("o", s, n, b, tu))
                tu += 1
        while nxt < NCH:
            ev.append(("C", s, nxt, s * NCH + nxt))
            nxt += 1
        ev.append(("LN", s))
        for t in range(NT):
            for b in range(2):
                ev.append(("r", s, t, b, tu))
                tu += 1
            ev.append(("R", s, t))
    return ev, tu


EVENTS, N_TU = schedule()
T_OF_UNIT = {e[3]: e[4] for e in EVENTS if e[0] == "T"}
FIRST_T = [min(e[4] for e in EVENTS if e[0] == "x" and e[1] == s) for s in range(NSEQ)]
LAST_O = [max(e[4] for e in EVENTS if e[0] == "o" and e[1] == s) for s in range(NSEQ)]
R_UNITS = {(s, t): [e[4] for e in EVENTS if e[0] == "r" and e[1:3] == (s, t)] for s in range(NSEQ) for t in range(NT)}


def build_kernel(nc, x, mem, w_in, w_mem_kv, sink, rpb, grp_g, w_out, ln1_g, ln1_b, w_router, router_bias,
                 w_gate, w_up, w_down, ln2_g, ln2_b, out):
    with ExitStack() as ctx:
        def sb(name, shape, dt=F32):
            return ctx.enter_context(nc.sbuf_tensor(name, shape, dt))

        def sem(name):
            return ctx.enter_context(nc.semaphore(name))

        def bank(name):
            return ctx.enter_context(nc.psum_tensor(name, [P, 512], F32))

        x1_dram = nc.dram_tensor("x1_dram", (TT * P, D), F32).ap()
        vbw_dram = nc.dram_tensor("vbw_dram", (NSEQ, 4, ROWS, BW, B_W), F32).ap()
        biasb_dram = nc.dram_tensor("biasb_dram", (12, 16, 15, BW), F32).ap()
        y_dram = nc.dram_tensor("y_dram", (SLOTS * P, D), F32).ap()
        pad_dram = nc.dram_tensor("pad_dram", (B_HEADS, 15, 64), F32).ap()

        R = sb("split_main", [P, 24576], F32R)
        RX = sb("split_aux", [P, 3072], F32R)

        def cut(t, at, *shape):
            n = 1
            for d in shape:
                n *= d
            ap = t[:, at:at + n]
            if len(shape) == 2:
                ap = ap.rearrange("p (a b) -> p a b", a=shape[0])
            if len(shape) == 3:
                ap = ap.rearrange("p (a b c) -> p a b c", a=shape[0], b=shape[1])
            return ap

        xT = [cut(R, 0, KD, S), cut(R, 4096, KD, S)]
        memT = [cut(R, 8192, KD, MEM), cut(R, 10240, KD, MEM)]
        qbT = [cut(R, 8192, 2, S), cut(R, 9216, 2, S)]
        kbT = [cut(R, 10240, 2, S), cut(R, 11264, 2, S)]
        wch = [cut(R, 12288, 2, KD, P), cut(R, 14336, 2, KD, P)]
        qaT = [cut(R, 16384, 4, S), cut(R, 18432, 4, S)]
        kaT = [cut(R, 20480, 1, S), cut(R, 20992, 1, S)]
        qmT = [cut(R, 21504, 2, S), cut(R, 22528, 2, S)]
        mkT = [cut(R, 23552, 2, MEM), cut(R, 24064, 2, MEM)]
        wu = [cut(R, 0, UNITS, 1024), cut(R, 12288, UNITS, 1024)]
        xgT = [cut(RX, 0, KD, P), cut(RX, 1024, KD, P)]
        hT = [cut(RX, 2048, KF, P), cut(RX, 2560, KF, P)]

        x_nat = sb("x_nat", [P, NT, D])
        tables = sb("tables", [P, 6144])
        biasA = cut(tables, 0, A_HEADS, 3 * P)
        biasB = cut(tables, 3072, 12, 256)
        raw = cut(tables, 0, RAW, 1024)
        va = sb("va", [P, NT, A_KV])
        vbw = sb("vbw", [P, 8, B_W])
        mem_nat = vbw[:, :, :].rearrange("p (t a) b -> p t (a b)", t=2)
        mv = sb("mv", [P, 2, M_W])
        vstg = sb("vstg", [P, NT, B_W])
        x1T = vstg[:, :, :].rearrange("p a (b c) -> p (a b) c", c=P)
        probs = sb("probs", [P, 2, 384])
        probsT = sb("probsT", [P, 2, 384])
        o_sb = sb("o_sb", [P, NT, D])
        wraw = sb("wraw", [P, 2, KD, P])
        ln = sb("ln", [P, 2, D])
        ident = sb("ident", [P, P])
        anti = sb("anti", [P, P])
        ones_b = sb("ones_b", [P, P], BF16)
        tri_b = sb("tri_b", [P, P], BF16)
        wr = sb("wr", [P, KD, NE])
        gcol = sb("gcol", [P, KD])
        sinkb = sb("sinkb", [P, A_HEADS])
        nsink = sb("nsink", [P, A_HEADS])
        rbb = sb("rbb", [P, NE])
        negm = sb("negm", [P, 2, A_HEADS])
        sums = sb("sums", [P, 2, A_HEADS])
        es = sb("es", [P, 2, A_HEADS])
        rden = sb("rden", [P, 2, A_HEADS])
        stats = sb("stats", [P, TT, 2, 6])
        mvv = sb("mvv", [P, 12, 2])
        nv = sb("nv", [P, 12])
        ny = sb("ny", [P, 12])
        nt_ = sb("nt_", [P, 12])
        sc = sb("sc", [P, TT, NE])
        idxc = sb("idxc", [P, 1], I32)
        idx = sb("idx", [P, SLOTS], I32)
        tiles_cum = sb("tiles_cum", [P, NE + 2], I32)
        slot_i = sb("slot_i", [P, 2, TT], I32)
        wts = sb("wts", [P, 2, TT])
        riota = sb("riota", [P, P])
        tokf = sb("tokf", [P, TT])
        mask_b = sb("mask_b", [P, TT * NE], BF16)
        carry = sb("carry", [1, 3])
        izero = sb("izero", [P, 1], I32)
        ints = sb("ints", [P, 32], I32)
        seed = sb("seed", [P, 8])
        scol = sb("scol", [P, 2], I32)

        scratch = o_sb[:, :, :].rearrange("p a b -> p (a b)")
        vbw_flat = vbw[:, :, :].rearrange("p a b -> p (a b)")
        xg = x_nat[:, 0, :]
        y_sb = x_nat[:, 1, :]
        sg = x_nat[:, 2, 0:512]
        h_sb = x_nat[:, 3, 0:512]
        zeros = x_nat[:, 3, 512:1024]

        Cb = [bank("C0"), bank("C1")]
        Tb = [bank("T0"), bank("T1")]
        Sb = [bank("S0"), bank("S1")]
        Ob = [bank("O0"), bank("O1")]

        x_loaded = [[sem(f"x_loaded{s}_{t}") for t in range(NT)] for s in range(NSEQ)]
        mem_loaded = [sem(f"mem_loaded{s}") for s in range(NSEQ)]
        small_loaded = sem("small_loaded")
        ln_loaded = sem("ln_loaded")
        rpb_loaded = sem("rpb_loaded")
        pad_stored = sem("pad_stored")
        biasb_loaded = sem("biasb_loaded")
        biasb_spread = sem("biasb_spread")
        chunk_loaded = [sem("chunk_loaded0"), sem("chunk_loaded1")]
        chunk_scaled = sem("chunk_scaled")
        chunk_hi = sem("chunk_hi")
        chunk_lo = sem("chunk_lo")
        t_ready = [sem("t_ready0"), sem("t_ready1")]
        t_hi = sem("t_hi")
        t_drained = [sem("t_drained0"), sem("t_drained1")]
        c_ready = [sem("c_ready0"), sem("c_ready1")]
        c_hi = sem("c_hi")
        c_drained = [sem("c_drained0"), sem("c_drained1")]
        s_ready = [sem("s_ready0"), sem("s_ready1")]
        biased = sem("biased")
        maxed = sem("maxed")
        exped = sem("exped")
        pv_done = sem("pv_done")
        o_drained = [sem("o_drained0"), sem("o_drained1")]
        sink_in = sem("sink_in")
        sink_exp = sem("sink_exp")
        vb_stored = sem("vb_stored")
        vbw_loaded = sem("vbw_loaded")
        mixed_done = sem("mixed_done")
        normed = sem("normed")
        x1_ready = sem("x1_ready")
        x1_stored = sem("x1_stored")
        route_psum = sem("route_psum")
        sig_done = sem("sig_done")
        setup_pool = sem("setup_pool")
        setup_dve = sem("setup_dve")
        setup_pe = sem("setup_pe")
        dch = sem("dve_chain")
        pch = sem("pool_chain")
        mask_ready = sem("mask_ready")
        rank_done = sem("rank_done")
        onehot_ready = sem("onehot_ready")
        onehot_used = sem("onehot_used")
        idx_psum = sem("idx_psum")
        routed = sem("routed")
        raw_loaded = [sem(f"raw_loaded{i}") for i in range(RAW)]
        unit_hi = sem("unit_hi")
        unit_lo_dve = sem("unit_lo_dve")
        unit_lo_pool = sem("unit_lo_pool")
        units_used = sem("units_used")
        xg_idx = sem("xg_idx")
        xg_loaded = sem("xg_loaded")
        xgT_psum = sem("xgT_psum")
        xgT_hi = sem("xgT_hi")
        xgT_lo = sem("xgT_lo")
        silu_done = sem("silu_done")
        h_mid = sem("h_mid")
        hT_psum = sem("hT_psum")
        hT_hi = sem("hT_hi")
        hT_lo = sem("hT_lo")
        y_half = [sem("y_half0"), sem("y_half1")]
        y_stored = sem("y_stored")
        y_zeroed = sem("y_zeroed")
        fin_loaded = [sem("fin_loaded0"), sem("fin_loaded1")]
        fin_acc = sem("fin_acc")
        fin_norm = sem("fin_norm")
        fin_y = sem("fin_y")
        out_stored = [sem(f"out_stored{i}") for i in range(NT)]

        win_v = w_in.rearrange("(k p) c -> p k c", p=P)
        wkv_v = w_mem_kv.rearrange("(k p) c -> p k c", p=P)
        wo_v = w_out.rearrange("(k p) c -> p k c", p=P)

        chunk_src = {"mk": (wkv_v, 0), "mv": (wkv_v, M_W), "qm": (win_v, QM0), "ka": (win_v, KA0), "va": (win_v, VA0),
                     "qb": (win_v, QB0), "kb": (win_v, KB0), "vb": (win_v, VB0), "wo": (wo_v, 0)}

        def chunk_loads(g):
            n = 0
            for i in range(g % 2, g + 1, 2):
                n += 32 if CHUNKS[i % NCH][0] == "qa" else 16
            return n

        split_T = [e for e in EVENTS if e[0] in ("x", "m", "o")]
        T_HI = {e[4]: i + 1 for i, e in enumerate(split_T)}
        split_C = ("mk", "qm", "qa", "ka", "qb", "kb")
        C_HI = {}
        for s_ in range(NSEQ):
            for c_, (kind_, _) in enumerate(CHUNKS):
                if kind_ in split_C:
                    C_HI[s_ * NCH + c_] = len(C_HI) + 1
        GI = {kn: i for i, kn in enumerate(GROUPS)}

        def group_of(s, i):
            k, n, h = UNIT_LIST[i]
            return s * len(GROUPS) + GI[(k, n)], h

        def t_waits(eng, last_unit):
            for b in range(2):
                eng.wait_ge(t_drained[b], (last_unit - b) // 2 + 1)

        def c_waits(eng, cu):
            for b in range(2):
                if cu - b >= 0:
                    eng.wait_ge(c_drained[b], (cu - b) // 2 + 1)

        def chunk_cu(s, kind, g):
            return s * NCH + CHUNKS.index((kind, g))

        def grid_view(xt, n):
            v = xt[:, 4:6, :].rearrange("p k (r c) -> p k r c", r=ROWS)
            return v[:, :, :, n * 16:(n + 1) * 16]

        def by_row(ap):
            return ap.rearrange("p (r n c) -> p r n c", r=ROWS, n=4)

        def by_block(ap):
            return ap.rearrange("p (n r c) -> p r n c", r=ROWS, n=4)

        def c_dest(kind, g):
            t = {"mk": mkT, "qm": qmT, "qa": qaT, "ka": kaT, "qb": qbT, "kb": kbT}[kind]
            return [t[0][:, g, :], t[1][:, g, :]], (MEM if kind == "mk" else S)

        def copy_probs(eng, copy, s, i, a, u):
            kind, tile, h = UNIT_LIST[i]
            w = key_range(tile)[1] if kind == "A" else 256
            eng.wait_ge(t_ready[u % 2], u // 2 + 1)
            if a >= 2:
                eng.wait_ge(pv_done, a - 1)
            copy(probsT[:, a % 2, 0:w], Tb[u % 2][:, 0:w]).then_inc(t_drained[u % 2], 1)

        def normalise_groups(s, link, rsqrt, dve):
            link(nc.vector.tensor_tensor(nv[:, :], mvv[:, :, 0], mvv[:, :, 0], ALU.mult))
            link(nc.vector.tensor_tensor(nv[:, :], nv[:, :], mvv[:, :, 1], ALU.add))
            link(nc.vector.tensor_scalar(nv[:, :], nv[:, :], EPS, None, ALU.add))
            rsqrt(12)
            for tile in range(NT):
                for kind in "ABM":
                    c0, w = OCOL[kind], HEADS[kind] * HD
                    gl = GI[(kind, tile)]
                    ins = nc.vector.tensor_scalar(o_sb[:, tile, c0:c0 + w], o_sb[:, tile, c0:c0 + w],
                                                  ny[:, gl:gl + 1], None, ALU.mult)
                ins.then_inc(mixed_done, 1)

        def routing(dve, link):
            G = TT * NG
            sel = cut(scratch, 0, TT, NE)
            w16 = [cut(scratch, 128 * i, G, EG) for i in range(8)]
            w32 = [scratch[:, 1024 + 32 * i:1024 + 32 * (i + 1)] for i in range(6)]
            w8 = [scratch[:, 1280 + 8 * i:1280 + 8 * (i + 1)] for i in range(8)]
            selv = w16[0]
            rev4 = w16[7]
            dve.wait_ge(sig_done, NSEQ)
            dve.wait_ge(x1_stored, 16 * TT)
            link(nc.vector.memset(zeros, 0.0))
            for i in range(EG):
                link(nc.vector.memset(rev4[:, :, i], float(EG - i)))
            link(nc.vector.tensor_tensor(sel, sc[:, :, :], rbb[:, :].unsqueeze(1).to_broadcast([P, TT, NE]), ALU.add))

            def first_max(v, m, oh, rows, key, mk, rev):
                link(nc.vector.tensor_reduce(m, v, AX.X, ALU.max))
                link(nc.vector.tensor_tensor(key, v, m.unsqueeze(2).to_broadcast([P, rows, 4]), ALU.is_equal))
                link(nc.vector.tensor_tensor(key, key, rev, ALU.mult))
                link(nc.vector.tensor_reduce(mk, key, AX.X, ALU.max))
                link(nc.vector.tensor_tensor(oh, key, mk.unsqueeze(2).to_broadcast([P, rows, 4]), ALU.is_equal))

            m1, m2, mk = w32[0], w32[1], w32[2]
            oh1, oh2, key, sel2 = w16[1], w16[2], w16[3], w16[4]
            first_max(selv, m1, oh1, G, key, mk, rev4)
            link(nc.vector.scalar_tensor_tensor(sel2, oh1, MASKED, selv, ALU.mult, ALU.add))
            first_max(sel2, m2, oh2, G, key, mk, rev4)
            link(nc.vector.tensor_tensor(m1, m1, m2, ALU.add))
            gsc = m1.rearrange("p (t g) -> p t g", t=TT)
            gkey = w32[3].rearrange("p (t g) -> p t g", t=TT)
            goh = w32[4].rearrange("p (t g) -> p t g", t=TT)
            first_max(gsc, w8[0], goh, TT, gkey, w8[1], rev4[:, 0:TT, :])
            gb = w32[4].unsqueeze(2).to_broadcast([P, G, EG])
            link(nc.vector.tensor_tensor(oh1, oh1, gb, ALU.mult))
            link(nc.vector.tensor_tensor(oh2, oh2, gb, ALU.mult))
            link(nc.vector.tensor_tensor(cut(mask_b, 0, G, EG), oh1, oh2, ALU.add))
            nc.vector.memset(seed[:, 6:7], 0.0).then_inc(mask_ready, 1)

            E1, E2 = cut(scratch, 128, TT, NE), cut(scratch, 256, TT, NE)
            tmp = cut(scratch, 384, TT, NE)
            w_a, w_b, w_s = w8[2], w8[3], w8[4]
            link(nc.vector.tensor_tensor(tmp, E1, sc[:, :, :], ALU.mult))
            link(nc.vector.tensor_reduce(w_a, tmp, AX.X, ALU.add))
            link(nc.vector.tensor_tensor(tmp, E2, sc[:, :, :], ALU.mult))
            link(nc.vector.tensor_reduce(w_b, tmp, AX.X, ALU.add))
            link(nc.vector.tensor_tensor(w_s, w_a, w_b, ALU.add))
            link(nc.vector.reciprocal(w_s, w_s))
            link(nc.vector.tensor_tensor(wts[:, 0, :], w_a, w_s, ALU.mult))
            link(nc.vector.tensor_tensor(wts[:, 1, :], w_b, w_s, ALU.mult))

            dve.wait_ge(rank_done, 1)
            thr = cut(scratch, 1408, NE, TT)
            for i in range(TT):
                link(nc.vector.memset(thr[:, :, i], float(P * i)))
            cmp = cut(scratch, 512, NE, TT)
            link(nc.vector.tensor_tensor(cmp, Ob[0][:, 128:128 + NE].unsqueeze(2).to_broadcast([P, NE, TT]), thr, ALU.is_gt))
            ntl, cum, base, one16 = (scratch[:, 1536 + 16 * i:1552 + 16 * i] for i in range(4))
            link(nc.vector.tensor_reduce(ntl, cmp, AX.X, ALU.add))
            link(nc.vector.tensor_scalar(ntl, ntl, 1.0, None, ALU.max))
            link(nc.vector.memset(one16, 1.0))
            link(nc.vector.tensor_tensor_scan(cum, one16, ntl, 0.0, ALU.mult, ALU.add))
            link(nc.vector.tensor_tensor(base, cum, ntl, ALU.subtract))
            link(nc.vector.tensor_copy(tiles_cum[:, 0:NE], base))
            link(nc.vector.tensor_copy(tiles_cum[:, NE:NE + 1], cum[:, NE - 1:NE]))
            link(nc.vector.tensor_scalar(tiles_cum[:, NE + 1:NE + 2], cum[:, NE - 1:NE], -1.0, float(SLOTS),
                                         ALU.mult, ALU.add))
            link(nc.vector.tensor_scalar(base, base, float(P), None, ALU.mult))
            pos = cut(scratch, 640, TT, NE)
            link(nc.vector.tensor_tensor(pos, Ob[0][:, 0:TT * NE].rearrange("p (t e) -> p t e", t=TT),
                                         base.unsqueeze(1).to_broadcast([P, TT, NE]), ALU.add))
            slot_f = scratch[:, 1600:1616]
            for c, E in enumerate((E1, E2)):
                link(nc.vector.tensor_tensor(tmp, E, pos, ALU.mult))
                link(nc.vector.tensor_reduce(slot_f[:, c * TT:(c + 1) * TT], tmp, AX.X, ALU.add))
            link(nc.vector.tensor_copy(slot_i[:, :, :].rearrange("p c t -> p (c t)"), slot_f))
            hi_i, lo_i = ints[:, 0:16], ints[:, 16:32]
            flat = slot_i[:, :, :].rearrange("p c t -> p (c t)")
            link(nc.vector.tensor_scalar(hi_i, flat, 7, None, ALU.logical_shift_right))
            link(nc.vector.tensor_scalar(lo_i, flat, P - 1, None, ALU.bitwise_and))
            hi_f, lo_f = scratch[:, 1616:1632], scratch[:, 1632:1648]
            link(nc.vector.tensor_copy(hi_f, hi_i))
            link(nc.vector.tensor_copy(lo_f, lo_i))
            rowoh = cut(vbw_flat, 0, 2 * TT, P)
            tileoh = cut(scratch, 1664, 2 * TT, SLOTS)
            for i in range(2 * TT):
                link(nc.vector.tensor_scalar(rowoh[:, i, :], riota[:, :], lo_f[:, i:i + 1], None, ALU.is_equal))
                link(nc.vector.tensor_scalar(tileoh[:, i, :], riota[:, 0:SLOTS], hi_f[:, i:i + 1],
                                             tokf[:, i % TT:i % TT + 1], ALU.is_equal, ALU.mult))
            nc.vector.memset(seed[:, 5:6], 0.0).then_inc(onehot_ready, 1)
            dve.wait_ge(idx_psum, 1)
            link(nc.vector.tensor_copy(idx[:, :], Ob[1][:, 0:SLOTS]))
            nc.vector.memset(seed[:, 4:5], 0.0).then_inc(routed, 1)

        block = ctx.enter_context(nc.Block())

        @block.sync
        def _(sp):
            for t in range(NT):
                sp.dma_start(x_nat[:, t, :], x[0][t * P:(t + 1) * P, :]).then_inc(x_loaded[0][t], 16)
            sp.dma_start(mem_nat, mem[0].rearrange("(t p) d -> p t d", p=P)).then_inc(mem_loaded[0], 16)

            def load_chunk(g):
                kind, i = CHUNKS[g % NCH]
                if g >= 2:
                    sp.wait_ge(chunk_lo, g - 1)
                slot = wraw[:, g % 2, :, :]
                if kind == "qa":
                    for half in range(2):
                        sp.dma_start(slot[:, :, half * HD:(half + 1) * HD],
                                     win_v[:, :, half * 256 + i * HD:half * 256 + (i + 1) * HD])\
                            .then_inc(chunk_loaded[g % 2], 16)
                else:
                    src, c0 = chunk_src[kind]
                    sp.dma_start(slot, src[:, :, c0 + i * P:c0 + (i + 1) * P]).then_inc(chunk_loaded[g % 2], 16)

            def small_loads():
                sp.dma_start(wr[:, :, :], w_router.rearrange("(k p) e -> p k e", p=P)).then_inc(small_loaded, 16)
                sp.dma_start(gcol[:, :], grp_g).then_inc(small_loaded, 16)
                sp.dma_start(sinkb[:, :], sink.partition_broadcast(P)).then_inc(small_loaded, 16)
                sp.dma_start(rbb[:, :], router_bias.partition_broadcast(P)).then_inc(small_loaded, 16)
                sp.wait_ge(setup_dve, 1)
                sp.dma_start(o_sb[0:60, 0, 16:47], rpb.rearrange("h r c -> (h r) c")).then_inc(rpb_loaded, 16)
                sp.wait_ge(rpb_loaded, 16)
                sp.dma_start(pad_dram.rearrange("h r c -> (h r) c"), o_sb[0:60, 0, 0:64]).then_inc(pad_stored, 16)
                sp.wait_ge(pad_stored, 16)
                for h in range(B_HEADS):
                    for kind, delta in enumerate((0, -8, -16)):
                        src = bass.AP(pad_dram.tensor, h * 15 * 64 + 16 + delta, [[1, 16], [64, 15], [1, BW]])
                        sp.dma_start(biasb_dram[h * 3 + kind], src).then_inc(biasb_spread, 16)
                sp.wait_ge(biasb_spread, 16 * 12)
                for rr in range(ROWS):
                    sp.dma_start(o_sb[rr * 16:(rr + 1) * 16, 1:4, :].rearrange("p a (b c) -> p (a b) c", c=256),
                                 biasb_dram[:, :, rr:rr + ROWS, :].rearrange("n i a b -> i n (a b)"))\
                        .then_inc(biasb_loaded, 16)
                sp.dma_start(ln[:, 0, :], ln1_g.partition_broadcast(P)).then_inc(ln_loaded, 16)
                sp.dma_start(ln[:, 1, :], ln1_b.partition_broadcast(P)).then_inc(ln_loaded, 16)

            for g in range(NSEQ * NCH):
                load_chunk(g)
                if g == 1:
                    small_loads()
                s, c = g // NCH, g % NCH
                if c == CHUNKS.index(("vb", 1)) + 2:
                    c_waits(sp, chunk_cu(s, "vb", 1))
                    for w in range(4):
                        for odd in range(2):
                            p0 = odd * GRID_W + WIN0[w]
                            sp.dma_start(vbw_dram[s, w].rearrange("(t o) c d -> o c t d", o=2)[odd],
                                         vstg[p0:p0 + BW, :, :]).then_inc(vb_stored, 16)
                    sp.wait_ge(vb_stored, 16 * 8 * (s + 1))
                    sp.dma_start(vbw[:, :, :], vbw_dram[s].rearrange("w (h r) c d -> (r c) (w h) d", h=2))\
                        .then_inc(vbw_loaded, 16)

            sp.wait_ge(x1_ready, TT)
            sp.dma_start(ln[:, 0, :], ln2_g.partition_broadcast(P)).then_inc(ln_loaded, 16)
            sp.dma_start(ln[:, 1, :], ln2_b.partition_broadcast(P)).then_inc(ln_loaded, 16)

            sp.wait_ge(biased, 2 * (32 + 16))
            with sp.Fori(0, NE) as e:
                for w in range(UNITS):
                    slot = w % RAW
                    lo_sem, owned = (unit_lo_pool, POOL_LO) if w in POOL_LO else (unit_lo_dve, DVE_LO)
                    if w < RAW:
                        sp.wait_ge(lo_sem, e * len(owned) + owned.index(w + RAW) + 1)
                    else:
                        sp.wait_ge(lo_sem, e * len(owned) + len(owned) + owned.index(w - RAW) + 1)
                    for half in range(2):
                        if w < KD:
                            src = (w_gate, w_up)[half][bass.ds(e, 1), w * P:(w + 1) * P, :]
                        else:
                            src = w_down[bass.ds(e, 1), (w - KD) * P:(w - KD + 1) * P, half * 512:(half + 1) * 512]
                        sp.dma_start(raw[:, slot, half * 512:(half + 1) * 512],
                                     src.rearrange("a p c -> (a p) c")).then_inc(raw_loaded[slot], 16)

            for t in range(TT):
                sp.wait_ge(fin_y, t + 1)
                sp.dma_start(out[t // NT][0, (t % NT) * P:(t % NT + 1) * P, :], o_sb[:, t % NT, :])\
                    .then_inc(out_stored[t % NT], 16)
            for i in range(NT):
                sp.wait_ge(out_stored[i], 16 * NSEQ)

        @block.gpsimd
        def _(pool):
            n = [0]

            def link(i):
                n[0] += 1
                i.then_inc(pch, 1)
                pool.wait_ge(pch, n[0])

            link(nc.gpsimd.memset(ident[:, :], 0.0))
            link(nc.gpsimd.memset(anti[:, :], 0.0))
            link(nc.gpsimd.memset(izero[:, :], 0))
            nc.gpsimd.affine_select(out=ident[:, :], in_=ident[:, :], compare_op=ALU.not_equal, fill=1.0, base=0,
                                    pattern=[[-1, P]], channel_multiplier=1).then_inc(setup_pool, 1)
            nc.gpsimd.affine_select(out=anti[:, :], in_=anti[:, :], compare_op=ALU.not_equal, fill=1.0, base=-(P - 1),
                                    pattern=[[1, P]], channel_multiplier=1).then_inc(setup_pool, 1)
            nc.gpsimd.memset(ones_b[:, :], 1.0).then_inc(setup_pool, 1)
            pool.wait_ge(setup_pool, 3)
            nc.gpsimd.affine_select(out=tri_b[:, :], in_=ones_b[:, :], compare_op=ALU.is_gt, fill=0.0, base=0,
                                    pattern=[[1, P]], channel_multiplier=-1).then_inc(setup_pool, 1)
            nc.gpsimd.iota(o_sb[:, 0, 512:896], pattern=[[-1, 3 * P]], base=P, channel_multiplier=1,
                           allow_small_or_imprecise_dtypes=True).then_inc(setup_pool, 1)
            nc.gpsimd.iota(scol[:, 0:1], pattern=[[0, 1]], base=0, channel_multiplier=1).then_inc(setup_pool, 1)
            nc.gpsimd.iota(o_sb[:, 0, 64:96], pattern=[[1, BW]], base=0, channel_multiplier=0,
                           allow_small_or_imprecise_dtypes=True).then_inc(setup_pool, 1)
            nc.gpsimd.iota(riota[:, :], pattern=[[1, P]], base=0, channel_multiplier=0,
                           allow_small_or_imprecise_dtypes=True).then_inc(setup_pool, 1)
            nc.gpsimd.iota(tokf[:, :], pattern=[[P, TT]], base=0, channel_multiplier=1,
                           allow_small_or_imprecise_dtypes=True).then_inc(setup_pool, 1)

            def lo_chunk(g):
                kind, _ = CHUNKS[g % NCH]
                slot = g % 2
                if kind == "wo":
                    pool.wait_ge(chunk_loaded[slot], chunk_loads(g))
                    pool.wait_ge(small_loaded, 64)
                    nc.gpsimd.tensor_tensor(wraw[:, slot, :, :], wraw[:, slot, :, :],
                                            gcol[:, :].unsqueeze(2).to_broadcast([P, KD, P]),
                                            ALU.mult).then_inc(chunk_scaled, 1)
                pool.wait_ge(chunk_hi, g + 1)
                nc.gpsimd.tensor_tensor(wch[1][:, slot, :, :], wraw[:, slot, :, :], wch[0][:, slot, :, :].bitcast(F32),
                                        ALU.subtract).then_inc(chunk_lo, 1)

            for s in range(NSEQ):
                for c in range(NCH):
                    lo_chunk(s * NCH + c)
                pool.wait_ge(ln_loaded, 32)
                for t in range(NT):
                    pool.wait_ge(normed, s * NT + t + 1)
                    link(nc.gpsimd.tensor_tensor(x_nat[:, t, :], x_nat[:, t, :], ln[:, 0, :], ALU.mult))
                    nc.gpsimd.tensor_tensor(x_nat[:, t, :], x_nat[:, t, :], ln[:, 1, :], ALU.add).then_inc(x1_ready, 1)
                    pool.wait_ge(x1_ready, s * NT + t + 1)
                    pool.dma_start(x1_dram[(s * NT + t) * P:(s * NT + t + 1) * P, :], x_nat[:, t, :]).then_inc(x1_stored, 16)
                pool.wait_ge(x1_stored, 16 * NT * (s + 1))
                if s == 0:
                    pool.dma_start(mem_nat, mem[1].rearrange("(t p) d -> p t d", p=P)).then_inc(mem_loaded[1], 16)
                    for t in range(NT):
                        for u in R_UNITS[(0, t)]:
                            pool.wait_ge(t_ready[u % 2], u // 2 + 1)
                        pool.dma_start(x_nat[:, t, :], x[1][t * P:(t + 1) * P, :]).then_inc(x_loaded[1][t], 16)

            pool.wait_ge(routed, 1)

            def gather():
                nc.gpsimd.indirect_dma_start(xg, None, x1_dram, bass.IndirectOffsetOnAxis(idxc[:, 0:1], 0))\
                    .then_inc(xg_loaded, 16)

            nc.gpsimd.tensor_copy(idxc[:, :], idx[:, 0:1]).then_inc(xg_idx, 1)
            pool.wait_ge(xg_idx, 1)
            gather()

            def lo_units(e):
                for w in POOL_LO:
                    pool.wait_ge(unit_hi, e * UNITS + w + 1)
                    nc.gpsimd.tensor_tensor(wu[1][:, w, :], raw[:, w % RAW, :], wu[0][:, w, :].bitcast(F32),
                                            ALU.subtract).then_inc(unit_lo_pool, 1)

            def next_gather(j):
                pool.wait_ge(xgT_psum, j + 1)
                nc.gpsimd.tensor_tensor(idxc[:, :], idx[:, bass.ds(j + 1, 1)], izero[:, :], ALU.add).then_inc(xg_idx, 1)
                pool.wait_ge(xg_idx, j + 2)
                nc.gpsimd.tensor_tensor(carry[:, 0:1], riota[0:1, 0:1], riota[0:1, 1:2], ALU.add)
                gather()

            lo_units(0)
            with pool.Fori(0, NE - 1) as e:
                lo = pool.value_load(tiles_cum[0:1, bass.ds(e, 1)], min_val=0, max_val=SLOTS - 1)
                hi = pool.value_load(tiles_cum[0:1, bass.ds(e + 1, 1)], min_val=1, max_val=SLOTS - 1)
                with pool.Fori(lo, hi) as j:
                    next_gather(j)
                lo_units(e + 1)
            lo = pool.value_load(tiles_cum[0:1, NE - 1:NE], min_val=0, max_val=SLOTS - 1)
            total = pool.value_load(tiles_cum[0:1, NE:NE + 1], min_val=1, max_val=SLOTS - 1)
            with pool.Fori(lo, total) as j:
                next_gather(j)

            pool.wait_ge(unit_lo_dve, (NE + 1) * len(DVE_LO))
            pool.wait_ge(unit_lo_pool, (NE + 1) * len(POOL_LO))
            pool.wait_ge(xg_loaded, total * 16 + 16)
            nc.gpsimd.tensor_tensor(carry[:, 2:3], riota[0:1, 0:1], riota[0:1, 1:2], ALU.add)
            spare = pool.value_load(tiles_cum[0:1, NE + 1:NE + 2], min_val=1, max_val=SLOTS - NE)
            pool.wait_ge(y_zeroed, spare * 32)
            pool.wait_ge(y_stored, total * 16 + 16)
            nc.gpsimd.tensor_tensor(carry[:, 1:2], riota[0:1, 0:1], riota[0:1, 1:2], ALU.add)

            def finish_tile(t):
                if t == 0:
                    pool.wait_ge(ln_loaded, 64)
                pool.wait_ge(fin_norm, t + 1)
                o = o_sb[:, t % NT, :]
                link(nc.gpsimd.tensor_tensor(o, o, ln[:, 0, :], ALU.mult))
                nc.gpsimd.tensor_tensor(o, o, ln[:, 1, :], ALU.add).then_inc(fin_y, 1)

            for t in range(TT):
                f = t % 2
                if t >= 2:
                    pool.wait_ge(fin_acc, t - 1)
                for c in range(2):
                    nc.gpsimd.indirect_dma_start(raw[:, 3 * f + c, :], None, y_dram,
                                                 bass.IndirectOffsetOnAxis(slot_i[:, c, t:t + 1], 0))\
                        .then_inc(fin_loaded[f], 16)
                pool.dma_start(raw[:, 3 * f + 2, :], x1_dram[t * P:(t + 1) * P, :]).then_inc(fin_loaded[f], 16)
                if t >= 1:
                    finish_tile(t - 1)
            finish_tile(TT - 1)

        @block.scalar
        def _(act):
            def hi_chunk(g):
                slot = g % 2
                kind, _ = CHUNKS[g % NCH]
                act.wait_ge(chunk_loaded[slot], chunk_loads(g))
                if kind == "wo":
                    act.wait_ge(chunk_scaled, (g // NCH) * 8 + CHUNKS[g % NCH][1] + 1)
                if g >= 2:
                    act.wait_ge(c_ready[slot], g // 2)
                nc.scalar.activation(wch[0][:, slot, :, :], wraw[:, slot, :, :], ACT.Copy).then_inc(chunk_hi, 1)

            for ev in EVENTS:
                what, s = ev[0], ev[1]
                if what in ("x", "m", "o"):
                    t, b, u = ev[2], ev[3], ev[4]
                    act.wait_ge(t_ready[u % 2], u // 2 + 1)
                    src = Tb[u % 2][:, :].rearrange("p (k c) -> p k c", k=4)
                    if what == "o" and b == 1:
                        nc.scalar.activation(grid_view(xT[0], t), src[:, 0:2, :].rearrange("p k (r c) -> p k r c", r=ROWS),
                                             ACT.Copy)
                        nc.scalar.activation(xT[0][:, 6:8, t * P:(t + 1) * P], src[:, 2:4, :], ACT.Copy).then_inc(t_hi, 1)
                    else:
                        dst = (memT if what == "m" else xT)[0]
                        nc.scalar.activation(dst[:, 4 * b:4 * b + 4, t * P:(t + 1) * P], src, ACT.Copy).then_inc(t_hi, 1)
                elif what == "C":
                    c, cu = ev[2], ev[3]
                    kind, g = CHUNKS[c]
                    bnk = Cb[cu % 2]
                    if cu == 0:
                        hi_chunk(0)
                        hi_chunk(1)
                    act.wait_ge(c_ready[cu % 2], cu // 2 + 1)
                    if kind in split_C:
                        dst, width = c_dest(kind, g)
                        src = bnk[:, 0:width]
                        if kind == "qb":
                            dst, src = [by_block(dst[0])], by_row(src)
                        nc.scalar.activation(dst[0], src, ACT.Copy,
                                             scale=SCALE if kind[0] == "q" else 1.0).then_inc(c_hi, 1)
                    gg = s * NCH + c + 2
                    if gg < NSEQ * NCH:
                        hi_chunk(gg)
                elif what == "S":
                    i, a = ev[2], ev[3]
                    kind, tile, h = UNIT_LIST[i]
                    gi, hs = group_of(s, i)
                    if h == 0 and gi >= 2:
                        act.wait_ge(o_drained[gi % 2], gi // 2)
                    pr = probs[:, a % 2, :]
                    if kind == "M":
                        act.wait_ge(maxed, s * 16 + i + 1)
                        if a >= 2:
                            u2 = T_OF_UNIT[a - 2]
                            act.wait_ge(t_ready[u2 % 2], u2 // 2 + 1)
                        nc.scalar.activation(pr[:, 0:MEM], Sb[a % 2][:, 0:MEM], ACT.Exp, bias=negm[:, gi % 2, h:h + 1],
                                             accum_out=sums[:, gi % 2, h:h + 1]).then_inc(exped, 1)
                    else:
                        w = key_range(tile)[1] if kind == "A" else 256
                        act.wait_ge(biased, s * 48 + i - 16 + 1)
                        nc.scalar.activation(pr[:, 0:w], pr[:, 0:w], ACT.Exp, scale=-1.0,
                                             bias=negm[:, gi % 2, h:h + 1],
                                             accum_out=sums[:, gi % 2, h:h + 1]).then_inc(exped, 1)
                        if kind == "A" and h == A_HEADS - 1:
                            act.wait_ge(sink_in, s * NT + tile + 1)
                            nc.scalar.activation(es[:, gi % 2, :], es[:, gi % 2, :], ACT.Exp).then_inc(sink_exp, 1)
                elif what == "T":
                    i, a, u = ev[2], ev[3], ev[4]
                    if UNIT_LIST[i][0] == "M" or i % 4 == 1:
                        copy_probs(act, nc.scalar.copy, s, i, a, u)
                elif what == "r":
                    t, b, u = ev[2], ev[3], ev[4]
                    act.wait_ge(t_ready[u % 2], u // 2 + 1)
                    if t == 0 and b == 0:
                        act.wait_ge(vb_stored, 16 * 8 * (s + 1))
                    if s * NT + t >= 1:
                        act.wait_ge(route_psum, s * NT + t)
                    nc.scalar.activation(x1T[:, 4 * b:4 * b + 4, :], Tb[u % 2][:, :].rearrange("p (k c) -> p k c", k=4),
                                         ACT.Copy).then_inc(t_drained[u % 2], 1)
                elif what == "R" and ev[2] == NT - 1:
                    act.wait_ge(route_psum, (s + 1) * NT)
                    nc.scalar.activation(sc[:, s * NT:(s + 1) * NT, :],
                                         Ob[1][:, 0:NT * NE].rearrange("p (t e) -> p t e", t=NT),
                                         ACT.Sigmoid).then_inc(sig_done, 1)

            def hi_units(e, cum_prev, ws):
                for w in ws:
                    slot, turn = w % RAW, w // RAW
                    act.wait_ge(raw_loaded[slot], e * 64 + 32 * turn + 32)
                    act.wait_ge(units_used, cum_prev * UNITS + w + 1)
                    nc.scalar.activation(wu[0][:, w, :], raw[:, slot, :], ACT.Copy).then_inc(unit_hi, 1)

            def xgT_his(j):
                act.wait_ge(xgT_psum, j + 1)
                for b in range(2):
                    ins = nc.scalar.activation(xgT[0][:, 4 * b:4 * b + 4, :],
                                               Tb[b][:, :].rearrange("p (k c) -> p k c", k=4), ACT.Copy)
                ins.then_inc(xgT_hi, 1)

            def tile_first(j):
                act.wait_ge(units_used, j * UNITS + UNITS + KD)
                act.wait_ge(h_mid, j + 1)
                nc.scalar.activation(sg, Cb[0][:, :], ACT.Silu).then_inc(silu_done, 1)
                xgT_his(j + 1)
                act.wait_ge(hT_psum, j + 1)
                nc.scalar.activation(hT[0], Sb[0][:, :].rearrange("p (k c) -> p k c", k=KF), ACT.Copy).then_inc(hT_hi, 1)

            def tile_last(j):
                act.wait_ge(units_used, j * UNITS + 2 * UNITS)
                act.wait_ge(y_stored, j * 16 + 16)
                nc.scalar.activation(y_sb[:, 0:512], Ob[0][:, :], ACT.Copy).then_inc(y_half[0], 1)
                act.wait_ge(y_half[0], j + 2)
                act.wait_ge(y_half[1], j + 2)
                act.dma_start(y_dram.rearrange("(j p) c -> j p c", p=P)[bass.ds(j, 1)].rearrange("a p c -> (a p) c"),
                              y_sb).then_inc(y_stored, 16)

            hi_units(0, 0, range(UNITS))
            act.wait_ge(routed, 1)
            y_tiles = y_dram.rearrange("(j p) c -> j p c", p=P)
            total = act.value_load(tiles_cum[0:1, NE:NE + 1], min_val=1, max_val=SLOTS - 1)
            with act.Fori(total, SLOTS) as j:
                for half in range(2):
                    act.dma_start(y_tiles[bass.ds(j, 1), :, half * 512:(half + 1) * 512].rearrange("a p c -> (a p) c"),
                                  zeros).then_inc(y_zeroed, 16)
            xgT_his(0)
            with act.Fori(0, NE - 1) as e:
                lo = act.value_load(tiles_cum[0:1, bass.ds(e, 1)], min_val=0, max_val=SLOTS - 1)
                hi = act.value_load(tiles_cum[0:1, bass.ds(e + 1, 1)], min_val=1, max_val=SLOTS - 1)
                with act.If(lo < hi - 1):
                    with act.Fori(lo, hi - 1) as j:
                        tile_first(j)
                        tile_last(j)
                hi_units(e + 1, hi, range(0, 6))
                tile_first(hi - 1)
                hi_units(e + 1, hi, range(6, UNITS))
                tile_last(hi - 1)
            lo = act.value_load(tiles_cum[0:1, NE - 1:NE], min_val=0, max_val=SLOTS - 1)
            hi = act.value_load(tiles_cum[0:1, NE:NE + 1], min_val=1, max_val=SLOTS - 1)
            with act.Fori(lo, hi) as j:
                tile_first(j)
                tile_last(j)

        @block.vector
        def _(dve):
            n = [0]

            def link(i):
                n[0] += 1
                i.then_inc(dch, 1)
                dve.wait_ge(dch, n[0])

            def rsqrt(w):
                v, t, y = nv[:, 0:w], nt_[:, 0:w], ny[:, 0:w]
                link(nc.vector.tensor_scalar(t.bitcast(I32), v.bitcast(I32), 1, None, ALU.logical_shift_right))
                link(nc.vector.tensor_scalar(y.bitcast(I32), t.bitcast(I32), -1.0, float(0x5F3759DF), ALU.mult, ALU.add))
                for _ in range(4):
                    link(nc.vector.tensor_tensor(t, y, y, ALU.mult))
                    link(nc.vector.tensor_tensor(t, t, v, ALU.mult))
                    link(nc.vector.tensor_scalar(t, t, -0.5, 1.5, ALU.mult, ALU.add))
                    link(nc.vector.tensor_tensor(y, y, t, ALU.mult))

            nc.vector.memset(o_sb[:, 0, 0:64], 0.0).then_inc(setup_dve, 1)
            for i, (sm, v) in enumerate(((units_used, UNITS), (unit_lo_dve, len(DVE_LO)), (unit_lo_pool, len(POOL_LO)),
                                         (h_mid, 1), (y_half[0], 1), (y_half[1], 1), (y_stored, 16))):
                nc.vector.memset(seed[:, i:i + 1], 0.0).then_inc(sm, v)
            dve.wait_ge(setup_pool, 9)
            dist = o_sb[:, 0, 512:896]
            link(nc.vector.scalar_tensor_tensor(dist, dist, -1.0, dist, ALU.mult, ALU.max))
            mask = probs[:, 0, :]
            link(nc.vector.tensor_scalar(mask, dist, float(WINDOW), MASKED, ALU.is_gt, ALU.mult))
            for h in range(A_HEADS):
                link(nc.vector.scalar_tensor_tensor(biasA[:, h, :], dist, -(2.0 ** -(h + 1)), mask, ALU.mult, ALU.add))
            link(nc.vector.tensor_scalar(scol[:, 1:2], scol[:, 0:1], 15, None, ALU.bitwise_and))
            link(nc.vector.tensor_copy(nv[:, 0:1], scol[:, 1:2]))
            d = o_sb[:, 0, 96:128]
            link(nc.vector.tensor_scalar(d, o_sb[:, 0, 64:96], nv[:, 0:1], None, ALU.subtract))
            gm = o_sb[:, 0, 128:224].rearrange("p (k c) -> p k c", k=3)
            link(nc.vector.tensor_scalar(gm[:, 0, 0:16], d[:, 0:16], -8.0, MASKED, ALU.is_lt, ALU.mult))
            link(nc.vector.tensor_scalar(gm[:, 0, 16:32], d[:, 16:32], 7.0, MASKED, ALU.is_gt, ALU.mult))
            link(nc.vector.tensor_scalar(gm[:, 1, :], d, 0.0, MASKED, ALU.is_lt, ALU.mult))
            link(nc.vector.tensor_scalar(o_sb[:, 0, 224:256], d, 15.0, MASKED, ALU.is_gt, ALU.mult))
            link(nc.vector.tensor_tensor(gm[:, 1, :], gm[:, 1, :], o_sb[:, 0, 224:256], ALU.add))
            link(nc.vector.tensor_scalar(gm[:, 2, 0:16], d[:, 0:16], 8.0, MASKED, ALU.is_lt, ALU.mult))
            link(nc.vector.tensor_scalar(gm[:, 2, 16:32], d[:, 16:32], 23.0, MASKED, ALU.is_gt, ALU.mult))
            dve.wait_ge(small_loaded, 64)
            link(nc.vector.tensor_scalar(nsink[:, :], sinkb[:, :], -1.0, None, ALU.mult))

            def bias_b_tables():
                for i in range(12):
                    kind = i % 3
                    bnk = Sb[(i // 2) % 2]
                    if i % 2 == 0:
                        dve.wait_ge(setup_pe, i // 2 + 1)
                    link(nc.vector.tensor_tensor(biasB[:, i, :].rearrange("p (r c) -> p r c", r=ROWS),
                                                 bnk[:, (i % 2) * 256:(i % 2 + 1) * 256].rearrange("p (r c) -> p r c", r=ROWS),
                                                 gm[:, kind, :].unsqueeze(1).to_broadcast([P, ROWS, BW]), ALU.add))
                    if i % 2 == 1:
                        nc.vector.memset(seed[:, 7:8], 0.0).then_inc(setup_dve, 1)
                        dve.wait_ge(setup_dve, 2 + i // 2)

            for ev in EVENTS:
                what, s = ev[0], ev[1]
                if what in ("x", "m", "o"):
                    t, b, u = ev[2], ev[3], ev[4]
                    if what == "o" and t == 0 and b == 0:
                        normalise_groups(s, link, rsqrt, dve)
                    dve.wait_ge(t_hi, T_HI[u])
                    src = Tb[u % 2][:, :].rearrange("p (k c) -> p k c", k=4)
                    if what == "o" and b == 1:
                        nc.vector.tensor_tensor(grid_view(xT[1], t), src[:, 0:2, :].rearrange("p k (r c) -> p k r c", r=ROWS),
                                                grid_view(xT[0], t).bitcast(F32), ALU.subtract)
                        nc.vector.tensor_tensor(xT[1][:, 6:8, t * P:(t + 1) * P], src[:, 2:4, :],
                                                xT[0][:, 6:8, t * P:(t + 1) * P].bitcast(F32), ALU.subtract)\
                            .then_inc(t_drained[u % 2], 1)
                    else:
                        tt = memT if what == "m" else xT
                        nc.vector.tensor_tensor(tt[1][:, 4 * b:4 * b + 4, t * P:(t + 1) * P], src,
                                                tt[0][:, 4 * b:4 * b + 4, t * P:(t + 1) * P].bitcast(F32),
                                                ALU.subtract).then_inc(t_drained[u % 2], 1)
                    if what == "m" and s == 0 and t == 1 and b == 1:
                        bias_b_tables()
                elif what == "C":
                    c, cu = ev[2], ev[3]
                    kind, g = CHUNKS[c]
                    bnk = Cb[cu % 2]
                    if kind in split_C:
                        dst, width = c_dest(kind, g)
                        dve.wait_ge(c_hi, C_HI[cu])
                        if kind == "qb":
                            for blk in range(4):
                                ins = nc.vector.scalar_tensor_tensor(
                                    by_block(dst[1])[:, :, blk, :], by_row(bnk[:, :])[:, :, blk, :], SCALE,
                                    by_block(dst[0].bitcast(F32))[:, :, blk, :], ALU.mult, ALU.subtract)
                        else:
                            ins = nc.vector.scalar_tensor_tensor(dst[1], bnk[:, 0:width], SCALE if kind[0] == "q" else 1.0,
                                                                 dst[0].bitcast(F32), ALU.mult, ALU.subtract)
                    else:
                        dve.wait_ge(c_ready[cu % 2], cu // 2 + 1)
                        if kind == "wo":
                            y = x_nat[:, :, g * P:(g + 1) * P]
                            ins = nc.vector.scalar_tensor_tensor(y, y, ALPHA, bnk[:, :].rearrange("p (t c) -> p t c", t=NT),
                                                                 ALU.mult, ALU.add)
                        elif kind == "mv":
                            ins = nc.vector.tensor_copy(mv[:, :, g * P:(g + 1) * P],
                                                        bnk[:, 0:256].rearrange("p (t c) -> p t c", t=2))
                        elif kind == "va":
                            ins = nc.vector.tensor_copy(va[:, :, :], bnk[:, :].rearrange("p (t c) -> p t c", t=NT))
                        else:
                            if s == 1 and g == 0:
                                dve.wait_ge(vb_stored, 16 * 8)
                                dve.wait_ge(route_psum, NT)
                            ins = nc.vector.tensor_copy(vstg[:, :, g * P:(g + 1) * P],
                                                        bnk[:, :].rearrange("p (t c) -> p t c", t=NT))
                    ins.then_inc(c_drained[cu % 2], 1)
                elif what == "S":
                    i, a = ev[2], ev[3]
                    kind, tile, h = UNIT_LIST[i]
                    gi, _ = group_of(s, i)
                    dve.wait_ge(s_ready[a % 2], a // 2 + 1)
                    if kind == "M":
                        nc.vector.tensor_reduce(negm[:, gi % 2, h:h + 1], Sb[a % 2][:, 0:MEM], AX.X, ALU.max,
                                                negate=True).then_inc(maxed, 1)
                    else:
                        u2 = T_OF_UNIT[a - 2]
                        dve.wait_ge(t_ready[u2 % 2], u2 // 2 + 1)
                        if kind == "A":
                            head = (h // 2) + 4 * (h % 2)
                            k0, w = key_range(tile)
                            off = k0 - (tile - 1) * P
                            bias, start = biasA[:, head, off:off + w], nsink[:, head:head + 1]
                        else:
                            w = 256
                            bias, start = biasB[:, h * 3 + (0, 1, 1, 2)[tile], :], 3.0e38
                        nc.vector.tensor_tensor_reduce(out=probs[:, a % 2, 0:w], in0=Sb[a % 2][:, 0:w], in1=bias,
                                                       scale=-1.0, scalar=start, op0=ALU.add, op1=ALU.min,
                                                       accum_out=negm[:, gi % 2, h:h + 1]).then_inc(biased, 1)
                        if kind == "A" and h == A_HEADS - 1:
                            dve.wait_ge(biased, s * 48 + i - 16 + 1)
                            nc.vector.tensor_tensor(
                                es[:, gi % 2, :].rearrange("p (a b) -> p b a", b=2),
                                negm[:, gi % 2, :].rearrange("p (a b) -> p b a", b=2),
                                sinkb[:, :].rearrange("p (b a) -> p b a", b=2), ALU.add).then_inc(sink_in, 1)
                elif what == "T":
                    i, a, u = ev[2], ev[3], ev[4]
                    if not (UNIT_LIST[i][0] == "M" or i % 4 == 1):
                        copy_probs(dve, nc.vector.tensor_copy, s, i, a, u)
                elif what == "PV":
                    i, a = ev[2], ev[3]
                    kind, tile, h = UNIT_LIST[i]
                    if h == HEADS[kind] - 1:
                        gi, _ = group_of(s, i)
                        nh = HEADS[kind]
                        den = sums[:, gi % 2, 0:nh]
                        dve.wait_ge(exped, a + 1)
                        if kind == "A":
                            dve.wait_ge(sink_exp, s * NT + tile + 1)
                            link(nc.vector.tensor_tensor(es[:, gi % 2, :], es[:, gi % 2, :], den, ALU.add))
                            den = es[:, gi % 2, :]
                        link(nc.vector.reciprocal(rden[:, gi % 2, 0:nh], den))
                        dve.wait_ge(pv_done, a + 1)
                        c0 = OCOL[kind]
                        dst = o_sb[:, tile, c0:c0 + nh * HD]
                        psv = Ob[gi % 2][:, 0:nh * HD]
                        rb = rden[:, gi % 2, 0:nh]
                        if kind == "A":
                            link(nc.vector.tensor_tensor(
                                dst.rearrange("p (b a d) -> p b a d", b=2, a=4),
                                psv.rearrange("p (a b d) -> p b a d", b=2, a=4),
                                rb.rearrange("p (a b) -> p b a", b=2).unsqueeze(3).to_broadcast([P, 2, 4, HD]),
                                ALU.mult))
                        else:
                            link(nc.vector.tensor_tensor(dst.rearrange("p (a d) -> p a d", a=nh),
                                                         psv.rearrange("p (a d) -> p a d", a=nh),
                                                         rb.unsqueeze(2).to_broadcast([P, nh, HD]), ALU.mult))
                        gl = gi % len(GROUPS)
                        nc.vector.bn_stats(stats[:, gl % TT, 0, :], dst).then_inc(o_drained[gi % 2], 1)
                        dve.wait_ge(o_drained[gi % 2], gi // 2 + 1)
                        link(nc.vector.bn_aggr(mvv[:, gl, :], stats[:, gl % TT, 0, :]))
                elif what == "LN":
                    c_waits(dve, s * NCH + NCH - 1)
                    for t in range(NT):
                        for half in range(2):
                            link(nc.vector.bn_stats(stats[:, t, half, :], x_nat[:, t, half * 512:(half + 1) * 512]))
                        link(nc.vector.bn_aggr(mvv[:, t, :], stats[:, t, :, :].rearrange("p a b -> p (a b)")))
                    link(nc.vector.tensor_scalar(nv[:, 0:NT], mvv[:, 0:NT, 1], EPS, None, ALU.add))
                    rsqrt(NT)
                    for t in range(NT):
                        nc.vector.tensor_scalar(x_nat[:, t, :], x_nat[:, t, :], mvv[:, t, 0:1], ny[:, t:t + 1],
                                                ALU.subtract, ALU.mult).then_inc(normed, 1)

            routing(dve, link)

            def lo_units(e, ws):
                for w in ws:
                    if w in POOL_LO:
                        continue
                    dve.wait_ge(unit_hi, e * UNITS + w + 1)
                    nc.vector.tensor_tensor(wu[1][:, w, :], raw[:, w % RAW, :], wu[0][:, w, :].bitcast(F32),
                                            ALU.subtract).then_inc(unit_lo_dve, 1)

            def xgT_los(j):
                dve.wait_ge(xgT_hi, j + 1)
                for b in range(2):
                    ins = nc.vector.tensor_tensor(xgT[1][:, 4 * b:4 * b + 4, :],
                                                  Tb[b][:, :].rearrange("p (k c) -> p k c", k=4),
                                                  xgT[0][:, 4 * b:4 * b + 4, :].bitcast(F32), ALU.subtract)
                ins.then_inc(xgT_lo, 1)

            def tile_first(j):
                dve.wait_ge(silu_done, j + 1)
                nc.vector.tensor_tensor(h_sb, sg, Cb[1][:, :], ALU.mult).then_inc(h_mid, 1)
                xgT_los(j + 1)
                dve.wait_ge(hT_hi, j + 1)
                nc.vector.tensor_tensor(hT[1], Sb[0][:, :].rearrange("p (k c) -> p k c", k=KF), hT[0].bitcast(F32),
                                        ALU.subtract).then_inc(hT_lo, 1)

            def tile_last(j):
                dve.wait_ge(units_used, j * UNITS + 2 * UNITS)
                dve.wait_ge(y_stored, j * 16 + 16)
                nc.vector.tensor_copy(y_sb[:, 512:1024], Ob[1][:, :]).then_inc(y_half[1], 1)

            lo_units(0, range(UNITS))
            xgT_los(0)
            with dve.Fori(0, NE - 1) as e:
                lo = dve.value_load(tiles_cum[0:1, bass.ds(e, 1)], min_val=0, max_val=SLOTS - 1)
                hi = dve.value_load(tiles_cum[0:1, bass.ds(e + 1, 1)], min_val=1, max_val=SLOTS - 1)
                with dve.If(lo < hi - 1):
                    with dve.Fori(lo, hi - 1) as j:
                        tile_first(j)
                        tile_last(j)
                lo_units(e + 1, range(0, 6))
                tile_first(hi - 1)
                lo_units(e + 1, range(6, UNITS))
                tile_last(hi - 1)
            lo = dve.value_load(tiles_cum[0:1, NE - 1:NE], min_val=0, max_val=SLOTS - 1)
            hi = dve.value_load(tiles_cum[0:1, NE:NE + 1], min_val=1, max_val=SLOTS - 1)
            with dve.Fori(lo, hi) as j:
                tile_first(j)
                tile_last(j)

            for t in range(TT):
                f = t % 2
                dve.wait_ge(fin_loaded[f], 48 * (t // 2 + 1))
                y1, y2, x1 = (raw[:, 3 * f + k, :] for k in range(3))
                o = o_sb[:, t % NT, :]
                if t >= NT:
                    dve.wait_ge(out_stored[t % NT], 16)
                link(nc.vector.tensor_scalar(x1, x1, ALPHA, None, ALU.mult))
                link(nc.vector.scalar_tensor_tensor(y1, y1, wts[:, 0, t:t + 1], x1, ALU.mult, ALU.add))
                nc.vector.scalar_tensor_tensor(o, y2, wts[:, 1, t:t + 1], y1, ALU.mult, ALU.add).then_inc(fin_acc, 1)
                dve.wait_ge(fin_acc, t + 1)
                for half in range(2):
                    link(nc.vector.bn_stats(stats[:, t, half, :], o[:, half * 512:(half + 1) * 512]))
                link(nc.vector.bn_aggr(mvv[:, t, :], stats[:, t, :, :].rearrange("p a b -> p (a b)")))
                link(nc.vector.tensor_scalar(nv[:, 0:1], mvv[:, t, 1:2], EPS, None, ALU.add))
                rsqrt(1)
                nc.vector.tensor_scalar(o, o, mvv[:, t, 0:1], ny[:, 0:1], ALU.subtract, ALU.mult).then_inc(fin_norm, 1)
                dve.wait_ge(fin_norm, t + 1)

        @block.tensor
        def _(pe):
            pe.wait_ge(setup_pool, 2)

            def three(out_ap, st, mvg, first, last, last_sem=None):
                ins = nc.tensor.matmul(out_ap, st[0], mvg[0], start=first, stop=False)
                ins = nc.tensor.matmul(out_ap, st[0], mvg[1], start=False, stop=False)
                ins = nc.tensor.matmul(out_ap, st[1], mvg[0], start=False, stop=last)
                return ins

            def bias_b_reverse():
                pe.wait_ge(biasb_loaded, 16 * ROWS)
                for i in range(6):
                    if i >= 2:
                        pe.wait_ge(setup_dve, i)
                    nc.tensor.matmul(Sb[i % 2][:, :], anti[:, :], o_sb[:, 1 + i // 2, (i % 2) * 512:(i % 2 + 1) * 512],
                                     start=True, stop=True).then_inc(setup_pe, 1)

            for ev in EVENTS:
                what, s = ev[0], ev[1]
                if what in ("x", "m", "o", "r"):
                    t, b, u = ev[2], ev[3], ev[4]
                    if u >= 2:
                        pe.wait_ge(t_drained[u % 2], u // 2)
                    if what == "x":
                        pe.wait_ge(x_loaded[s][t], 16)
                        src = x_nat[:, t, :]
                    elif what == "m":
                        pe.wait_ge(mem_loaded[s], 16)
                        src = mem_nat[:, t, :]
                    elif what == "o":
                        pe.wait_ge(mixed_done, s * NT + t + 1)
                        src = o_sb[:, t, :]
                    else:
                        pe.wait_ge(x1_ready, s * NT + t + 1)
                        src = x_nat[:, t, :]
                    for k in range(4):
                        ins = nc.tensor.transpose(Tb[u % 2][:, k * P:(k + 1) * P],
                                                  src[:, (4 * b + k) * P:(4 * b + k + 1) * P], ident[:, :])
                    ins.then_inc(t_ready[u % 2], 1)
                    if what == "m" and s == 0 and t == 1 and b == 1:
                        bias_b_reverse()
                elif what == "C":
                    c, cu = ev[2], ev[3]
                    kind, g = CHUNKS[c]
                    gg = s * NCH + c
                    sl = gg % 2
                    pe.wait_ge(chunk_lo, gg + 1)
                    if cu >= 2:
                        pe.wait_ge(c_drained[cu % 2], cu // 2)
                    if c == 0:
                        t_waits(pe, FIRST_T[s] + 11)
                    if kind == "wo" and g == 0:
                        t_waits(pe, LAST_O[s])
                    W = [wch[0][:, sl], wch[1][:, sl]]
                    bnk = Cb[cu % 2]
                    if kind in ("mv", "va", "vb", "wo"):
                        src = memT if kind == "mv" else xT
                        tiles = 2 if kind == "mv" else NT
                        for t in range(tiles):
                            for k in range(KD):
                                ins = three(bnk[:, t * P:(t + 1) * P],
                                            [src[0][:, k, t * P:(t + 1) * P], src[1][:, k, t * P:(t + 1) * P]],
                                            [W[0][:, k, :], W[1][:, k, :]], k == 0, k == KD - 1)
                    else:
                        src = memT if kind == "mk" else xT
                        width = MEM if kind == "mk" else S
                        for k in range(KD):
                            ins = three(bnk[:, 0:width], [W[0][:, k, :], W[1][:, k, :]],
                                        [src[0][:, k, :], src[1][:, k, :]], k == 0, k == KD - 1)
                    ins.then_inc(c_ready[cu % 2], 1)
                elif what == "S":
                    i, a = ev[2], ev[3]
                    kind, tile, h = UNIT_LIST[i]
                    if a == 0:
                        pe.wait_ge(setup_dve, 7)
                    if a >= 2:
                        s2, i2 = (a - 2) // NU, (a - 2) % NU
                        if UNIT_LIST[i2][0] == "M":
                            pe.wait_ge(exped, a - 1)
                        else:
                            pe.wait_ge(biased, s2 * 48 + i2 - 16 + 1)
                    if h == 0 and tile == 0:
                        c_waits(pe, s * NCH + {"M": 5, "A": 11, "B": 15}[kind])
                    bnk = Sb[a % 2]
                    if kind == "M":
                        lo_p = (h % 2) * HD
                        q = [t_[lo_p:lo_p + HD, h // 2, tile * P:(tile + 1) * P] for t_ in qmT]
                        kk = [t_[lo_p:lo_p + HD, h // 2, :] for t_ in mkT]
                        o = bnk[:, 0:MEM]
                    elif kind == "A":
                        lo_p = (h % 2) * HD
                        k0, w = key_range(tile)
                        q = [t_[lo_p:lo_p + HD, h // 2, tile * P:(tile + 1) * P] for t_ in qaT]
                        kk = [t_[lo_p:lo_p + HD, 0, k0:k0 + w] for t_ in kaT]
                        o = bnk[:, 0:w]
                    else:
                        lo_p = (h % 2) * HD
                        q = [t_[lo_p:lo_p + HD, h // 2, tile * P:(tile + 1) * P] for t_ in qbT]
                        kk = [t_[lo_p:lo_p + HD, h // 2, :].rearrange("p (r c) -> p r c", r=ROWS)
                              [:, :, WIN0[tile]:WIN0[tile] + BW] for t_ in kbT]
                        o = bnk[:, 0:256]
                    three(o, q, kk, True, True).then_inc(s_ready[a % 2], 1)
                elif what == "T":
                    i, a, u = ev[2], ev[3], ev[4]
                    kind, tile, h = UNIT_LIST[i]
                    w = key_range(tile)[1] if kind == "A" else 256
                    pe.wait_ge(exped, a + 1)
                    if u >= 2:
                        pe.wait_ge(t_drained[u % 2], u // 2)
                    for k in range(w // P):
                        ins = nc.tensor.transpose(Tb[u % 2][:, k * P:(k + 1) * P], probs[:, a % 2, k * P:(k + 1) * P],
                                                  ident[:, :])
                    ins.then_inc(t_ready[u % 2], 1)
                elif what == "PV":
                    i, a = ev[2], ev[3]
                    kind, tile, h = UNIT_LIST[i]
                    gi, _ = group_of(s, i)
                    u = T_OF_UNIT[a]
                    pe.wait_ge(t_drained[u % 2], u // 2 + 1)
                    if h == 0 and gi >= 2:
                        pe.wait_ge(o_drained[gi % 2], gi // 2)
                    if s == 1 and i == 0:
                        pe.wait_ge(sig_done, 1)
                    if kind == "M":
                        vs = [mv[:, k, h * HD:(h + 1) * HD] for k in range(2)]
                    elif kind == "A":
                        k0, w = key_range(tile)
                        vs = [va[:, k0 // P + k, (h % 2) * HD:(h % 2 + 1) * HD] for k in range(w // P)]
                    else:
                        if h == 0 and tile == 0:
                            pe.wait_ge(vbw_loaded, 16 * (s + 1))
                        vs = [vbw[:, 2 * tile + k, h * HD:(h + 1) * HD] for k in range(2)]
                    for k, v in enumerate(vs):
                        ins = nc.tensor.matmul(Ob[gi % 2][:, h * HD:(h + 1) * HD], probsT[:, a % 2, k * P:(k + 1) * P], v,
                                               start=(k == 0), stop=(k == len(vs) - 1))
                    ins.then_inc(pv_done, 1)
                elif what == "R":
                    t = ev[2]
                    for u in R_UNITS[(s, t)]:
                        pe.wait_ge(t_drained[u % 2], u // 2 + 1)
                    if t == 0:
                        pe.wait_ge(small_loaded, 64)
                        pe.wait_ge(o_drained[1], (s + 1) * len(GROUPS) // 2)
                    for k in range(KD):
                        ins = nc.tensor.matmul(Ob[1][:, t * NE:(t + 1) * NE], x1T[:, k, :], wr[:, k, :],
                                               start=(k == 0), stop=(k == KD - 1))
                    ins.then_inc(route_psum, 1)

            pe.wait_ge(mask_ready, 1)
            m = mask_b[:, :].rearrange("p (t e) -> p t e", t=TT)
            for i in range(TT):
                for k in range(i):
                    nc.tensor.matmul(Ob[0][:, i * NE:(i + 1) * NE], ones_b[:, :], m[:, k, :], start=(k == 0), stop=False)
                nc.tensor.matmul(Ob[0][:, i * NE:(i + 1) * NE], tri_b[:, :], m[:, i, :], start=(i == 0), stop=True)
            for k in range(TT):
                ins = nc.tensor.matmul(Ob[0][:, TT * NE:TT * NE + NE], ones_b[:, :], m[:, k, :], start=(k == 0),
                                       stop=(k == TT - 1))
            ins.then_inc(rank_done, 1)
            pe.wait_ge(onehot_ready, 1)
            for i in range(2 * TT):
                ins = nc.tensor.matmul(Ob[1][:, 0:SLOTS], vbw_flat[:, i * P:(i + 1) * P],
                                       scratch[:, 1664 + i * SLOTS:1664 + (i + 1) * SLOTS], start=(i == 0),
                                       stop=(i == 2 * TT - 1))
            ins.then_inc(idx_psum, 1)

            def transpose_rows(j):
                pe.wait_ge(xg_loaded, j * 16 + 16)
                for k in range(KD):
                    ins = nc.tensor.transpose(Tb[k // 4][:, (k % 4) * P:(k % 4 + 1) * P], xg[:, k * P:(k + 1) * P], ident[:, :])
                ins.then_inc(xgT_psum, 1)

            def unit_wait(e, w):
                lo_sem, owned = (unit_lo_pool, POOL_LO) if w in POOL_LO else (unit_lo_dve, DVE_LO)
                pe.wait_ge(lo_sem, e * len(owned) + len(owned) + owned.index(w) + 1)

            pe.wait_ge(routed, 1)
            transpose_rows(0)
            with pe.Fori(0, NE) as e:
                lo = pe.value_load(tiles_cum[0:1, bass.ds(e, 1)], min_val=0, max_val=SLOTS - 1)
                hi = pe.value_load(tiles_cum[0:1, bass.ds(e + 1, 1)], min_val=1, max_val=SLOTS - 1)
                with pe.Fori(lo, hi) as j:
                    pe.wait_ge(xgT_lo, j + 1)
                    for k in range(KD):
                        unit_wait(e, k)
                        st = [xgT[0][:, k, :], xgT[1][:, k, :]]
                        for a_, b_ in ((0, 0), (0, 1), (1, 0)):
                            for half in range(2):
                                ins = nc.tensor.matmul(Cb[half][:, :], st[a_], wu[b_][:, k, half * 512:(half + 1) * 512],
                                                       start=(k == 0 and a_ + b_ == 0), stop=(k == KD - 1 and a_ == 1))
                        ins.then_inc(units_used, 1)
                    transpose_rows(j + 1)
                    pe.wait_ge(h_mid, j + 2)
                    for f in range(KF):
                        ins = nc.tensor.transpose(Sb[0][:, f * P:(f + 1) * P], h_sb[:, f * P:(f + 1) * P], ident[:, :])
                    ins.then_inc(hT_psum, 1)
                    pe.wait_ge(hT_lo, j + 1)
                    pe.wait_ge(y_half[0], j + 1)
                    pe.wait_ge(y_half[1], j + 1)
                    for f in range(KF):
                        unit_wait(e, KD + f)
                        st = [hT[0][:, f, :], hT[1][:, f, :]]
                        for a_, b_ in ((0, 0), (0, 1), (1, 0)):
                            for half in range(2):
                                ins = nc.tensor.matmul(Ob[half][:, :], st[a_], wu[b_][:, KD + f, half * 512:(half + 1) * 512],
                                                       start=(f == 0 and a_ + b_ == 0), stop=(f == KF - 1 and a_ == 1))
                        ins.then_inc(units_used, 1)


_INS = ["x", "mem", "w_in", "w_mem_kv", "sink", "rpb", "grp_g", "w_out", "ln1_g", "ln1_b", "w_router", "router_bias",
        "w_gate", "w_up", "w_down", "ln2_g", "ln2_b"]


def kernel(x_prompt, x_sample, mem_prompt, mem_sample, w_in, w_mem_kv, sink_logits, rpb, grp_norm_g, w_out,
           ln1_g, ln1_b, w_router, router_bias, w_gate, w_up, w_down, ln2_g, ln2_b):
    import concourse.bacc as bacc
    import numpy as np
    from concourse.bass_utils import run_bass_kernel_spmd

    nc = bacc.Bacc("TRN2", target_bir_lowering=False, num_devices=1)
    given = {
        "x0": x_prompt, "x1": x_sample, "mem0": mem_prompt, "mem1": mem_sample, "w_in": w_in[0],
        "w_mem_kv": w_mem_kv[0], "sink": sink_logits[0], "rpb": rpb[0], "grp_g": np.asarray(grp_norm_g[0]).reshape(KD, P).T, "w_out": w_out[0],
        "ln1_g": ln1_g[0], "ln1_b": ln1_b[0], "w_router": w_router, "router_bias": router_bias,
        "w_gate": w_gate[0], "w_up": w_up[0], "w_down": w_down[0], "ln2_g": ln2_g[0], "ln2_b": ln2_b[0]}
    arrays, aps = {}, {}
    for name, a in given.items():
        a = np.ascontiguousarray(a)
        arrays[f"in_{name}"] = a
        aps[name] = nc.dram_tensor(f"in_{name}", a.shape, mybir.dt.from_np(a.dtype), kind="ExternalInput").ap()
    outs = [nc.dram_tensor(f"out_{s}", (1, S, D), F32, kind="ExternalOutput").ap() for s in range(NSEQ)]
    aps["x"] = [aps.pop("x0")[0], aps.pop("x1")[0]]
    aps["mem"] = [aps.pop("mem0")[0], aps.pop("mem1")[0]]
    build_kernel(nc, *[aps[n] for n in _INS], outs)
    r = run_bass_kernel_spmd(nc, [arrays], core_ids=[0]).results[0]
    return r["out_0"], r["out_1"]
```

```python
from contextlib import ExitStack

import concourse.bass as bass
from concourse import mybir

F32 = mybir.dt.float32
F32R = mybir.dt.float32r
BF16 = mybir.dt.bfloat16
I32 = mybir.dt.int32
ALU = mybir.AluOpType
ACT = mybir.ActivationFunctionType
AX = mybir.AxisListType

P = 128
D = 1024
KD = D // P
S = 512
NSEQ = 2
NT = S // P
TT = NSEQ * NT
HD = 64
A_HEADS, B_HEADS, M_HEADS = 8, 4, 4
WINDOW = 128
GRID_W, ROWS, NA_ROWS, NA_COLS = 64, 8, 8, 16
BW = 32
WIN0 = (0, 8, 24, 32)
MEM = 256
NE, NG, EG = 16, 4, 4
FE = 512
KF = FE // P
EPS = 1e-5
ALPHA = 2.0 ** 0.25
SCALE = HD ** -0.5
MASKED = -1.0e30
SLOTS = 32
A_Q, A_KV, B_W, M_W = 512, 128, 256, 256
IN_W = A_Q + 2 * A_KV + 3 * B_W + M_W
QA0, KA0, VA0 = 0, A_Q, A_Q + A_KV
QB0 = VA0 + A_KV
KB0, VB0 = QB0 + B_W, QB0 + 2 * B_W
QM0 = QB0 + 3 * B_W
UNITS = KD + KF
RAW = 6
POOL_LO = (1, 4, 7, 10)
DVE_LO = tuple(w for w in range(UNITS) if w not in POOL_LO)


def key_range(n):
    k0 = max(0, (n - 1) * P)
    return k0, min(S, (n + 2) * P) - k0


def chunk_order():
    c = [("mk", 0), ("mk", 1), ("mv", 0), ("mv", 1), ("qm", 0), ("qm", 1)]
    c += [("qa", g) for g in range(4)] + [("ka", 0), ("va", 0)]
    c += [("qb", 0), ("qb", 1), ("kb", 0), ("kb", 1), ("vb", 0), ("vb", 1)]
    return c + [("wo", g) for g in range(8)]


VALUES = ("mv", "va", "vb")


CHUNKS = chunk_order()
NCH = len(CHUNKS)
UNIT_LIST = ([("M", n, h) for n in range(NT) for h in range(M_HEADS)]
             + [("A", n, h) for n in range(NT) for h in range(A_HEADS)]
             + [("B", n, h) for n in range(NT) for h in range(B_HEADS)])
NU = len(UNIT_LIST)
GROUPS = [(k, n) for k in "MAB" for n in range(NT)]
HEADS = {"M": M_HEADS, "A": A_HEADS, "B": B_HEADS}
OCOL = {"A": 0, "B": A_Q, "M": A_Q + B_W}


def schedule():
    ev, tu, late = [], [0], []

    def t_unit(*e):
        ev.append((*e, tu[0]))
        tu[0] += 1

    def inputs(s):
        for kind, tiles in (("m", MEM // P), ("x", NT)) if s else (("x", NT), ("m", MEM // P)):
            for t in range(tiles):
                for b in range(2):
                    t_unit(kind, s, t, b)

    def chunk(s, c):
        ev.append(("C", s, c, s * NCH + c))
        if late:
            t_unit("v", *late.pop())
        if CHUNKS[c][0] in VALUES:
            late.append((s, c))

    for s in range(NSEQ):
        if s == 0:
            inputs(0)
        for c in range(6):
            chunk(s, c)
            if s == 0 and c == 1:
                ev.append(("BB", 0))
            if s > 0 and c < NT:
                ev.append(("LN", s - 1, c))
        if s > 0:
            for t in range(NT):
                for b in range(2):
                    t_unit("r", s - 1, t, b)
                ev.append(("R", s - 1, t))
        nxt = 6
        for i in range(NU + 2):
            if i < NU:
                ev.append(("S", s, i, s * NU + i))
            if 1 <= i <= NU:
                t_unit("T", s, i - 1, s * NU + i - 1)
            if i >= 2:
                ev.append(("PV", s, i - 2, s * NU + i - 2))
            if nxt < 12 and i < 16 and i * 6 // 14 + 7 > nxt:
                chunk(s, nxt)
                nxt += 1
            elif 16 <= i < 48 and nxt < 18 and (i - 14) // 4 + 12 > nxt:
                chunk(s, nxt)
                nxt += 1
            elif late:
                t_unit("v", *late.pop())
        for n in range(NT):
            for b in range(2):
                t_unit("o", s, n, b)
        while nxt < NCH:
            chunk(s, nxt)
            nxt += 1
        ev.append(("VAR", s))
        if s + 1 < NSEQ:
            inputs(s + 1)
    for t in range(NT):
        ev.append(("LN", NSEQ - 1, t))
    for t in range(NT):
        for b in range(2):
            t_unit("r", NSEQ - 1, t, b)
        ev.append(("R", NSEQ - 1, t))
    return ev, tu[0]


EVENTS, N_TU = schedule()
T_OF_UNIT = {e[3]: e[4] for e in EVENTS if e[0] == "T"}
T_OF_VALUES = {(e[1], *CHUNKS[e[2]]): e[3] for e in EVENTS if e[0] == "v"}
LAST_IN = [max(e[4] for e in EVENTS if e[0] in ("x", "m") and e[1] == s) for s in range(NSEQ)]
LAST_M = [max(e[4] for e in EVENTS if e[0] == "m" and e[1] == s) for s in range(NSEQ)]
LAST_O = [max(e[4] for e in EVENTS if e[0] == "o" and e[1] == s) for s in range(NSEQ)]
R_UNITS = {(s, t): [e[4] for e in EVENTS if e[0] == "r" and e[1:3] == (s, t)] for s in range(NSEQ) for t in range(NT)}


def build_kernel(nc, x, mem, w_in, w_mem_kv, sink, rpb, grp_g, w_out, ln1_g, ln1_b, w_router, router_bias,
                 w_gate, w_up, w_down, ln2_g, ln2_b, out):
    with ExitStack() as ctx:
        def sb(name, shape, dt=F32):
            return ctx.enter_context(nc.sbuf_tensor(name, shape, dt))

        def sem(name):
            return ctx.enter_context(nc.semaphore(name))

        def bank(name):
            return ctx.enter_context(nc.psum_tensor(name, [P, 512], F32))

        x1_dram = nc.dram_tensor("x1_dram", (TT * P, D), F32).ap()
        vbw_dram = nc.dram_tensor("vbw_dram", (NSEQ, 4, ROWS, BW, B_W), F32).ap()
        biasb_dram = nc.dram_tensor("biasb_dram", (12, 16, 15, BW), F32).ap()
        y_dram = nc.dram_tensor("y_dram", (SLOTS * P, D), F32).ap()
        pad_dram = nc.dram_tensor("pad_dram", (B_HEADS, 15, 64), F32).ap()

        R = sb("split_main", [P, 24576], F32R)
        RX = sb("split_aux", [P, 3072], F32R)

        def cut(t, at, *shape):
            n = 1
            for d in shape:
                n *= d
            ap = t[:, at:at + n]
            if len(shape) == 2:
                ap = ap.rearrange("p (a b) -> p a b", a=shape[0])
            if len(shape) == 3:
                ap = ap.rearrange("p (a b c) -> p a b c", a=shape[0], b=shape[1])
            return ap

        xT = [cut(R, 0, KD, S), cut(R, 4096, KD, S)]
        memT = [cut(R, 8192, KD, MEM), cut(R, 10240, KD, MEM)]
        qbT = [cut(R, 8192, 2, S), cut(R, 9216, 2, S)]
        kbT = [cut(R, 10240, 2, S), cut(R, 11264, 2, S)]
        wch = [cut(R, 12288, 2, KD, P), cut(R, 14336, 2, KD, P)]
        qaT = [cut(R, 16384, 4, S), cut(R, 18432, 4, S)]
        kaT = [cut(R, 20480, 1, S), cut(R, 20992, 1, S)]
        qmT = [cut(R, 21504, 2, S), cut(R, 22528, 2, S)]
        mkT = [cut(R, 23552, 2, MEM), cut(R, 24064, 2, MEM)]
        wu = [cut(R, 0, UNITS, 1024), cut(R, 12288, UNITS, 1024)]
        xgT = [cut(RX, 0, KD, P), cut(RX, 1024, KD, P)]
        hT = [cut(RX, 2048, KF, P), cut(RX, 2560, KF, P)]

        x_nat = sb("x_nat", [P, NT, D])
        tables = sb("tables", [P, 6144])
        biasA = cut(tables, 0, A_HEADS, 3 * P)
        biasB = cut(tables, 3072, 12, 256)
        raw = cut(tables, 0, RAW, 1024)
        va = sb("va", [P, NT, A_KV])
        vbw = sb("vbw", [P, 8, B_W])
        mem_nat = vbw[:, :, :].rearrange("p (t a) b -> p t (a b)", t=2)
        mv = sb("mv", [P, 2, M_W])
        vstg = sb("vstg", [P, NT, B_W])
        x1T = vstg[:, :, :].rearrange("p a (b c) -> p (a b) c", c=P)
        probs = sb("probs", [P, 2, 384])
        probsT = sb("probsT", [P, 2, 384])
        o_sb = sb("o_sb", [P, NT, D])
        wraw = sb("wraw", [P, 2, KD, P])
        ln = sb("ln", [P, 2, D])
        ident = sb("ident", [P, P])
        anti = sb("anti", [P, P])
        ones_b = sb("ones_b", [P, P], BF16)
        tri_b = sb("tri_b", [P, P], BF16)
        wr = sb("wr", [P, KD, NE])
        gcol = sb("gcol", [P, KD])
        sinkb = sb("sinkb", [P, A_HEADS])
        nsink = sb("nsink", [P, A_HEADS])
        rbb = sb("rbb", [P, NE])
        negm = sb("negm", [P, 2, A_HEADS])
        sums = sb("sums", [P, 2, A_HEADS])
        es = sb("es", [P, 2, A_HEADS])
        rden = sb("rden", [P, 2, A_HEADS])
        stats = sb("stats", [P, TT, 2, 6])
        mvv = sb("mvv", [P, 12, 2])
        nv = sb("nv", [P, 12])
        ny = sb("ny", [P, 12])
        rstd = sb("rstd", [P, TT])
        nt_ = sb("nt_", [P, 12])
        sc = sb("sc", [P, TT, NE])
        idxc = sb("idxc", [P, 1], I32)
        idx = sb("idx", [P, SLOTS], I32)
        tiles_cum = sb("tiles_cum", [P, NE + 2], I32)
        slot_i = sb("slot_i", [P, 2, TT], I32)
        wts = sb("wts", [P, 2, TT])
        riota = sb("riota", [P, P])
        tokf = sb("tokf", [P, TT])
        mask_b = sb("mask_b", [P, TT * NE], BF16)
        carry = sb("carry", [1, 3])
        izero = sb("izero", [P, 1], I32)
        ints = sb("ints", [P, 32], I32)
        seed = sb("seed", [P, 12])
        scol = sb("scol", [P, 2], I32)

        scratch = o_sb[:, :, :].rearrange("p a b -> p (a b)")
        vbw_flat = vbw[:, :, :].rearrange("p a b -> p (a b)")
        vT = o_sb[:, 2:4, A_Q:A_Q + B_W]
        xg = x_nat[:, 0, :]
        y_sb = x_nat[:, 1, :]
        sg = x_nat[:, 2, 0:512]
        h_sb = x_nat[:, 3, 0:512]
        zeros = x_nat[:, 3, 512:1024]

        Cb = [bank("C0"), bank("C1")]
        Tb = [bank("T0"), bank("T1")]
        Sb = [bank("S0"), bank("S1")]
        Ob = [bank("O0"), bank("O1")]

        x_loaded = [[sem(f"x_loaded{s}_{t}") for t in range(NT)] for s in range(NSEQ)]
        mem_loaded = [sem(f"mem_loaded{s}") for s in range(NSEQ)]
        small_loaded = sem("small_loaded")
        ln_loaded = sem("ln_loaded")
        ln2_loaded = sem("ln2_loaded")
        rpb_loaded = sem("rpb_loaded")
        pad_stored = sem("pad_stored")
        biasb_loaded = sem("biasb_loaded")
        biasb_spread = sem("biasb_spread")
        chunk_loaded = [sem("chunk_loaded0"), sem("chunk_loaded1")]
        chunk_scaled = sem("chunk_scaled")
        chunk_hi = sem("chunk_hi")
        chunk_lo = sem("chunk_lo")
        t_ready = [sem("t_ready0"), sem("t_ready1")]
        t_hi = sem("t_hi")
        t_drained = [sem("t_drained0"), sem("t_drained1")]
        c_ready = [sem("c_ready0"), sem("c_ready1")]
        c_hi = sem("c_hi")
        c_drained = [sem("c_drained0"), sem("c_drained1")]
        s_ready = [sem("s_ready0"), sem("s_ready1")]
        biased = sem("biased")
        maxed = sem("maxed")
        exped = sem("exped")
        pv_done = sem("pv_done")
        o_drained = [sem("o_drained0"), sem("o_drained1")]
        sink_in = sem("sink_in")
        sink_exp = sem("sink_exp")
        vb_stored = sem("vb_stored")
        vbw_loaded = sem("vbw_loaded")
        v_staged = sem("v_staged")
        wo_ready = sem("wo_ready")
        wo_drained = sem("wo_drained")
        x_again = [sem(f"x_again{t}") for t in range(NT)]
        mixed_done = sem("mixed_done")
        normed = sem("normed")
        x1_ready = sem("x1_ready")
        x1_stored = sem("x1_stored")
        route_psum = sem("route_psum")
        sig_done = sem("sig_done")
        setup_pool = sem("setup_pool")
        setup_dve = sem("setup_dve")
        setup_pe = sem("setup_pe")
        dch = sem("dve_chain")
        pch = sem("pool_chain")
        mask_ready = sem("mask_ready")
        rank_done = sem("rank_done")
        onehot_ready = sem("onehot_ready")
        onehot_used = sem("onehot_used")
        idx_psum = sem("idx_psum")
        routed = sem("routed")
        raw_loaded = [sem(f"raw_loaded{i}") for i in range(RAW)]
        unit_hi = sem("unit_hi")
        unit_lo_dve = sem("unit_lo_dve")
        unit_lo_pool = sem("unit_lo_pool")
        units_used = sem("units_used")
        xg_idx = sem("xg_idx")
        xg_loaded = sem("xg_loaded")
        xgT_psum = sem("xgT_psum")
        xgT_hi = sem("xgT_hi")
        xgT_lo = sem("xgT_lo")
        silu_done = sem("silu_done")
        h_mid = sem("h_mid")
        hT_psum = sem("hT_psum")
        hT_hi = sem("hT_hi")
        hT_lo = sem("hT_lo")
        y_half = [sem("y_half0"), sem("y_half1")]
        y_stored = sem("y_stored")
        y_zeroed = sem("y_zeroed")
        fin_loaded = [sem("fin_loaded0"), sem("fin_loaded1")]
        fin_acc = sem("fin_acc")
        fin_norm = sem("fin_norm")
        fin_scaled = sem("fin_scaled")
        fin_rstd = sem("fin_rstd")
        fin_y = sem("fin_y")
        out_stored = [sem(f"out_stored{i}") for i in range(NT)]

        win_v = w_in.rearrange("(k p) c -> p k c", p=P)
        wkv_v = w_mem_kv.rearrange("(k p) c -> p k c", p=P)
        wo_v = w_out.rearrange("(k p) c -> p k c", p=P)

        chunk_src = {"mk": (wkv_v, 0), "mv": (wkv_v, M_W), "qm": (win_v, QM0), "ka": (win_v, KA0), "va": (win_v, VA0),
                     "qb": (win_v, QB0), "kb": (win_v, KB0), "vb": (win_v, VB0), "wo": (wo_v, 0)}

        def chunk_loads(g):
            n = 0
            for i in range(g % 2, g + 1, 2):
                n += 32 if CHUNKS[i % NCH][0] == "qa" else 16
            return n

        split_T = [e for e in EVENTS if e[0] in ("x", "m", "o")]
        T_HI = {e[4]: i + 1 for i, e in enumerate(split_T)}
        split_C = ("mk", "qm", "qa", "ka", "qb", "kb")
        C_HI = {}
        for s_ in range(NSEQ):
            for c_, (kind_, _) in enumerate(CHUNKS):
                if kind_ in split_C:
                    C_HI[s_ * NCH + c_] = len(C_HI) + 1
        C_OUT = {}
        for b in range(2):
            n_out = 0
            for cu in range(b, NSEQ * NCH, 2):
                n_out += CHUNKS[cu % NCH][0] != "wo"
                C_OUT[cu] = n_out
        V_TURNED = [e[3] for e in EVENTS if e[0] == "v"]
        V_UNITS = [c for c, (kind_, _) in enumerate(CHUNKS) if kind_ in VALUES]

        def wo_bank(half, t):
            return ([Sb[0], Sb[1], Ob[0], Ob[1]], [Cb[0], Cb[1], Sb[0], Sb[1]])[half][t]

        GI = {kn: i for i, kn in enumerate(GROUPS)}

        def group_of(s, i):
            k, n, h = UNIT_LIST[i]
            return s * len(GROUPS) + GI[(k, n)], h

        def t_waits(eng, last_unit):
            for b in range(2):
                eng.wait_ge(t_drained[b], (last_unit - b) // 2 + 1)

        def c_waits(eng, cu):
            for b in range(2):
                if cu - b >= 0:
                    eng.wait_ge(c_drained[b], C_OUT[cu - (cu - b) % 2])

        def by_pair(slot):
            return slot.rearrange("p (a b) c -> p a (b c)", a=2)

        def chunk_cu(s, kind, g):
            return s * NCH + CHUNKS.index((kind, g))

        def grid_view(xt, n):
            v = xt[:, 4:6, :].rearrange("p k (r c) -> p k r c", r=ROWS)
            return v[:, :, :, n * 16:(n + 1) * 16]

        def by_row(ap):
            return ap.rearrange("p (r n c) -> p r n c", r=ROWS, n=4)

        def by_block(ap):
            return ap.rearrange("p (n r c) -> p r n c", r=ROWS, n=4)

        def hT_part(part, i):
            return hT[part][:, 2 * i:2 * i + 2, :], Sb[i][:, 0:256].rearrange("p (k c) -> p k c", k=2)

        def c_dest(kind, g):
            t = {"mk": mkT, "qm": qmT, "qa": qaT, "ka": kaT, "qb": qbT, "kb": kbT}[kind]
            return [t[0][:, g, :], t[1][:, g, :]], (MEM if kind == "mk" else S)

        def copy_probs(eng, copy, s, i, a, u):
            kind, tile, h = UNIT_LIST[i]
            w = key_range(tile)[1] if kind == "A" else 256
            eng.wait_ge(t_ready[u % 2], u // 2 + 1)
            if a >= 2:
                eng.wait_ge(pv_done, a - 1)
            copy(probsT[:, a % 2, 0:w], Tb[u % 2][:, 0:w]).then_inc(t_drained[u % 2], 1)

        def normalise_groups(s, link, rsqrt, dve):
            link(nc.vector.tensor_tensor(nv[:, :], mvv[:, :, 0], mvv[:, :, 0], ALU.mult))
            link(nc.vector.tensor_tensor(nv[:, :], nv[:, :], mvv[:, :, 1], ALU.add))
            link(nc.vector.tensor_scalar(nv[:, :], nv[:, :], EPS, None, ALU.add))
            rsqrt(ny[:, :], 12)
            for tile in range(NT):
                for kind in "ABM":
                    c0, w = OCOL[kind], HEADS[kind] * HD
                    gl = GI[(kind, tile)]
                    ins = nc.vector.tensor_scalar(o_sb[:, tile, c0:c0 + w], o_sb[:, tile, c0:c0 + w],
                                                  ny[:, gl:gl + 1], None, ALU.mult)
                ins.then_inc(mixed_done, 1)

        def routing(dve, link):
            G = TT * NG
            sel = cut(scratch, 0, TT, NE)
            w16 = [cut(scratch, 128 * i, G, EG) for i in range(8)]
            w32 = [scratch[:, 1024 + 32 * i:1024 + 32 * (i + 1)] for i in range(6)]
            w8 = [scratch[:, 1280 + 8 * i:1280 + 8 * (i + 1)] for i in range(8)]
            selv = w16[0]
            rev4 = w16[7]
            dve.wait_ge(sig_done, NSEQ)
            dve.wait_ge(x1_stored, 16 * TT)
            link(nc.vector.memset(zeros, 0.0))
            for i in range(EG):
                link(nc.vector.memset(rev4[:, :, i], float(EG - i)))
            link(nc.vector.tensor_tensor(sel, sc[:, :, :], rbb[:, :].unsqueeze(1).to_broadcast([P, TT, NE]), ALU.add))

            def first_max(v, m, oh, rows, key, mk, rev):
                link(nc.vector.tensor_reduce(m, v, AX.X, ALU.max))
                link(nc.vector.tensor_tensor(key, v, m.unsqueeze(2).to_broadcast([P, rows, 4]), ALU.is_equal))
                link(nc.vector.tensor_tensor(key, key, rev, ALU.mult))
                link(nc.vector.tensor_reduce(mk, key, AX.X, ALU.max))
                link(nc.vector.tensor_tensor(oh, key, mk.unsqueeze(2).to_broadcast([P, rows, 4]), ALU.is_equal))

            m1, m2, mk = w32[0], w32[1], w32[2]
            oh1, oh2, key, sel2 = w16[1], w16[2], w16[3], w16[4]
            first_max(selv, m1, oh1, G, key, mk, rev4)
            link(nc.vector.scalar_tensor_tensor(sel2, oh1, MASKED, selv, ALU.mult, ALU.add))
            first_max(sel2, m2, oh2, G, key, mk, rev4)
            link(nc.vector.tensor_tensor(m1, m1, m2, ALU.add))
            gsc = m1.rearrange("p (t g) -> p t g", t=TT)
            gkey = w32[3].rearrange("p (t g) -> p t g", t=TT)
            goh = w32[4].rearrange("p (t g) -> p t g", t=TT)
            first_max(gsc, w8[0], goh, TT, gkey, w8[1], rev4[:, 0:TT, :])
            gb = w32[4].unsqueeze(2).to_broadcast([P, G, EG])
            link(nc.vector.tensor_tensor(oh1, oh1, gb, ALU.mult))
            link(nc.vector.tensor_tensor(oh2, oh2, gb, ALU.mult))
            link(nc.vector.tensor_tensor(cut(mask_b, 0, G, EG), oh1, oh2, ALU.add))
            nc.vector.memset(seed[:, 6:7], 0.0).then_inc(mask_ready, 1)

            E1, E2 = cut(scratch, 128, TT, NE), cut(scratch, 256, TT, NE)
            tmp = cut(scratch, 384, TT, NE)
            w_a, w_b, w_s = w8[2], w8[3], w8[4]
            link(nc.vector.tensor_tensor(tmp, E1, sc[:, :, :], ALU.mult))
            link(nc.vector.tensor_reduce(w_a, tmp, AX.X, ALU.add))
            link(nc.vector.tensor_tensor(tmp, E2, sc[:, :, :], ALU.mult))
            link(nc.vector.tensor_reduce(w_b, tmp, AX.X, ALU.add))
            link(nc.vector.tensor_tensor(w_s, w_a, w_b, ALU.add))
            link(nc.vector.reciprocal(w_s, w_s))
            link(nc.vector.tensor_tensor(wts[:, 0, :], w_a, w_s, ALU.mult))
            link(nc.vector.tensor_tensor(wts[:, 1, :], w_b, w_s, ALU.mult))

            dve.wait_ge(rank_done, 1)
            thr = cut(scratch, 1408, NE, TT)
            for i in range(TT):
                link(nc.vector.memset(thr[:, :, i], float(P * i)))
            cmp = cut(scratch, 512, NE, TT)
            link(nc.vector.tensor_tensor(cmp, Ob[0][:, 128:128 + NE].unsqueeze(2).to_broadcast([P, NE, TT]), thr, ALU.is_gt))
            ntl, cum, base, one16 = (scratch[:, 1536 + 16 * i:1552 + 16 * i] for i in range(4))
            link(nc.vector.tensor_reduce(ntl, cmp, AX.X, ALU.add))
            link(nc.vector.tensor_scalar(ntl, ntl, 1.0, None, ALU.max))
            link(nc.vector.memset(one16, 1.0))
            link(nc.vector.tensor_tensor_scan(cum, one16, ntl, 0.0, ALU.mult, ALU.add))
            link(nc.vector.tensor_tensor(base, cum, ntl, ALU.subtract))
            link(nc.vector.tensor_copy(tiles_cum[:, 0:NE], base))
            link(nc.vector.tensor_copy(tiles_cum[:, NE:NE + 1], cum[:, NE - 1:NE]))
            link(nc.vector.tensor_scalar(tiles_cum[:, NE + 1:NE + 2], cum[:, NE - 1:NE], -1.0, float(SLOTS),
                                         ALU.mult, ALU.add))
            link(nc.vector.tensor_scalar(base, base, float(P), None, ALU.mult))
            pos = cut(scratch, 640, TT, NE)
            link(nc.vector.tensor_tensor(pos, Ob[0][:, 0:TT * NE].rearrange("p (t e) -> p t e", t=TT),
                                         base.unsqueeze(1).to_broadcast([P, TT, NE]), ALU.add))
            slot_f = scratch[:, 1600:1616]
            for c, E in enumerate((E1, E2)):
                link(nc.vector.tensor_tensor(tmp, E, pos, ALU.mult))
                link(nc.vector.tensor_reduce(slot_f[:, c * TT:(c + 1) * TT], tmp, AX.X, ALU.add))
            link(nc.vector.tensor_copy(slot_i[:, :, :].rearrange("p c t -> p (c t)"), slot_f))
            hi_i, lo_i = ints[:, 0:16], ints[:, 16:32]
            flat = slot_i[:, :, :].rearrange("p c t -> p (c t)")
            link(nc.vector.tensor_scalar(hi_i, flat, 7, None, ALU.logical_shift_right))
            link(nc.vector.tensor_scalar(lo_i, flat, P - 1, None, ALU.bitwise_and))
            hi_f, lo_f = scratch[:, 1616:1632], scratch[:, 1632:1648]
            link(nc.vector.tensor_copy(hi_f, hi_i))
            link(nc.vector.tensor_copy(lo_f, lo_i))
            rowoh = cut(vbw_flat, 0, 2 * TT, P)
            tileoh = cut(scratch, 1664, 2 * TT, SLOTS)
            for i in range(2 * TT):
                link(nc.vector.tensor_scalar(rowoh[:, i, :], riota[:, :], lo_f[:, i:i + 1], None, ALU.is_equal))
                link(nc.vector.tensor_scalar(tileoh[:, i, :], riota[:, 0:SLOTS], hi_f[:, i:i + 1],
                                             tokf[:, i % TT:i % TT + 1], ALU.is_equal, ALU.mult))
            nc.vector.memset(seed[:, 5:6], 0.0).then_inc(onehot_ready, 1)
            dve.wait_ge(idx_psum, 1)
            link(nc.vector.tensor_copy(idx[:, :], Ob[1][:, 0:SLOTS]))
            nc.vector.memset(seed[:, 4:5], 0.0).then_inc(routed, 1)

        block = ctx.enter_context(nc.Block())

        @block.sync
        def _(sp):
            for t in range(NT):
                sp.dma_start(x_nat[:, t, :], x[0][t * P:(t + 1) * P, :]).then_inc(x_loaded[0][t], 16)
            sp.dma_start(mem_nat, mem[0].rearrange("(t p) d -> p t d", p=P)).then_inc(mem_loaded[0], 16)

            def load_chunk(g):
                kind, i = CHUNKS[g % NCH]
                if g >= 2:
                    sp.wait_ge(chunk_lo, g - 1)
                slot = wraw[:, g % 2, :, :]
                if kind == "qa":
                    for half in range(2):
                        sp.dma_start(slot[:, :, half * HD:(half + 1) * HD],
                                     win_v[:, :, half * 256 + i * HD:half * 256 + (i + 1) * HD])\
                            .then_inc(chunk_loaded[g % 2], 16)
                else:
                    src, c0 = chunk_src[kind]
                    if kind == "wo":
                        half, pair = i // 4, i % 4
                        slot = by_pair(slot)
                        part = src[:, 2 * pair:2 * pair + 2, half * 512:(half + 1) * 512]
                    else:
                        part = src[:, :, c0 + i * P:c0 + (i + 1) * P]
                    sp.dma_start(slot, part).then_inc(chunk_loaded[g % 2], 16)

            def small_loads():
                sp.dma_start(wr[:, :, :], w_router.rearrange("(k p) e -> p k e", p=P)).then_inc(small_loaded, 16)
                sp.dma_start(gcol[:, :], grp_g).then_inc(small_loaded, 16)
                sp.dma_start(sinkb[:, :], sink.partition_broadcast(P)).then_inc(small_loaded, 16)
                sp.dma_start(rbb[:, :], router_bias.partition_broadcast(P)).then_inc(small_loaded, 16)
                sp.wait_ge(setup_dve, 1)
                sp.dma_start(o_sb[0:60, 0, 16:47], rpb.rearrange("h r c -> (h r) c")).then_inc(rpb_loaded, 16)
                sp.wait_ge(rpb_loaded, 16)
                sp.dma_start(pad_dram.rearrange("h r c -> (h r) c"), o_sb[0:60, 0, 0:64]).then_inc(pad_stored, 16)
                sp.wait_ge(pad_stored, 16)
                for h in range(B_HEADS):
                    for kind, delta in enumerate((0, -8, -16)):
                        src = bass.AP(pad_dram.tensor, h * 15 * 64 + 16 + delta, [[1, 16], [64, 15], [1, BW]])
                        sp.dma_start(biasb_dram[h * 3 + kind], src).then_inc(biasb_spread, 16)
                sp.wait_ge(biasb_spread, 16 * 12)
                for rr in range(ROWS):
                    sp.dma_start(o_sb[rr * 16:(rr + 1) * 16, 1:4, :].rearrange("p a (b c) -> p (a b) c", c=256),
                                 biasb_dram[:, :, rr:rr + ROWS, :].rearrange("n i a b -> i n (a b)"))\
                        .then_inc(biasb_loaded, 16)
                sp.dma_start(ln[:, 0, :], ln1_g.partition_broadcast(P)).then_inc(ln_loaded, 16)
                sp.dma_start(ln[:, 1, :], ln1_b.partition_broadcast(P)).then_inc(ln_loaded, 16)

            for g in range(NSEQ * NCH):
                load_chunk(g)
                if g == 1:
                    small_loads()
                s, c = g // NCH, g % NCH
                if c == CHUNKS.index(("vb", 1)) + 2:
                    t_waits(sp, T_OF_VALUES[(s, "vb", 1)])
                    for w in range(4):
                        for odd in range(2):
                            p0 = odd * GRID_W + WIN0[w]
                            sp.dma_start(vbw_dram[s, w].rearrange("(t o) c d -> o c t d", o=2)[odd],
                                         vstg[p0:p0 + BW, :, :]).then_inc(vb_stored, 16)
                    sp.wait_ge(vb_stored, 16 * 8 * (s + 1))
                    sp.dma_start(vbw[:, :, :], vbw_dram[s].rearrange("w (h r) c d -> (r c) (w h) d", h=2))\
                        .then_inc(vbw_loaded, 16)

            sp.wait_ge(biased, 2 * (32 + 16))
            with sp.Fori(0, NE) as e:
                for w in range(UNITS):
                    slot = w % RAW
                    lo_sem, owned = (unit_lo_pool, POOL_LO) if w in POOL_LO else (unit_lo_dve, DVE_LO)
                    if w < RAW:
                        sp.wait_ge(lo_sem, e * len(owned) + owned.index(w + RAW) + 1)
                    else:
                        sp.wait_ge(lo_sem, e * len(owned) + len(owned) + owned.index(w - RAW) + 1)
                    if w < KD:
                        src = (w_gate, w_up)[w // 4][bass.ds(e, 1), (w % 4) * 2 * P:(w % 4 + 1) * 2 * P, :]
                        sp.dma_start(raw[:, slot, :].rearrange("p (k c) -> p k c", k=2),
                                     src.rearrange("a (k p) c -> p (a k) c", p=P)).then_inc(raw_loaded[slot], 16)
                    else:
                        src = w_down[bass.ds(e, 1), (w - KD) * P:(w - KD + 1) * P, :]
                        sp.dma_start(raw[:, slot, :], src.rearrange("a p c -> (a p) c")).then_inc(raw_loaded[slot], 16)

            for t in range(TT):
                sp.wait_ge(fin_y, t + 1)
                sp.dma_start(out[t // NT][0, (t % NT) * P:(t % NT + 1) * P, :], o_sb[:, t % NT, :])\
                    .then_inc(out_stored[t % NT], 16)
            for i in range(NT):
                sp.wait_ge(out_stored[i], 16 * NSEQ)

        @block.gpsimd
        def _(pool):
            n = [0]

            def link(i):
                n[0] += 1
                i.then_inc(pch, 1)
                pool.wait_ge(pch, n[0])

            link(nc.gpsimd.memset(ident[:, :], 0.0))
            link(nc.gpsimd.memset(anti[:, :], 0.0))
            link(nc.gpsimd.memset(izero[:, :], 0))
            nc.gpsimd.affine_select(out=ident[:, :], in_=ident[:, :], compare_op=ALU.not_equal, fill=1.0, base=0,
                                    pattern=[[-1, P]], channel_multiplier=1).then_inc(setup_pool, 1)
            nc.gpsimd.affine_select(out=anti[:, :], in_=anti[:, :], compare_op=ALU.not_equal, fill=1.0, base=-(P - 1),
                                    pattern=[[1, P]], channel_multiplier=1).then_inc(setup_pool, 1)
            nc.gpsimd.memset(ones_b[:, :], 1.0).then_inc(setup_pool, 1)
            pool.wait_ge(setup_pool, 3)
            nc.gpsimd.affine_select(out=tri_b[:, :], in_=ones_b[:, :], compare_op=ALU.is_gt, fill=0.0, base=0,
                                    pattern=[[1, P]], channel_multiplier=-1).then_inc(setup_pool, 1)
            nc.gpsimd.iota(o_sb[:, 0, 512:896], pattern=[[-1, 3 * P]], base=P, channel_multiplier=1,
                           allow_small_or_imprecise_dtypes=True).then_inc(setup_pool, 1)
            nc.gpsimd.iota(scol[:, 0:1], pattern=[[0, 1]], base=0, channel_multiplier=1).then_inc(setup_pool, 1)
            nc.gpsimd.iota(o_sb[:, 0, 64:96], pattern=[[1, BW]], base=0, channel_multiplier=0,
                           allow_small_or_imprecise_dtypes=True).then_inc(setup_pool, 1)
            nc.gpsimd.iota(riota[:, :], pattern=[[1, P]], base=0, channel_multiplier=0,
                           allow_small_or_imprecise_dtypes=True).then_inc(setup_pool, 1)
            nc.gpsimd.iota(tokf[:, :], pattern=[[P, TT]], base=0, channel_multiplier=1,
                           allow_small_or_imprecise_dtypes=True).then_inc(setup_pool, 1)

            def lo_chunk(g):
                kind, _ = CHUNKS[g % NCH]
                slot = g % 2
                if kind == "wo":
                    pool.wait_ge(chunk_loaded[slot], chunk_loads(g))
                    pool.wait_ge(small_loaded, 64)
                    pair = CHUNKS[g % NCH][1] % 4
                    w = by_pair(wraw[:, slot, :, :])
                    nc.gpsimd.tensor_tensor(w, w, gcol[:, 2 * pair:2 * pair + 2].unsqueeze(2).to_broadcast([P, 2, 512]),
                                            ALU.mult).then_inc(chunk_scaled, 1)
                pool.wait_ge(chunk_hi, g + 1)
                nc.gpsimd.tensor_tensor(wch[1][:, slot, :, :], wraw[:, slot, :, :], wch[0][:, slot, :, :].bitcast(F32),
                                        ALU.subtract).then_inc(chunk_lo, 1)

            def lo_first_expert(ws):
                for w in ws:
                    pool.wait_ge(unit_hi, w + 1)
                    nc.gpsimd.tensor_tensor(wu[1][:, w, :], raw[:, w % RAW, :], wu[0][:, w, :].bitcast(F32),
                                            ALU.subtract).then_inc(unit_lo_pool if w in POOL_LO else unit_lo_dve, 1)

            for ev in EVENTS:
                what, s = ev[0], ev[1]
                if what == "C":
                    g = ev[3]
                    if g == 0:
                        lo_chunk(0)
                        lo_chunk(1)
                    if g + 2 < NSEQ * NCH:
                        lo_chunk(g + 2)
                elif what == "o" and s == 0 and ev[3] == 1:
                    t, u = ev[2], ev[4]
                    if t == 0:
                        pool.wait_ge(pv_done, NU)
                        pool.dma_start(mem_nat, mem[1].rearrange("(t p) d -> p t d", p=P)).then_inc(mem_loaded[1], 16)
                    for v in (u - 1, u):
                        pool.wait_ge(t_ready[v % 2], v // 2 + 1)
                    pool.dma_start(o_sb[:, t, :], x[1][t * P:(t + 1) * P, :]).then_inc(x_loaded[1][t], 16)
                elif what == "LN":
                    t = ev[2]
                    pool.wait_ge(ln_loaded, 32)
                    pool.wait_ge(normed, s * NT + t + 1)
                    nc.gpsimd.tensor_tensor(x_nat[:, t, :], x_nat[:, t, :], ln[:, 1, :], ALU.add).then_inc(x1_ready, 1)
                    pool.wait_ge(x1_ready, s * NT + t + 1)
                    pool.dma_start(x1_dram[(s * NT + t) * P:(s * NT + t + 1) * P, :], x_nat[:, t, :]).then_inc(x1_stored, 16)
                elif what == "R" and s == 0:
                    t = ev[2]
                    if t == 0:
                        pool.wait_ge(x1_stored, 16 * NT)
                    for u in R_UNITS[(0, t)]:
                        pool.wait_ge(t_ready[u % 2], u // 2 + 1)
                    pool.dma_start(x_nat[:, t, :], x[1][t * P:(t + 1) * P, :]).then_inc(x_again[t], 16)
            pool.dma_start(ln[:, 0, :], ln2_g.partition_broadcast(P)).then_inc(ln2_loaded, 16)
            pool.dma_start(ln[:, 1, :], ln2_b.partition_broadcast(P)).then_inc(ln2_loaded, 16)
            lo_first_expert(range(UNITS))

            pool.wait_ge(routed, 1)

            def gather():
                nc.gpsimd.indirect_dma_start(xg, None, x1_dram, bass.IndirectOffsetOnAxis(idxc[:, 0:1], 0))\
                    .then_inc(xg_loaded, 16)

            nc.gpsimd.tensor_copy(idxc[:, :], idx[:, 0:1]).then_inc(xg_idx, 1)
            pool.wait_ge(xg_idx, 1)
            gather()

            def lo_units(e):
                for w in POOL_LO:
                    pool.wait_ge(unit_hi, e * UNITS + w + 1)
                    nc.gpsimd.tensor_tensor(wu[1][:, w, :], raw[:, w % RAW, :], wu[0][:, w, :].bitcast(F32),
                                            ALU.subtract).then_inc(unit_lo_pool, 1)

            def next_gather(j):
                pool.wait_ge(xgT_psum, j + 1)
                nc.gpsimd.tensor_tensor(idxc[:, :], idx[:, bass.ds(j + 1, 1)], izero[:, :], ALU.add).then_inc(xg_idx, 1)
                pool.wait_ge(xg_idx, j + 2)
                nc.gpsimd.tensor_tensor(carry[:, 0:1], riota[0:1, 0:1], riota[0:1, 1:2], ALU.add)
                gather()

            with pool.Fori(0, NE - 1) as e:
                lo = pool.value_load(tiles_cum[0:1, bass.ds(e, 1)], min_val=0, max_val=SLOTS - 1)
                hi = pool.value_load(tiles_cum[0:1, bass.ds(e + 1, 1)], min_val=1, max_val=SLOTS - 1)
                with pool.Fori(lo, hi) as j:
                    next_gather(j)
                lo_units(e + 1)
            lo = pool.value_load(tiles_cum[0:1, NE - 1:NE], min_val=0, max_val=SLOTS - 1)
            total = pool.value_load(tiles_cum[0:1, NE:NE + 1], min_val=1, max_val=SLOTS - 1)
            with pool.Fori(lo, total) as j:
                next_gather(j)

            pool.wait_ge(unit_lo_dve, (NE + 1) * len(DVE_LO))
            pool.wait_ge(unit_lo_pool, (NE + 1) * len(POOL_LO))
            pool.wait_ge(xg_loaded, total * 16 + 16)
            nc.gpsimd.tensor_tensor(carry[:, 2:3], riota[0:1, 0:1], riota[0:1, 1:2], ALU.add)
            spare = pool.value_load(tiles_cum[0:1, NE + 1:NE + 2], min_val=1, max_val=SLOTS - NE)
            pool.wait_ge(y_zeroed, spare * 32)
            pool.wait_ge(y_stored, total * 16 + 16)
            nc.gpsimd.tensor_tensor(carry[:, 1:2], riota[0:1, 0:1], riota[0:1, 1:2], ALU.add)

            def finish_tile(t):
                if t == 0:
                    pool.wait_ge(ln2_loaded, 32)
                pool.wait_ge(fin_rstd, t + 1)
                o = o_sb[:, t % NT, :]
                nc.gpsimd.tensor_tensor(o, o, ln[:, 1, :], ALU.add).then_inc(fin_y, 1)

            for t in range(TT):
                f = t % 2
                if t >= 2:
                    pool.wait_ge(fin_acc, t - 1)
                for c in range(2):
                    nc.gpsimd.indirect_dma_start(raw[:, 3 * f + c, :], None, y_dram,
                                                 bass.IndirectOffsetOnAxis(slot_i[:, c, t:t + 1], 0))\
                        .then_inc(fin_loaded[f], 16)
                pool.dma_start(raw[:, 3 * f + 2, :], x1_dram[t * P:(t + 1) * P, :]).then_inc(fin_loaded[f], 16)
                if t >= 1:
                    finish_tile(t - 1)
            finish_tile(TT - 1)

        @block.scalar
        def _(act):
            def hi_chunk(g):
                slot = g % 2
                kind, _ = CHUNKS[g % NCH]
                act.wait_ge(chunk_loaded[slot], chunk_loads(g))
                if kind == "wo":
                    act.wait_ge(chunk_scaled, (g // NCH) * 8 + CHUNKS[g % NCH][1] + 1)
                if g >= 2:
                    act.wait_ge(c_ready[slot], g // 2)
                nc.scalar.activation(wch[0][:, slot, :, :], wraw[:, slot, :, :], ACT.Copy).then_inc(chunk_hi, 1)

            def hi_units(cum_prev, e, ws):
                for w in ws:
                    slot, turn = w % RAW, w // RAW
                    act.wait_ge(raw_loaded[slot], e * 32 + 16 * turn + 16)
                    act.wait_ge(units_used, cum_prev * UNITS + w + 1)
                    nc.scalar.activation(wu[0][:, w, :], raw[:, slot, :], ACT.Copy).then_inc(unit_hi, 1)

            for ev in EVENTS:
                what, s = ev[0], ev[1]
                if what in ("x", "m", "o"):
                    t, b, u = ev[2], ev[3], ev[4]
                    act.wait_ge(t_ready[u % 2], u // 2 + 1)
                    src = Tb[u % 2][:, :].rearrange("p (k c) -> p k c", k=4)
                    if what == "o" and b == 1:
                        nc.scalar.activation(grid_view(xT[0], t), src[:, 0:2, :].rearrange("p k (r c) -> p k r c", r=ROWS),
                                             ACT.Copy)
                        nc.scalar.activation(xT[0][:, 6:8, t * P:(t + 1) * P], src[:, 2:4, :], ACT.Copy).then_inc(t_hi, 1)
                    else:
                        dst = (memT if what == "m" else xT)[0]
                        nc.scalar.activation(dst[:, 4 * b:4 * b + 4, t * P:(t + 1) * P], src, ACT.Copy).then_inc(t_hi, 1)
                elif what == "C":
                    c, cu = ev[2], ev[3]
                    kind, g = CHUNKS[c]
                    bnk = Cb[cu % 2]
                    if cu == 0:
                        hi_chunk(0)
                        hi_chunk(1)
                    if kind in VALUES:
                        width = MEM if kind == "mv" else S
                        act.wait_ge(c_ready[cu % 2], cu // 2 + 1)
                        done = s * len(V_UNITS) + V_UNITS.index(c)
                        if done:
                            u2 = V_TURNED[done - 1]
                            act.wait_ge(t_ready[u2 % 2], u2 // 2 + 1)
                        nc.scalar.activation(vT[:, 0:width // 256, :],
                                             bnk[:, 0:width].rearrange("p (a b) -> p a b", b=256), ACT.Copy)\
                            .then_inc(c_drained[cu % 2], 1)
                    if kind in split_C:
                        act.wait_ge(c_ready[cu % 2], cu // 2 + 1)
                        dst, width = c_dest(kind, g)
                        src = bnk[:, 0:width]
                        if kind == "qb":
                            dst, src = [by_block(dst[0])], by_row(src)
                        nc.scalar.activation(dst[0], src, ACT.Copy,
                                             scale=SCALE if kind[0] == "q" else 1.0).then_inc(c_hi, 1)
                    gg = s * NCH + c + 2
                    if gg < NSEQ * NCH:
                        hi_chunk(gg)
                elif what == "S":
                    i, a = ev[2], ev[3]
                    kind, tile, h = UNIT_LIST[i]
                    gi, hs = group_of(s, i)
                    if h == 0 and gi >= 2:
                        act.wait_ge(o_drained[gi % 2], gi // 2)
                    pr = probs[:, a % 2, :]
                    if kind == "M":
                        act.wait_ge(maxed, s * 16 + i + 1)
                        if a >= 2:
                            u2 = T_OF_UNIT[a - 2]
                            act.wait_ge(t_ready[u2 % 2], u2 // 2 + 1)
                        nc.scalar.activation(pr[:, 0:MEM], Sb[a % 2][:, 0:MEM], ACT.Exp, bias=negm[:, gi % 2, h:h + 1],
                                             accum_out=sums[:, gi % 2, h:h + 1]).then_inc(exped, 1)
                    else:
                        w = key_range(tile)[1] if kind == "A" else 256
                        act.wait_ge(biased, s * 48 + i - 16 + 1)
                        nc.scalar.activation(pr[:, 0:w], pr[:, 0:w], ACT.Exp, scale=-1.0,
                                             bias=negm[:, gi % 2, h:h + 1],
                                             accum_out=sums[:, gi % 2, h:h + 1]).then_inc(exped, 1)
                        if kind == "A" and h == A_HEADS - 1:
                            act.wait_ge(sink_in, s * NT + tile + 1)
                            nc.scalar.activation(es[:, gi % 2, :], es[:, gi % 2, :], ACT.Exp).then_inc(sink_exp, 1)
                elif what == "T":
                    i, a, u = ev[2], ev[3], ev[4]
                    if UNIT_LIST[i][0] == "M" or i % 4 == 1:
                        copy_probs(act, nc.scalar.copy, s, i, a, u)
                elif what == "r":
                    t, b, u = ev[2], ev[3], ev[4]
                    act.wait_ge(t_ready[u % 2], u // 2 + 1)
                    if t == 0 and b == 0:
                        act.wait_ge(vb_stored, 16 * 8 * (s + 1))
                    if s * NT + t >= 1:
                        act.wait_ge(route_psum, s * NT + t)
                    nc.scalar.activation(x1T[:, 4 * b:4 * b + 4, :], Tb[u % 2][:, :].rearrange("p (k c) -> p k c", k=4),
                                         ACT.Copy).then_inc(t_drained[u % 2], 1)
                elif what == "VAR" and s == NSEQ - 1:
                    for b in range(2):
                        act.wait_ge(c_ready[b], NSEQ * NCH // 2)
                    hi_units(0, 0, range(RAW))
                elif what == "R" and ev[2] == NT - 1:
                    act.wait_ge(route_psum, (s + 1) * NT)
                    nc.scalar.activation(sc[:, s * NT:(s + 1) * NT, :],
                                         Ob[1][:, 0:NT * NE].rearrange("p (t e) -> p t e", t=NT),
                                         ACT.Sigmoid).then_inc(sig_done, 1)

            def xgT_his(j):
                act.wait_ge(xgT_psum, j + 1)
                for b in range(2):
                    ins = nc.scalar.activation(xgT[0][:, 4 * b:4 * b + 4, :],
                                               Tb[b][:, :].rearrange("p (k c) -> p k c", k=4), ACT.Copy)
                ins.then_inc(xgT_hi, 1)

            def tile_gate(n):
                act.wait_ge(units_used, n * UNITS + 4)
                act.wait_ge(h_mid, n * 2)
                nc.scalar.activation(sg, Cb[0][:, :], ACT.Silu).then_inc(silu_done, 1)

            def tile_hidden(n):
                for i in range(2):
                    act.wait_ge(hT_psum, n * 2 + i + 1)
                    dst, src = hT_part(0, i)
                    nc.scalar.activation(dst, src, ACT.Copy).then_inc(hT_hi, 1)
                xgT_his(n)

            def tile_last(n):
                act.wait_ge(units_used, n * UNITS + UNITS)
                act.wait_ge(y_stored, n * 16)
                nc.scalar.activation(y_sb[:, 0:512], Ob[0][:, :], ACT.Copy).then_inc(y_half[0], 1)
                act.wait_ge(y_half[0], n + 1)
                act.wait_ge(y_half[1], n + 1)
                act.dma_start(y_dram.rearrange("(j p) c -> j p c", p=P)[bass.ds(n - 1, 1)].rearrange("a p c -> (a p) c"),
                              y_sb).then_inc(y_stored, 16)

            hi_units(0, 0, range(RAW, UNITS))
            act.wait_ge(routed, 1)
            y_tiles = y_dram.rearrange("(j p) c -> j p c", p=P)
            total = act.value_load(tiles_cum[0:1, NE:NE + 1], min_val=1, max_val=SLOTS - 1)
            with act.Fori(total, SLOTS) as j:
                for half in range(2):
                    act.dma_start(y_tiles[bass.ds(j, 1), :, half * 512:(half + 1) * 512].rearrange("a p c -> (a p) c"),
                                  zeros).then_inc(y_zeroed, 16)
            xgT_his(0)
            with act.Fori(0, NE - 1) as e:
                lo = act.value_load(tiles_cum[0:1, bass.ds(e, 1)], min_val=0, max_val=SLOTS - 1)
                hi = act.value_load(tiles_cum[0:1, bass.ds(e + 1, 1)], min_val=1, max_val=SLOTS - 1)
                with act.If(lo < hi - 1):
                    with act.Fori(lo, hi - 1) as j:
                        tile_gate(j + 1)
                        tile_hidden(j + 1)
                        tile_last(j + 1)
                hi_units(hi, e + 1, range(0, 4))
                tile_gate(hi)
                hi_units(hi, e + 1, range(4, 6))
                tile_hidden(hi)
                hi_units(hi, e + 1, range(6, UNITS))
                tile_last(hi)
            lo = act.value_load(tiles_cum[0:1, NE - 1:NE], min_val=0, max_val=SLOTS - 1)
            hi = act.value_load(tiles_cum[0:1, NE:NE + 1], min_val=1, max_val=SLOTS - 1)
            with act.Fori(lo, hi) as j:
                tile_gate(j + 1)
                tile_hidden(j + 1)
                tile_last(j + 1)

            for t in range(TT + 1):
                if t < TT:
                    f = t % 2
                    act.wait_ge(fin_loaded[f], 48 * (t // 2 + 1))
                    nc.scalar.activation(raw[:, 3 * f + 2, :], raw[:, 3 * f + 2, :], ACT.Copy, scale=ALPHA)\
                        .then_inc(fin_scaled, 1)
                if t >= 1:
                    act.wait_ge(fin_norm, t)
                    o = o_sb[:, (t - 1) % NT, :]
                    nc.scalar.activation(o, o, ACT.Copy, scale=rstd[:, t - 1:t]).then_inc(fin_rstd, 1)

        @block.vector
        def _(dve):
            n = [0]

            def link(i):
                n[0] += 1
                i.then_inc(dch, 1)
                dve.wait_ge(dch, n[0])

            def rsqrt(y, w):
                v, t = nv[:, 0:w], nt_[:, 0:w]
                link(nc.vector.tensor_scalar(t.bitcast(I32), v.bitcast(I32), 1, None, ALU.logical_shift_right))
                link(nc.vector.tensor_scalar(y.bitcast(I32), t.bitcast(I32), -1.0, float(0x5F3759DF), ALU.mult, ALU.add))
                for _ in range(4):
                    link(nc.vector.tensor_tensor(t, y, y, ALU.mult))
                    link(nc.vector.tensor_tensor(t, t, v, ALU.mult))
                    link(nc.vector.tensor_scalar(t, t, -0.5, 1.5, ALU.mult, ALU.add))
                    link(nc.vector.tensor_tensor(y, y, t, ALU.mult))

            nc.vector.memset(o_sb[:, 0, 0:64], 0.0).then_inc(setup_dve, 1)
            for i, (sm, v) in enumerate(((units_used, UNITS), (unit_lo_dve, len(DVE_LO)), (unit_lo_pool, len(POOL_LO)),
                                         (h_mid, 2), (hT_psum, 2), (hT_hi, 2), (y_half[0], 1), (y_half[1], 1), (y_stored, 16))):
                nc.vector.memset(seed[:, i:i + 1], 0.0).then_inc(sm, v)
            dve.wait_ge(setup_pool, 9)
            dist = o_sb[:, 0, 512:896]
            link(nc.vector.scalar_tensor_tensor(dist, dist, -1.0, dist, ALU.mult, ALU.max))
            mask = probs[:, 0, :]
            link(nc.vector.tensor_scalar(mask, dist, float(WINDOW), MASKED, ALU.is_gt, ALU.mult))
            for h in range(A_HEADS):
                link(nc.vector.scalar_tensor_tensor(biasA[:, h, :], dist, -(2.0 ** -(h + 1)), mask, ALU.mult, ALU.add))
            link(nc.vector.tensor_scalar(scol[:, 1:2], scol[:, 0:1], 15, None, ALU.bitwise_and))
            link(nc.vector.tensor_copy(nv[:, 0:1], scol[:, 1:2]))
            d = o_sb[:, 0, 96:128]
            link(nc.vector.tensor_scalar(d, o_sb[:, 0, 64:96], nv[:, 0:1], None, ALU.subtract))
            gm = o_sb[:, 0, 128:224].rearrange("p (k c) -> p k c", k=3)
            link(nc.vector.tensor_scalar(gm[:, 0, 0:16], d[:, 0:16], -8.0, MASKED, ALU.is_lt, ALU.mult))
            link(nc.vector.tensor_scalar(gm[:, 0, 16:32], d[:, 16:32], 7.0, MASKED, ALU.is_gt, ALU.mult))
            link(nc.vector.tensor_scalar(gm[:, 1, :], d, 0.0, MASKED, ALU.is_lt, ALU.mult))
            link(nc.vector.tensor_scalar(o_sb[:, 0, 224:256], d, 15.0, MASKED, ALU.is_gt, ALU.mult))
            link(nc.vector.tensor_tensor(gm[:, 1, :], gm[:, 1, :], o_sb[:, 0, 224:256], ALU.add))
            link(nc.vector.tensor_scalar(gm[:, 2, 0:16], d[:, 0:16], 8.0, MASKED, ALU.is_lt, ALU.mult))
            link(nc.vector.tensor_scalar(gm[:, 2, 16:32], d[:, 16:32], 23.0, MASKED, ALU.is_gt, ALU.mult))
            dve.wait_ge(small_loaded, 64)
            link(nc.vector.tensor_scalar(nsink[:, :], sinkb[:, :], -1.0, None, ALU.mult))

            def bias_b_tables():
                for i in range(12):
                    kind = i % 3
                    bnk = Sb[(i // 2) % 2]
                    if i % 2 == 0:
                        dve.wait_ge(setup_pe, i // 2 + 1)
                    link(nc.vector.tensor_tensor(biasB[:, i, :].rearrange("p (r c) -> p r c", r=ROWS),
                                                 bnk[:, (i % 2) * 256:(i % 2 + 1) * 256].rearrange("p (r c) -> p r c", r=ROWS),
                                                 gm[:, kind, :].unsqueeze(1).to_broadcast([P, ROWS, BW]), ALU.add))
                    if i % 2 == 1:
                        nc.vector.memset(seed[:, 7:8], 0.0).then_inc(setup_dve, 1)
                        dve.wait_ge(setup_dve, 2 + i // 2)

            for ev in EVENTS:
                what, s = ev[0], ev[1]
                if what in ("x", "m", "o"):
                    t, b, u = ev[2], ev[3], ev[4]
                    if what == "o" and t == 0 and b == 0:
                        normalise_groups(s, link, rsqrt, dve)
                    dve.wait_ge(t_hi, T_HI[u])
                    src = Tb[u % 2][:, :].rearrange("p (k c) -> p k c", k=4)
                    if what == "o" and b == 1:
                        nc.vector.tensor_tensor(grid_view(xT[1], t), src[:, 0:2, :].rearrange("p k (r c) -> p k r c", r=ROWS),
                                                grid_view(xT[0], t).bitcast(F32), ALU.subtract)
                        nc.vector.tensor_tensor(xT[1][:, 6:8, t * P:(t + 1) * P], src[:, 2:4, :],
                                                xT[0][:, 6:8, t * P:(t + 1) * P].bitcast(F32), ALU.subtract)\
                            .then_inc(t_drained[u % 2], 1)
                    else:
                        tt = memT if what == "m" else xT
                        nc.vector.tensor_tensor(tt[1][:, 4 * b:4 * b + 4, t * P:(t + 1) * P], src,
                                                tt[0][:, 4 * b:4 * b + 4, t * P:(t + 1) * P].bitcast(F32),
                                                ALU.subtract).then_inc(t_drained[u % 2], 1)
                elif what == "BB":
                    bias_b_tables()
                elif what == "C":
                    c, cu = ev[2], ev[3]
                    kind, g = CHUNKS[c]
                    bnk = Cb[cu % 2]
                    if kind in split_C:
                        dst, width = c_dest(kind, g)
                        dve.wait_ge(c_hi, C_HI[cu])
                        if kind == "qb":
                            for blk in range(4):
                                ins = nc.vector.scalar_tensor_tensor(
                                    by_block(dst[1])[:, :, blk, :], by_row(bnk[:, :])[:, :, blk, :], SCALE,
                                    by_block(dst[0].bitcast(F32))[:, :, blk, :], ALU.mult, ALU.subtract)
                        else:
                            ins = nc.vector.scalar_tensor_tensor(dst[1], bnk[:, 0:width], SCALE if kind[0] == "q" else 1.0,
                                                                 dst[0].bitcast(F32), ALU.mult, ALU.subtract)
                        ins.then_inc(c_drained[cu % 2], 1)
                    elif kind == "wo" and g % 4 == 3:
                        half = g // 4
                        for t in range(NT):
                            if t < NT - 1:
                                dve.wait_ge(wo_ready, (s * 2 + half) * (NT - 1) + t + 1)
                            else:
                                dve.wait_ge(c_ready[cu % 2], cu // 2 + 1)
                            if s > 0:
                                dve.wait_ge(x_again[t], 16)
                            y = x_nat[:, t, half * 512:(half + 1) * 512]
                            nc.vector.scalar_tensor_tensor(y, y, ALPHA, wo_bank(half, t)[:, :], ALU.mult,
                                                           ALU.add).then_inc(wo_drained, 1)
                            dve.wait_ge(wo_drained, (s * 2 + half) * NT + t + 1)
                            link(nc.vector.bn_stats(stats[:, t, half, :], y))
                elif what == "v":
                    c, u = ev[2], ev[3]
                    kind, g = CHUNKS[c]
                    dve.wait_ge(t_ready[u % 2], u // 2 + 1)
                    if kind == "vb" and g == 0 and s > 0:
                        dve.wait_ge(vb_stored, 16 * 8)
                        dve.wait_ge(route_psum, NT)
                    width, dst = {"mv": (MEM, mv[:, :, g * P:(g + 1) * P]), "va": (S, va[:, :, :]),
                                  "vb": (S, vstg[:, :, g * P:(g + 1) * P])}[kind]
                    nc.vector.tensor_copy(dst, Tb[u % 2][:, 0:width].rearrange("p (t c) -> p t c", c=P))\
                        .then_inc(t_drained[u % 2], 1)
                elif what == "S":
                    i, a = ev[2], ev[3]
                    kind, tile, h = UNIT_LIST[i]
                    gi, _ = group_of(s, i)
                    dve.wait_ge(s_ready[a % 2], a // 2 + 1)
                    if kind == "M":
                        nc.vector.tensor_reduce(negm[:, gi % 2, h:h + 1], Sb[a % 2][:, 0:MEM], AX.X, ALU.max,
                                                negate=True).then_inc(maxed, 1)
                    else:
                        u2 = T_OF_UNIT[a - 2]
                        dve.wait_ge(t_ready[u2 % 2], u2 // 2 + 1)
                        if kind == "A":
                            head = (h // 2) + 4 * (h % 2)
                            k0, w = key_range(tile)
                            off = k0 - (tile - 1) * P
                            bias, start = biasA[:, head, off:off + w], nsink[:, head:head + 1]
                        else:
                            w = 256
                            bias, start = biasB[:, h * 3 + (0, 1, 1, 2)[tile], :], 3.0e38
                        nc.vector.tensor_tensor_reduce(out=probs[:, a % 2, 0:w], in0=Sb[a % 2][:, 0:w], in1=bias,
                                                       scale=-1.0, scalar=start, op0=ALU.add, op1=ALU.min,
                                                       accum_out=negm[:, gi % 2, h:h + 1]).then_inc(biased, 1)
                        if kind == "A" and h == A_HEADS - 1:
                            dve.wait_ge(biased, s * 48 + i - 16 + 1)
                            nc.vector.tensor_tensor(
                                es[:, gi % 2, :].rearrange("p (a b) -> p b a", b=2),
                                negm[:, gi % 2, :].rearrange("p (a b) -> p b a", b=2),
                                sinkb[:, :].rearrange("p (b a) -> p b a", b=2), ALU.add).then_inc(sink_in, 1)
                elif what == "T":
                    i, a, u = ev[2], ev[3], ev[4]
                    if not (UNIT_LIST[i][0] == "M" or i % 4 == 1):
                        copy_probs(dve, nc.vector.tensor_copy, s, i, a, u)
                elif what == "PV":
                    i, a = ev[2], ev[3]
                    kind, tile, h = UNIT_LIST[i]
                    if h == HEADS[kind] - 1:
                        gi, _ = group_of(s, i)
                        nh = HEADS[kind]
                        den = sums[:, gi % 2, 0:nh]
                        dve.wait_ge(exped, a + 1)
                        if kind == "A":
                            dve.wait_ge(sink_exp, s * NT + tile + 1)
                            link(nc.vector.tensor_tensor(es[:, gi % 2, :], es[:, gi % 2, :], den, ALU.add))
                            den = es[:, gi % 2, :]
                        link(nc.vector.reciprocal(rden[:, gi % 2, 0:nh], den))
                        dve.wait_ge(pv_done, a + 1)
                        c0 = OCOL[kind]
                        dst = o_sb[:, tile, c0:c0 + nh * HD]
                        psv = Ob[gi % 2][:, 0:nh * HD]
                        rb = rden[:, gi % 2, 0:nh]
                        if kind == "A":
                            link(nc.vector.tensor_tensor(
                                dst.rearrange("p (b a d) -> p b a d", b=2, a=4),
                                psv.rearrange("p (a b d) -> p b a d", b=2, a=4),
                                rb.rearrange("p (a b) -> p b a", b=2).unsqueeze(3).to_broadcast([P, 2, 4, HD]),
                                ALU.mult))
                        else:
                            link(nc.vector.tensor_tensor(dst.rearrange("p (a d) -> p a d", a=nh),
                                                         psv.rearrange("p (a d) -> p a d", a=nh),
                                                         rb.unsqueeze(2).to_broadcast([P, nh, HD]), ALU.mult))
                        gl = gi % len(GROUPS)
                        nc.vector.bn_stats(stats[:, gl % TT, 0, :], dst).then_inc(o_drained[gi % 2], 1)
                        dve.wait_ge(o_drained[gi % 2], gi // 2 + 1)
                        link(nc.vector.bn_aggr(mvv[:, gl, :], stats[:, gl % TT, 0, :]))
                elif what == "VAR":
                    for t in range(NT):
                        link(nc.vector.bn_aggr(mvv[:, t, :], stats[:, t, :, :].rearrange("p a b -> p (a b)")))
                    link(nc.vector.tensor_scalar(nv[:, 0:NT], mvv[:, 0:NT, 1], EPS, None, ALU.add))
                    rsqrt(rstd[:, s * NT:(s + 1) * NT], NT)
                elif what == "LN":
                    t = ev[2]
                    if s == 0 and t == 0:
                        dve.wait_ge(ln_loaded, 32)
                    link(nc.vector.tensor_scalar(x_nat[:, t, :], x_nat[:, t, :], mvv[:, t, 0:1],
                                                 rstd[:, s * NT + t:s * NT + t + 1], ALU.subtract, ALU.mult))
                    nc.vector.tensor_tensor(x_nat[:, t, :], x_nat[:, t, :], ln[:, 0, :], ALU.mult).then_inc(normed, 1)

            routing(dve, link)

            def lo_units(e, ws):
                for w in ws:
                    if w in POOL_LO:
                        continue
                    dve.wait_ge(unit_hi, e * UNITS + w + 1)
                    nc.vector.tensor_tensor(wu[1][:, w, :], raw[:, w % RAW, :], wu[0][:, w, :].bitcast(F32),
                                            ALU.subtract).then_inc(unit_lo_dve, 1)

            def xgT_los(j):
                dve.wait_ge(xgT_hi, j + 1)
                for b in range(2):
                    ins = nc.vector.tensor_tensor(xgT[1][:, 4 * b:4 * b + 4, :],
                                                  Tb[b][:, :].rearrange("p (k c) -> p k c", k=4),
                                                  xgT[0][:, 4 * b:4 * b + 4, :].bitcast(F32), ALU.subtract)
                ins.then_inc(xgT_lo, 1)

            def tile_first(n):
                dve.wait_ge(silu_done, n)
                dve.wait_ge(units_used, n * UNITS + KD)
                for i in range(2):
                    nc.vector.tensor_tensor(h_sb[:, i * 256:(i + 1) * 256], sg[:, i * 256:(i + 1) * 256],
                                            Cb[1][:, i * 256:(i + 1) * 256], ALU.mult).then_inc(h_mid, 1)
                for i in range(2):
                    dve.wait_ge(hT_hi, n * 2 + i + 1)
                    dst, src = hT_part(1, i)
                    nc.vector.tensor_tensor(dst, src, hT_part(0, i)[0].bitcast(F32), ALU.subtract).then_inc(hT_lo, 1)
                xgT_los(n)

            def tile_last(n):
                dve.wait_ge(units_used, n * UNITS + UNITS)
                dve.wait_ge(y_stored, n * 16)
                nc.vector.tensor_copy(y_sb[:, 512:1024], Ob[1][:, :]).then_inc(y_half[1], 1)

            xgT_los(0)
            with dve.Fori(0, NE - 1) as e:
                lo = dve.value_load(tiles_cum[0:1, bass.ds(e, 1)], min_val=0, max_val=SLOTS - 1)
                hi = dve.value_load(tiles_cum[0:1, bass.ds(e + 1, 1)], min_val=1, max_val=SLOTS - 1)
                with dve.If(lo < hi - 1):
                    with dve.Fori(lo, hi - 1) as j:
                        tile_first(j + 1)
                        tile_last(j + 1)
                lo_units(e + 1, range(0, 6))
                tile_first(hi)
                lo_units(e + 1, range(6, UNITS))
                tile_last(hi)
            lo = dve.value_load(tiles_cum[0:1, NE - 1:NE], min_val=0, max_val=SLOTS - 1)
            hi = dve.value_load(tiles_cum[0:1, NE:NE + 1], min_val=1, max_val=SLOTS - 1)
            with dve.Fori(lo, hi) as j:
                tile_first(j + 1)
                tile_last(j + 1)

            def last_norm(t):
                link(nc.vector.bn_aggr(mvv[:, t, :], stats[:, t, :, :].rearrange("p a b -> p (a b)")))
                link(nc.vector.tensor_scalar(nv[:, 0:1], mvv[:, t, 1:2], EPS, None, ALU.add))
                rsqrt(rstd[:, t:t + 1], 1)
                o = o_sb[:, t % NT, :]
                nc.vector.scalar_tensor_tensor(o, o, mvv[:, t, 0:1], ln[:, 0, :], ALU.subtract, ALU.mult)\
                    .then_inc(fin_norm, 1)

            dve.wait_ge(ln2_loaded, 32)
            for t in range(TT):
                f = t % 2
                y1, y2, x1 = (raw[:, 3 * f + k, :] for k in range(3))
                o = o_sb[:, t % NT, :]
                dve.wait_ge(fin_scaled, t + 1)
                link(nc.vector.scalar_tensor_tensor(y1, y1, wts[:, 0, t:t + 1], x1, ALU.mult, ALU.add))
                if t >= NT:
                    dve.wait_ge(out_stored[t % NT], 16)
                nc.vector.scalar_tensor_tensor(o, y2, wts[:, 1, t:t + 1], y1, ALU.mult, ALU.add).then_inc(fin_acc, 1)
                dve.wait_ge(fin_acc, t + 1)
                for half in range(2):
                    link(nc.vector.bn_stats(stats[:, t, half, :], o[:, half * 512:(half + 1) * 512]))
                last_norm(t)

        @block.tensor
        def _(pe):
            pe.wait_ge(setup_pool, 2)

            def three(out_ap, st, mvg, first, last, last_sem=None):
                ins = nc.tensor.matmul(out_ap, st[0], mvg[0], start=first, stop=False)
                ins = nc.tensor.matmul(out_ap, st[0], mvg[1], start=False, stop=False)
                ins = nc.tensor.matmul(out_ap, st[1], mvg[0], start=False, stop=last)
                return ins

            def bias_b_reverse():
                pe.wait_ge(biasb_loaded, 16 * ROWS)
                for i in range(6):
                    if i >= 2:
                        pe.wait_ge(setup_dve, i)
                    nc.tensor.matmul(Sb[i % 2][:, :], anti[:, :], o_sb[:, 1 + i // 2, (i % 2) * 512:(i % 2 + 1) * 512],
                                     start=True, stop=True).then_inc(setup_pe, 1)

            for ev in EVENTS:
                what, s = ev[0], ev[1]
                if what in ("x", "m", "o", "r"):
                    t, b, u = ev[2], ev[3], ev[4]
                    if u >= 2:
                        pe.wait_ge(t_drained[u % 2], u // 2)
                    if what == "x":
                        pe.wait_ge(x_loaded[s][t], 16)
                        src = (o_sb if s else x_nat)[:, t, :]
                    elif what == "m":
                        pe.wait_ge(mem_loaded[s], 16)
                        src = mem_nat[:, t, :]
                    elif what == "o":
                        pe.wait_ge(mixed_done, s * NT + t + 1)
                        src = o_sb[:, t, :]
                    else:
                        pe.wait_ge(x1_ready, s * NT + t + 1)
                        src = x_nat[:, t, :]
                    for k in range(4):
                        ins = nc.tensor.transpose(Tb[u % 2][:, k * P:(k + 1) * P],
                                                  src[:, (4 * b + k) * P:(4 * b + k + 1) * P], ident[:, :])
                    ins.then_inc(t_ready[u % 2], 1)
                elif what == "BB":
                    bias_b_reverse()
                elif what == "v":
                    c, u = ev[2], ev[3]
                    pe.wait_ge(t_drained[u % 2], u // 2)
                    pe.wait_ge(c_drained[c % 2], C_OUT[s * NCH + c])
                    for t in range((MEM if CHUNKS[c][0] == "mv" else S) // P):
                        ins = nc.tensor.transpose(Tb[u % 2][:, t * P:(t + 1) * P],
                                                  vT[:, t // 2, (t % 2) * P:(t % 2 + 1) * P], ident[:, :])
                    ins.then_inc(t_ready[u % 2], 1)
                elif what == "C":
                    c, cu = ev[2], ev[3]
                    kind, g = CHUNKS[c]
                    gg = s * NCH + c
                    sl = gg % 2
                    pe.wait_ge(chunk_lo, gg + 1)
                    if cu >= 2 and kind != "wo":
                        pe.wait_ge(c_drained[cu % 2], C_OUT[cu - 2])
                    if c == 0:
                        t_waits(pe, LAST_M[s])
                        if s > 0:
                            pe.wait_ge(wo_drained, s * 2 * NT)
                    if kind == "qm" and g == 0:
                        t_waits(pe, LAST_IN[s])
                    if kind == "wo" and g == 0:
                        t_waits(pe, LAST_O[s])
                    W = [wch[0][:, sl], wch[1][:, sl]]
                    bnk = Cb[cu % 2]
                    if kind == "wo":
                        half, pair = g // 4, g % 4
                        Wp = [by_pair(w_) for w_ in W]
                        for t in range(NT):
                            if pair == 0 and half == 0 and t == 0:
                                c_waits(pe, s * NCH + NCH - 9)
                            if pair == 0 and half == 1 and t >= 2:
                                pe.wait_ge(wo_drained, s * 2 * NT + t - 1)
                            for k in range(2):
                                kk = 2 * pair + k
                                ins = three(wo_bank(half, t)[:, :],
                                            [xT[0][:, kk, t * P:(t + 1) * P], xT[1][:, kk, t * P:(t + 1) * P]],
                                            [Wp[0][:, k, :], Wp[1][:, k, :]], kk == 0, kk == KD - 1)
                            if pair == 3 and t < NT - 1:
                                ins.then_inc(wo_ready, 1)
                    else:
                        src = memT if kind in ("mk", "mv") else xT
                        width = MEM if kind in ("mk", "mv") else S
                        for k in range(KD):
                            ins = three(bnk[:, 0:width], [W[0][:, k, :], W[1][:, k, :]],
                                        [src[0][:, k, :], src[1][:, k, :]], k == 0, k == KD - 1)
                    ins.then_inc(c_ready[cu % 2], 1)
                elif what == "S":
                    i, a = ev[2], ev[3]
                    kind, tile, h = UNIT_LIST[i]
                    if a == 0:
                        pe.wait_ge(setup_dve, 7)
                    if a >= 2:
                        s2, i2 = (a - 2) // NU, (a - 2) % NU
                        if UNIT_LIST[i2][0] == "M":
                            pe.wait_ge(exped, a - 1)
                        else:
                            pe.wait_ge(biased, s2 * 48 + i2 - 16 + 1)
                    if h == 0 and tile == 0:
                        c_waits(pe, s * NCH + {"M": 5, "A": 11, "B": 15}[kind])
                    bnk = Sb[a % 2]
                    if kind == "M":
                        lo_p = (h % 2) * HD
                        q = [t_[lo_p:lo_p + HD, h // 2, tile * P:(tile + 1) * P] for t_ in qmT]
                        kk = [t_[lo_p:lo_p + HD, h // 2, :] for t_ in mkT]
                        o = bnk[:, 0:MEM]
                    elif kind == "A":
                        lo_p = (h % 2) * HD
                        k0, w = key_range(tile)
                        q = [t_[lo_p:lo_p + HD, h // 2, tile * P:(tile + 1) * P] for t_ in qaT]
                        kk = [t_[lo_p:lo_p + HD, 0, k0:k0 + w] for t_ in kaT]
                        o = bnk[:, 0:w]
                    else:
                        lo_p = (h % 2) * HD
                        q = [t_[lo_p:lo_p + HD, h // 2, tile * P:(tile + 1) * P] for t_ in qbT]
                        kk = [t_[lo_p:lo_p + HD, h // 2, :].rearrange("p (r c) -> p r c", r=ROWS)
                              [:, :, WIN0[tile]:WIN0[tile] + BW] for t_ in kbT]
                        o = bnk[:, 0:256]
                    three(o, q, kk, True, True).then_inc(s_ready[a % 2], 1)
                elif what == "T":
                    i, a, u = ev[2], ev[3], ev[4]
                    kind, tile, h = UNIT_LIST[i]
                    w = key_range(tile)[1] if kind == "A" else 256
                    pe.wait_ge(exped, a + 1)
                    if u >= 2:
                        pe.wait_ge(t_drained[u % 2], u // 2)
                    for k in range(w // P):
                        ins = nc.tensor.transpose(Tb[u % 2][:, k * P:(k + 1) * P], probs[:, a % 2, k * P:(k + 1) * P],
                                                  ident[:, :])
                    ins.then_inc(t_ready[u % 2], 1)
                elif what == "PV":
                    i, a = ev[2], ev[3]
                    kind, tile, h = UNIT_LIST[i]
                    gi, _ = group_of(s, i)
                    u = T_OF_UNIT[a]
                    pe.wait_ge(t_drained[u % 2], u // 2 + 1)
                    if h == 0 and gi >= 2:
                        pe.wait_ge(o_drained[gi % 2], gi // 2)
                    if s == 1 and i == 0:
                        pe.wait_ge(sig_done, 1)
                    if kind == "M":
                        vs = [mv[:, k, h * HD:(h + 1) * HD] for k in range(2)]
                    elif kind == "A":
                        k0, w = key_range(tile)
                        vs = [va[:, k0 // P + k, (h % 2) * HD:(h % 2 + 1) * HD] for k in range(w // P)]
                    else:
                        if h == 0 and tile == 0:
                            pe.wait_ge(vbw_loaded, 16 * (s + 1))
                        vs = [vbw[:, 2 * tile + k, h * HD:(h + 1) * HD] for k in range(2)]
                    for k, v in enumerate(vs):
                        ins = nc.tensor.matmul(Ob[gi % 2][:, h * HD:(h + 1) * HD], probsT[:, a % 2, k * P:(k + 1) * P], v,
                                               start=(k == 0), stop=(k == len(vs) - 1))
                    ins.then_inc(pv_done, 1)
                elif what == "R":
                    t = ev[2]
                    for u in R_UNITS[(s, t)]:
                        pe.wait_ge(t_drained[u % 2], u // 2 + 1)
                    if t == 0:
                        pe.wait_ge(small_loaded, 64)
                        pe.wait_ge(o_drained[1], (s + 1) * len(GROUPS) // 2)
                    for k in range(KD):
                        ins = nc.tensor.matmul(Ob[1][:, t * NE:(t + 1) * NE], x1T[:, k, :], wr[:, k, :],
                                               start=(k == 0), stop=(k == KD - 1))
                    ins.then_inc(route_psum, 1)

            pe.wait_ge(mask_ready, 1)
            m = mask_b[:, :].rearrange("p (t e) -> p t e", t=TT)
            for i in range(TT):
                for k in range(i):
                    nc.tensor.matmul(Ob[0][:, i * NE:(i + 1) * NE], ones_b[:, :], m[:, k, :], start=(k == 0), stop=False)
                nc.tensor.matmul(Ob[0][:, i * NE:(i + 1) * NE], tri_b[:, :], m[:, i, :], start=(i == 0), stop=True)
            for k in range(TT):
                ins = nc.tensor.matmul(Ob[0][:, TT * NE:TT * NE + NE], ones_b[:, :], m[:, k, :], start=(k == 0),
                                       stop=(k == TT - 1))
            ins.then_inc(rank_done, 1)
            pe.wait_ge(onehot_ready, 1)
            for i in range(2 * TT):
                ins = nc.tensor.matmul(Ob[1][:, 0:SLOTS], vbw_flat[:, i * P:(i + 1) * P],
                                       scratch[:, 1664 + i * SLOTS:1664 + (i + 1) * SLOTS], start=(i == 0),
                                       stop=(i == 2 * TT - 1))
            ins.then_inc(idx_psum, 1)

            def transpose_rows(j):
                pe.wait_ge(xg_loaded, j * 16 + 16)
                for k in range(KD):
                    ins = nc.tensor.transpose(Tb[k // 4][:, (k % 4) * P:(k % 4 + 1) * P], xg[:, k * P:(k + 1) * P], ident[:, :])
                ins.then_inc(xgT_psum, 1)

            def unit_wait(e, w):
                lo_sem, owned = (unit_lo_pool, POOL_LO) if w in POOL_LO else (unit_lo_dve, DVE_LO)
                pe.wait_ge(lo_sem, e * len(owned) + len(owned) + owned.index(w) + 1)

            pe.wait_ge(routed, 1)
            transpose_rows(0)
            with pe.Fori(0, NE) as e:
                lo = pe.value_load(tiles_cum[0:1, bass.ds(e, 1)], min_val=0, max_val=SLOTS - 1)
                hi = pe.value_load(tiles_cum[0:1, bass.ds(e + 1, 1)], min_val=1, max_val=SLOTS - 1)
                with pe.Fori(lo, hi) as j:
                    pe.wait_ge(xgT_lo, j + 1)
                    for w in range(KD):
                        unit_wait(e, w)
                        for k in range(2 * (w % 4), 2 * (w % 4) + 2):
                            ins = three(Cb[w // 4][:, :], [xgT[0][:, k, :], xgT[1][:, k, :]],
                                        [wu[b_][:, w, (k % 2) * 512:(k % 2 + 1) * 512] for b_ in range(2)],
                                        k == 0, k == KD - 1)
                        ins.then_inc(units_used, 1)
                    transpose_rows(j + 1)
                    for i in range(2):
                        pe.wait_ge(h_mid, j * 2 + 2 + i + 1)
                        for f in range(2):
                            ins = nc.tensor.transpose(Sb[i][:, f * P:(f + 1) * P],
                                                      h_sb[:, (2 * i + f) * P:(2 * i + f + 1) * P], ident[:, :])
                        ins.then_inc(hT_psum, 1)
                    pe.wait_ge(y_half[0], j + 1)
                    pe.wait_ge(y_half[1], j + 1)
                    for f in range(KF):
                        unit_wait(e, KD + f)
                        pe.wait_ge(hT_lo, j * 2 + f // 2 + 1)
                        st = [hT[0][:, f, :], hT[1][:, f, :]]
                        for a_, b_ in ((0, 0), (0, 1), (1, 0)):
                            for half in range(2):
                                ins = nc.tensor.matmul(Ob[half][:, :], st[a_], wu[b_][:, KD + f, half * 512:(half + 1) * 512],
                                                       start=(f == 0 and a_ + b_ == 0), stop=(f == KF - 1 and a_ == 1))
                        ins.then_inc(units_used, 1)


_INS = ["x", "mem", "w_in", "w_mem_kv", "sink", "rpb", "grp_g", "w_out", "ln1_g", "ln1_b", "w_router", "router_bias",
        "w_gate", "w_up", "w_down", "ln2_g", "ln2_b"]


def kernel(x_prompt, x_sample, mem_prompt, mem_sample, w_in, w_mem_kv, sink_logits, rpb, grp_norm_g, w_out,
           ln1_g, ln1_b, w_router, router_bias, w_gate, w_up, w_down, ln2_g, ln2_b):
    import concourse.bacc as bacc
    import numpy as np
    from concourse.bass_utils import run_bass_kernel_spmd

    nc = bacc.Bacc("TRN2", target_bir_lowering=False, num_devices=1)
    given = {
        "x0": x_prompt, "x1": x_sample, "mem0": mem_prompt, "mem1": mem_sample, "w_in": w_in[0],
        "w_mem_kv": w_mem_kv[0], "sink": sink_logits[0], "rpb": rpb[0], "grp_g": np.asarray(grp_norm_g[0]).reshape(KD, P).T, "w_out": w_out[0],
        "ln1_g": ln1_g[0], "ln1_b": ln1_b[0], "w_router": w_router, "router_bias": router_bias,
        "w_gate": w_gate[0], "w_up": w_up[0], "w_down": w_down[0], "ln2_g": ln2_g[0], "ln2_b": ln2_b[0]}
    arrays, aps = {}, {}
    for name, a in given.items():
        a = np.ascontiguousarray(a)
        arrays[f"in_{name}"] = a
        aps[name] = nc.dram_tensor(f"in_{name}", a.shape, mybir.dt.from_np(a.dtype), kind="ExternalInput").ap()
    outs = [nc.dram_tensor(f"out_{s}", (1, S, D), F32, kind="ExternalOutput").ap() for s in range(NSEQ)]
    aps["x"] = [aps.pop("x0")[0], aps.pop("x1")[0]]
    aps["mem"] = [aps.pop("mem0")[0], aps.pop("mem1")[0]]
    build_kernel(nc, *[aps[n] for n in _INS], outs)
    r = run_bass_kernel_spmd(nc, [arrays], core_ids=[0]).results[0]
    return r["out_0"], r["out_1"]
```

```python
from contextlib import ExitStack

import concourse.bass as bass
from concourse import mybir

F32 = mybir.dt.float32
F32R = mybir.dt.float32r
BF16 = mybir.dt.bfloat16
I32 = mybir.dt.int32
ALU = mybir.AluOpType
ACT = mybir.ActivationFunctionType
AX = mybir.AxisListType

P = 128
D = 1024
KD = D // P
S = 512
NSEQ = 2
NT = S // P
TT = NSEQ * NT
HD = 64
A_HEADS, B_HEADS, M_HEADS = 8, 4, 4
WINDOW = 128
GRID_W, ROWS, NA_ROWS, NA_COLS = 64, 8, 8, 16
BW = 32
WIN0 = (0, 8, 24, 32)
MEM = 256
NE, NG, EG = 16, 4, 4
FE = 512
KF = FE // P
EPS = 1e-5
ALPHA = 2.0 ** 0.25
SCALE = HD ** -0.5
MASKED = -1.0e30
SLOTS = 32
A_Q, A_KV, B_W, M_W = 512, 128, 256, 256
IN_W = A_Q + 2 * A_KV + 3 * B_W + M_W
QA0, KA0, VA0 = 0, A_Q, A_Q + A_KV
QB0 = VA0 + A_KV
KB0, VB0 = QB0 + B_W, QB0 + 2 * B_W
QM0 = QB0 + 3 * B_W
UNITS = KD + KF
POOL_LO = (1, 4, 7, 10)
DVE_LO = tuple(w for w in range(UNITS) if w not in POOL_LO)


def key_range(n):
    k0 = max(0, (n - 1) * P)
    return k0, min(S, (n + 2) * P) - k0


def chunk_order():
    c = [("mk", 0), ("mk", 1), ("mv", 0), ("mv", 1), ("qm", 0), ("qm", 1)]
    c += [("qa", g) for g in range(4)] + [("ka", 0), ("va", 0)]
    c += [("qb", 0), ("qb", 1), ("kb", 0), ("kb", 1), ("vb", 0), ("vb", 1)]
    return c + [("wo", g) for g in range(8)]


VALUES = ("mv", "va", "vb")


CHUNKS = chunk_order()
NCH = len(CHUNKS)
UNIT_LIST = ([("M", n, h) for n in range(NT) for h in range(M_HEADS)]
             + [("A", n, h) for n in range(NT) for h in range(A_HEADS)]
             + [("B", n, h) for n in range(NT) for h in range(B_HEADS)])
NU = len(UNIT_LIST)
GROUPS = [(k, n) for k in "MAB" for n in range(NT)]
HEADS = {"M": M_HEADS, "A": A_HEADS, "B": B_HEADS}
OCOL = {"A": 0, "B": A_Q, "M": A_Q + B_W}


def schedule():
    ev, tu, late = [], [0], []

    def t_unit(*e):
        ev.append((*e, tu[0]))
        tu[0] += 1

    def inputs(s, kind, tiles):
        for t in tiles:
            for b in range(2):
                t_unit(kind, s, t, b)

    def router(s):
        for t in range(NT + 1):
            if t < NT:
                for b in range(2):
                    t_unit("r", s, t, b)
            if t > 0:
                ev.append(("R", s, t - 1))

    def chunk(s, c):
        ev.append(("C", s, c, s * NCH + c))
        if late:
            t_unit("v", *late.pop())
        if CHUNKS[c][0] in VALUES:
            late.append((s, c))

    inputs(0, "m", range(MEM // P))
    for s in range(NSEQ):
        for c in range(6):
            chunk(s, c)
            if s == 0 and c == 5:
                ev.append(("BB", 0))
            if c < NT:
                if s == 0:
                    inputs(s, "x", (c,))
                else:
                    ev.append(("LN", s - 1, c))
        if s > 0:
            router(s - 1)
        nxt = 6
        for i in range(NU + 2):
            if i < NU:
                ev.append(("S", s, i, s * NU + i))
            if 1 <= i <= NU:
                t_unit("T", s, i - 1, s * NU + i - 1)
            if i >= 2:
                ev.append(("PV", s, i - 2, s * NU + i - 2))
            if nxt < 12 and i < 16 and i * 6 // 14 + 7 > nxt:
                chunk(s, nxt)
                nxt += 1
            elif 16 <= i < 48 and nxt < 18 and (i - 14) // 4 + 12 > nxt:
                chunk(s, nxt)
                nxt += 1
            elif late:
                t_unit("v", *late.pop())
            if s == 0 and i < A_HEADS:
                ev.append(("TA", 0, i))
            if i in (20, 50):
                ev.append(("N", s, "MA"[i // 50]))
            if 54 <= i < 54 + 2 * NT and i % 2 == 0:
                t_unit("o", s, (i - 54) // 2, 0)
        ev.append(("N", s, "B"))
        for c in range(18, NCH):
            chunk(s, c)
            if c == 18:
                for n in range(NT):
                    t_unit("o", s, n, 1)
        ev.append(("VAR", s))
        if s + 1 < NSEQ:
            inputs(s + 1, "m", range(MEM // P))
            inputs(s + 1, "x", range(NT))
    for t in range(NT):
        ev.append(("LN", NSEQ - 1, t))
    router(NSEQ - 1)
    return ev, tu[0]


EVENTS, N_TU = schedule()
FIN_ACT = 6
T_OF_UNIT = {e[3]: e[4] for e in EVENTS if e[0] == "T"}
T_OF_VALUES = {(e[1], *CHUNKS[e[2]]): e[3] for e in EVENTS if e[0] == "v"}
LAST_IN = [max(e[4] for e in EVENTS if e[0] in ("x", "m") and e[1] == s) for s in range(NSEQ)]
LAST_M = [max(e[4] for e in EVENTS if e[0] == "m" and e[1] == s) for s in range(NSEQ)]
LAST_OA = [max(e[4] for e in EVENTS if e[0] == "o" and e[1] == s and e[3] == 0) for s in range(NSEQ)]
LAST_O = [max(e[4] for e in EVENTS if e[0] == "o" and e[1] == s) for s in range(NSEQ)]
R_UNITS = {(s, t): [e[4] for e in EVENTS if e[0] == "r" and e[1:3] == (s, t)] for s in range(NSEQ) for t in range(NT)}


def build_kernel(nc, x, mem, w_in, w_mem_kv, sink, rpb, grp_g, w_out, ln1_g, ln1_b, w_router, router_bias,
                 w_gate, w_up, w_down, ln2_g, ln2_b, out):
    with ExitStack() as ctx:
        def sb(name, shape, dt=F32):
            return ctx.enter_context(nc.sbuf_tensor(name, shape, dt))

        def sem(name):
            return ctx.enter_context(nc.semaphore(name))

        def bank(name):
            return ctx.enter_context(nc.psum_tensor(name, [P, 512], F32))

        x1_dram = nc.dram_tensor("x1_dram", (TT * P, D), F32).ap()
        vbw_dram = nc.dram_tensor("vbw_dram", (NSEQ, 4, ROWS, BW, B_W), F32).ap()
        biasb_dram = nc.dram_tensor("biasb_dram", (12, 16, 15, BW), F32).ap()
        y_dram = nc.dram_tensor("y_dram", (SLOTS * P, D), F32).ap()
        pad_dram = nc.dram_tensor("pad_dram", (B_HEADS, 15, 64), F32).ap()

        R = sb("split_main", [P, 24576], F32R)
        RX = sb("split_aux", [P, 3072], F32R)

        def cut(t, at, *shape):
            n = 1
            for d in shape:
                n *= d
            ap = t[:, at:at + n]
            if len(shape) == 2:
                ap = ap.rearrange("p (a b) -> p a b", a=shape[0])
            if len(shape) == 3:
                ap = ap.rearrange("p (a b c) -> p a b c", a=shape[0], b=shape[1])
            return ap

        xT = [cut(R, 0, KD, S), cut(R, 4096, KD, S)]
        memT = [cut(R, 8192, KD, MEM), cut(R, 10240, KD, MEM)]
        qbT = [cut(R, 8192, 2, S), cut(R, 9216, 2, S)]
        kbT = [cut(R, 10240, 2, S), cut(R, 11264, 2, S)]
        wch = [cut(R, 12288, 2, KD, P), cut(R, 14336, 2, KD, P)]
        qaT = [cut(R, 16384, 4, S), cut(R, 18432, 4, S)]
        kaT = [cut(R, 20480, 1, S), cut(R, 20992, 1, S)]
        qmT = [cut(R, 21504, 2, S), cut(R, 22528, 2, S)]
        mkT = [cut(R, 23552, 2, MEM), cut(R, 24064, 2, MEM)]
        wu = [cut(R, 0, UNITS, 1024), cut(R, 12288, UNITS, 1024)]
        xgT = [cut(RX, 0, KD, P), cut(RX, 1024, KD, P)]
        hT = [cut(RX, 2048, KF, P), cut(RX, 2560, KF, P)]

        x_nat = sb("x_nat", [P, NT, D])
        mixing = sb("mixing", [P, UNITS * 1024])
        biasA = cut(mixing, 0, A_HEADS, 3 * P)
        biasB = cut(mixing, 3072, 12, 256)
        biasB_rows = mixing[:, 0:3072]
        wraw = mixing[:, 6144:8192].rearrange("p (a b c) -> p a b c", a=2, b=KD)
        o_sb = cut(mixing, 8192, NT, D)
        raw = cut(mixing, 0, UNITS, 1024)
        va = sb("va", [P, NT, A_KV])
        vbw = sb("vbw", [P, 8, B_W])
        mem_nat = vbw[:, :, :].rearrange("p (t a) b -> p t (a b)", t=2)
        mv = sb("mv", [P, 2, M_W])
        vstg = sb("vstg", [P, NT, B_W])
        x1T = [vstg[:, :, :].rearrange("p a (b c) -> p (a b) c", c=P),
               vbw[:, 0:4, :].rearrange("p a (b c) -> p (a b) c", c=P)]
        probs = sb("probs", [P, 2, 384])
        probsT = sb("probsT", [P, 2, 384])
        ln = sb("ln", [P, 2, D])
        ident = sb("ident", [P, P])
        anti = sb("anti", [P, P])
        ones_b = sb("ones_b", [P, P], BF16)
        tri_b = sb("tri_b", [P, P], BF16)
        wr = sb("wr", [P, KD, NE])
        gcol = sb("gcol", [P, KD])
        sinkb = sb("sinkb", [P, A_HEADS])
        nsink = sb("nsink", [P, A_HEADS])
        rbb = sb("rbb", [P, NE])
        negm = sb("negm", [P, 2, A_HEADS])
        sums = sb("sums", [P, 2, A_HEADS])
        es = sb("es", [P, 2, A_HEADS])
        rden = sb("rden", [P, 2, A_HEADS])
        stats = sb("stats", [P, TT, 2, 6])
        mvv = sb("mvv", [P, 12, 2])
        nv = sb("nv", [P, 12])
        ny = sb("ny", [P, 12])
        rstd = sb("rstd", [P, TT])
        nt_ = sb("nt_", [P, 12])
        sc = sb("sc", [P, TT, NE])
        idxc = sb("idxc", [P, 1], I32)
        idx = sb("idx", [P, SLOTS], I32)
        tiles_cum = sb("tiles_cum", [P, NE + 2], I32)
        slot_i = sb("slot_i", [P, 2, TT], I32)
        wts = sb("wts", [P, 2, TT])
        riota = sb("riota", [P, P])
        tokf = sb("tokf", [P, TT])
        mask_b = sb("mask_b", [P, TT * NE], BF16)
        carry = sb("carry", [1, 3])
        fin_bias = sb("fin_bias", [P, FIN_ACT])
        izero = sb("izero", [P, 1], I32)
        ints = sb("ints", [P, 32], I32)
        seed = sb("seed", [P, 12])
        scol = sb("scol", [P, 2], I32)

        dist = vstg[:, :, :].rearrange("p a b -> p (a b)")[:, 0:3 * P]
        mask = vstg[:, :, :].rearrange("p a b -> p (a b)")[:, 3 * P:6 * P]
        scratch = mixing[:, 8192:12288]
        vbw_flat = vbw[:, :, :].rearrange("p a b -> p (a b)")
        vT = vbw[:, 4:6, :]
        rowoh = vbw_flat[:, 0:TT * P].bitcast(BF16).rearrange("p (a b) -> p a b", a=2 * TT)
        tileoh = scratch[:, 2560:2560 + TT * 2 * SLOTS].bitcast(BF16).rearrange("p (a b) -> p a b", a=2 * TT)
        xg = x_nat[:, 0, :]
        y_sb = x_nat[:, 1, :]
        sg = x_nat[:, 2, 0:512]
        h_sb = x_nat[:, 3, 0:512]
        zeros = x_nat[:, 3, 512:1024]
        fin = [raw[:, t, :] for t in range(TT)]
        fin_rows = [[cut(R, (2 * t + c) * D, D).bitcast(F32) for c in range(2)] for t in range(TT)]

        Cb = [bank("C0"), bank("C1")]
        Tb = [bank("T0"), bank("T1")]
        Sb = [bank("S0"), bank("S1")]
        Ob = [bank("O0"), bank("O1")]

        x_loaded = [[sem(f"x_loaded{s}_{t}") for t in range(NT)] for s in range(NSEQ)]
        mem_loaded = [sem(f"mem_loaded{s}") for s in range(NSEQ)]
        small_loaded = sem("small_loaded")
        ln_loaded = sem("ln_loaded")
        ln2_loaded = sem("ln2_loaded")
        rpb_loaded = sem("rpb_loaded")
        pad_stored = sem("pad_stored")
        biasb_loaded = sem("biasb_loaded")
        biasb_spread = sem("biasb_spread")
        chunk_loaded = [sem("chunk_loaded0"), sem("chunk_loaded1")]
        chunk_scaled = sem("chunk_scaled")
        chunk_hi = sem("chunk_hi")
        chunk_lo = sem("chunk_lo")
        t_ready = [sem("t_ready0"), sem("t_ready1")]
        t_hi = sem("t_hi")
        t_drained = [sem("t_drained0"), sem("t_drained1")]
        c_ready = [sem("c_ready0"), sem("c_ready1")]
        c_hi = sem("c_hi")
        c_drained = [sem("c_drained0"), sem("c_drained1")]
        s_ready = [sem("s_ready0"), sem("s_ready1")]
        biased = sem("biased")
        maxed = sem("maxed")
        exped = sem("exped")
        pv_done = sem("pv_done")
        o_drained = [sem("o_drained0"), sem("o_drained1")]
        sink_in = sem("sink_in")
        sink_exp = sem("sink_exp")
        vb_stored = sem("vb_stored")
        vbw_loaded = sem("vbw_loaded")
        v_staged = sem("v_staged")
        wo_ready = sem("wo_ready")
        wo_drained = sem("wo_drained")
        x_again = [sem(f"x_again{t}") for t in range(NT)]
        mixed_done = sem("mixed_done")
        x1_ready = sem("x1_ready")
        x1_stored = sem("x1_stored")
        route_psum = sem("route_psum")
        sig_done = sem("sig_done")
        setup_pool = sem("setup_pool")
        setup_dve = sem("setup_dve")
        setup_pe = sem("setup_pe")
        dch = sem("dve_chain")
        pch = sem("pool_chain")
        mask_ready = sem("mask_ready")
        rank_done = sem("rank_done")
        onehot_ready = sem("onehot_ready")
        onehot_used = sem("onehot_used")
        idx_psum = sem("idx_psum")
        routed = sem("routed")
        raw_loaded = [sem(f"raw_loaded{i}") for i in range(UNITS)]
        unit_hi = sem("unit_hi")
        unit_lo_dve = sem("unit_lo_dve")
        unit_lo_pool = sem("unit_lo_pool")
        units_used = sem("units_used")
        xg_idx = sem("xg_idx")
        xg_loaded = sem("xg_loaded")
        xgT_psum = sem("xgT_psum")
        xgT_hi = sem("xgT_hi")
        xgT_lo = sem("xgT_lo")
        silu_done = sem("silu_done")
        h_mid = sem("h_mid")
        hT_psum = sem("hT_psum")
        hT_hi = sem("hT_hi")
        hT_lo = sem("hT_lo")
        y_half = [sem("y_half0"), sem("y_half1")]
        y_stored = sem("y_stored")
        y_zeroed = sem("y_zeroed")
        x1_back = [sem(f"x1_back{t}") for t in range(TT)]
        fin_loaded = [sem(f"fin_loaded{t}") for t in range(TT)]
        fin_scaled = sem("fin_scaled")
        fin_acc = sem("fin_acc")
        fin_norm = sem("fin_norm")
        fin_rstd = sem("fin_rstd")
        fin_y = sem("fin_y")
        fin_last = sem("fin_last")
        fin_gain = sem("fin_gain")
        out_stored = sem("out_stored")

        win_v = w_in.rearrange("(k p) c -> p k c", p=P)
        wkv_v = w_mem_kv.rearrange("(k p) c -> p k c", p=P)
        wo_v = w_out.rearrange("(k p) c -> p k c", p=P)

        chunk_src = {"mk": (wkv_v, 0), "mv": (wkv_v, M_W), "qm": (win_v, QM0), "ka": (win_v, KA0), "va": (win_v, VA0),
                     "qb": (win_v, QB0), "kb": (win_v, KB0), "vb": (win_v, VB0), "wo": (wo_v, 0)}

        def chunk_loads(g):
            n = 0
            for i in range(g % 2, g + 1, 2):
                n += 32 if CHUNKS[i % NCH][0] == "qa" else 16
            return n

        split_T = [e for e in EVENTS if e[0] in ("x", "m", "o")]
        T_HI = {e[4]: i + 1 for i, e in enumerate(split_T)}
        split_C = ("mk", "qm", "qa", "ka", "qb", "kb")
        C_HI = {}
        for s_ in range(NSEQ):
            for c_, (kind_, _) in enumerate(CHUNKS):
                if kind_ in split_C:
                    C_HI[s_ * NCH + c_] = len(C_HI) + 1
        C_OUT = {}
        for b in range(2):
            n_out = 0
            for cu in range(b, NSEQ * NCH, 2):
                n_out += CHUNKS[cu % NCH][0] != "wo"
                C_OUT[cu] = n_out
        V_TURNED = [e[3] for e in EVENTS if e[0] == "v"]
        V_UNITS = [c for c, (kind_, _) in enumerate(CHUNKS) if kind_ in VALUES]

        def wo_bank(half, t):
            return ([Sb[0], Sb[1], Ob[0], Ob[1]], [Cb[0], Cb[1], Sb[0], Sb[1]])[half][t]

        GI = {kn: i for i, kn in enumerate(GROUPS)}

        def group_of(s, i):
            k, n, h = UNIT_LIST[i]
            return s * len(GROUPS) + GI[(k, n)], h

        def t_waits(eng, last_unit):
            for b in range(2):
                eng.wait_ge(t_drained[b], (last_unit - b) // 2 + 1)

        def c_waits(eng, cu):
            for b in range(2):
                if cu - b >= 0:
                    eng.wait_ge(c_drained[b], C_OUT[cu - (cu - b) % 2])

        def by_pair(slot):
            return slot.rearrange("p (a b) c -> p a (b c)", a=2)

        def chunk_cu(s, kind, g):
            return s * NCH + CHUNKS.index((kind, g))

        def grid_view(xt, n):
            v = xt[:, 4:6, :].rearrange("p k (r c) -> p k r c", r=ROWS)
            return v[:, :, :, n * 16:(n + 1) * 16]

        def by_row(ap):
            return ap.rearrange("p (r n c) -> p r n c", r=ROWS, n=4)

        def by_block(ap):
            return ap.rearrange("p (n r c) -> p r n c", r=ROWS, n=4)

        def hT_part(part, i):
            return hT[part][:, 2 * i:2 * i + 2, :], Sb[i][:, 0:256].rearrange("p (k c) -> p k c", k=2)

        def c_dest(kind, g):
            t = {"mk": mkT, "qm": qmT, "qa": qaT, "ka": kaT, "qb": qbT, "kb": kbT}[kind]
            return [t[0][:, g, :], t[1][:, g, :]], (MEM if kind == "mk" else S)

        def act_copies(i):
            return i % 4 == 1 or i % 2 == (0 if UNIT_LIST[i][0] == "M" else 1)

        def copy_probs(eng, copy, s, i, a, u):
            kind, tile, h = UNIT_LIST[i]
            w = key_range(tile)[1] if kind == "A" else 256
            eng.wait_ge(t_ready[u % 2], u // 2 + 1)
            if a >= 2:
                eng.wait_ge(pv_done, a - 1)
            copy(probsT[:, a % 2, 0:w], Tb[u % 2][:, 0:w]).then_inc(t_drained[u % 2], 1)

        def normalise_groups(kind, link, rsqrt):
            g0 = GI[(kind, 0)]
            mv4, nv4 = mvv[:, g0:g0 + NT, :], nv[:, 0:NT]
            link(nc.vector.tensor_tensor(nv4, mv4[:, :, 0], mv4[:, :, 0], ALU.mult))
            link(nc.vector.scalar_tensor_tensor(nv4, nv4, EPS, mv4[:, :, 1], ALU.add, ALU.add))
            rsqrt(ny[:, 0:NT], NT)
            for tile in range(NT):
                c0, w = OCOL[kind], HEADS[kind] * HD
                ins = nc.vector.tensor_scalar(o_sb[:, tile, c0:c0 + w], o_sb[:, tile, c0:c0 + w],
                                              ny[:, tile:tile + 1], None, ALU.mult)
            ins.then_inc(mixed_done, 1)

        def routing(dve, link):
            G = TT * NG
            sel = cut(scratch, 0, TT, NE)
            w16 = [cut(scratch, 128 * i, G, EG) for i in range(8)]
            w32 = [scratch[:, 1024 + 32 * i:1024 + 32 * (i + 1)] for i in range(6)]
            w8 = [scratch[:, 1280 + 8 * i:1280 + 8 * (i + 1)] for i in range(8)]
            selv = w16[0]
            lo_p = scratch[:, 2176:2176 + SLOTS]
            rev4 = w16[7]
            thr = cut(scratch, 1408, NE, TT)
            one16, tnum = scratch[:, 1584:1600], scratch[:, 1648:1656]
            for i in range(EG):
                nc.vector.memset(rev4[:, :, i], float(EG - i))
            for i in range(TT):
                nc.vector.memset(thr[:, :, i], float(P * i))
            nc.vector.memset(one16, 1.0)
            link(nc.vector.tensor_scalar(tnum, tokf[:, :], tokf[:, 0:1], 1.0 / P, ALU.subtract, ALU.mult))
            dve.wait_ge(x1_stored, 16 * TT)
            dve.wait_ge(route_psum, TT)
            link(nc.vector.memset(zeros, 0.0))
            dve.wait_ge(sig_done, NSEQ)
            link(nc.vector.tensor_tensor(sel, sc[:, :, :], rbb[:, :].unsqueeze(1).to_broadcast([P, TT, NE]), ALU.add))

            def first_max(v, m, oh, rows, key, mk, rev):
                link(nc.vector.tensor_reduce(m, v, AX.X, ALU.max))
                link(nc.vector.tensor_tensor(key, v, m.unsqueeze(2).to_broadcast([P, rows, 4]), ALU.is_equal))
                link(nc.vector.tensor_tensor(key, key, rev, ALU.mult))
                link(nc.vector.tensor_reduce(mk, key, AX.X, ALU.max))
                link(nc.vector.tensor_tensor(oh, key, mk.unsqueeze(2).to_broadcast([P, rows, 4]), ALU.is_equal))

            m1, m2, mk = w32[0], w32[1], w32[2]
            oh1, oh2, key, sel2 = w16[1], w16[2], w16[3], w16[4]
            first_max(selv, m1, oh1, G, key, mk, rev4)
            link(nc.vector.scalar_tensor_tensor(sel2, oh1, MASKED, selv, ALU.mult, ALU.add))
            first_max(sel2, m2, oh2, G, key, mk, rev4)
            link(nc.vector.tensor_tensor(m1, m1, m2, ALU.add))
            gsc = m1.rearrange("p (t g) -> p t g", t=TT)
            gkey = w32[3].rearrange("p (t g) -> p t g", t=TT)
            goh = w32[4].rearrange("p (t g) -> p t g", t=TT)
            first_max(gsc, w8[0], goh, TT, gkey, w8[1], rev4[:, 0:TT, :])
            gb = w32[4].unsqueeze(2).to_broadcast([P, G, EG])
            link(nc.vector.tensor_tensor(oh1, oh1, gb, ALU.mult))
            link(nc.vector.tensor_tensor(oh2, oh2, gb, ALU.mult))
            link(nc.vector.tensor_tensor(cut(mask_b, 0, G, EG), oh1, oh2, ALU.add))
            nc.vector.memset(seed[:, 6:7], 0.0).then_inc(mask_ready, 1)

            E1, E2 = cut(scratch, 128, TT, NE), cut(scratch, 256, TT, NE)
            tmp = cut(scratch, 384, TT, NE)
            w_a, w_b, w_s = w8[2], w8[3], w8[4]
            link(nc.vector.tensor_tensor(tmp, E1, sc[:, :, :], ALU.mult))
            link(nc.vector.tensor_reduce(w_a, tmp, AX.X, ALU.add))
            link(nc.vector.tensor_tensor(tmp, E2, sc[:, :, :], ALU.mult))
            link(nc.vector.tensor_reduce(w_b, tmp, AX.X, ALU.add))
            link(nc.vector.tensor_tensor(w_s, w_a, w_b, ALU.add))
            link(nc.vector.reciprocal(w_s, w_s))
            link(nc.vector.tensor_tensor(wts[:, 0, :], w_a, w_s, ALU.mult))
            link(nc.vector.tensor_tensor(wts[:, 1, :], w_b, w_s, ALU.mult))

            dve.wait_ge(rank_done, 1)
            cmp = cut(scratch, 512, NE, TT)
            link(nc.vector.tensor_tensor(cmp, Ob[0][:, 128:128 + NE].unsqueeze(2).to_broadcast([P, NE, TT]), thr, ALU.is_gt))
            ntl, cum, base = (scratch[:, 1536 + 16 * i:1552 + 16 * i] for i in range(3))
            link(nc.vector.tensor_reduce(ntl, cmp, AX.X, ALU.add))
            link(nc.vector.tensor_scalar(ntl, ntl, 1.0, None, ALU.max))
            link(nc.vector.tensor_tensor_scan(cum, one16, ntl, 0.0, ALU.mult, ALU.add))
            link(nc.vector.tensor_tensor(base, cum, ntl, ALU.subtract))
            link(nc.vector.tensor_copy(tiles_cum[:, 0:NE], base))
            link(nc.vector.tensor_copy(tiles_cum[:, NE:NE + 1], cum[:, NE - 1:NE]))
            link(nc.vector.tensor_scalar(tiles_cum[:, NE + 1:NE + 2], cum[:, NE - 1:NE], -1.0, float(SLOTS),
                                         ALU.mult, ALU.add))
            link(nc.vector.tensor_scalar(base, base, float(P), None, ALU.mult))
            pos = cut(scratch, 640, TT, NE)
            link(nc.vector.tensor_tensor(pos, Ob[0][:, 0:TT * NE].rearrange("p (t e) -> p t e", t=TT),
                                         base.unsqueeze(1).to_broadcast([P, TT, NE]), ALU.add))
            slot_f = scratch[:, 1600:1616]
            for c, E in enumerate((E1, E2)):
                link(nc.vector.tensor_tensor(tmp, E, pos, ALU.mult))
                link(nc.vector.tensor_reduce(slot_f[:, c * TT:(c + 1) * TT], tmp, AX.X, ALU.add))
            link(nc.vector.tensor_copy(slot_i[:, :, :].rearrange("p c t -> p (c t)"), slot_f))
            hi_i, lo_i = ints[:, 0:16], ints[:, 16:32]
            flat = slot_i[:, :, :].rearrange("p c t -> p (c t)")
            link(nc.vector.tensor_scalar(hi_i, flat, 7, None, ALU.logical_shift_right))
            link(nc.vector.tensor_scalar(lo_i, flat, P - 1, None, ALU.bitwise_and))
            hi_f, lo_f = scratch[:, 1616:1632], scratch[:, 1632:1648]
            link(nc.vector.tensor_copy(hi_f, hi_i))
            link(nc.vector.tensor_copy(lo_f, lo_i))
            N2 = 2 * TT
            nc.vector.tensor_tensor(rowoh, riota[:, :].unsqueeze(1).to_broadcast([P, N2, P]),
                                    lo_f.unsqueeze(2).to_broadcast([P, N2, P]), ALU.is_equal)
            tile_eq = cut(scratch, 1664, N2, SLOTS)
            link(nc.vector.tensor_tensor(tile_eq, riota[:, 0:SLOTS].unsqueeze(1).to_broadcast([P, N2, SLOTS]),
                                         hi_f.unsqueeze(2).to_broadcast([P, N2, SLOTS]), ALU.is_equal))
            for c in range(2):
                nc.vector.tensor_tensor(tileoh[:, c * TT:(c + 1) * TT, 0:SLOTS], tile_eq[:, c * TT:(c + 1) * TT, :],
                                        tnum.unsqueeze(2).to_broadcast([P, TT, SLOTS]), ALU.mult)
            link(nc.vector.tensor_scalar(tileoh[:, :, SLOTS:2 * SLOTS], tile_eq, tokf[:, 0:1], None, ALU.mult))
            nc.vector.memset(seed[:, 5:6], 0.0).then_inc(onehot_ready, 1)
            dve.wait_ge(idx_psum, 1)
            link(nc.vector.tensor_copy(lo_p, Ob[1][:, SLOTS:2 * SLOTS]))
            link(nc.vector.scalar_tensor_tensor(idx[:, :], Ob[1][:, 0:SLOTS], float(P), lo_p, ALU.mult, ALU.add))
            nc.vector.memset(seed[:, 4:5], 0.0).then_inc(routed, 1)

        block = ctx.enter_context(nc.Block())

        @block.sync
        def _(sp):
            sp.dma_start(mem_nat, mem[0].rearrange("(t p) d -> p t d", p=P)).then_inc(mem_loaded[0], 16)

            def load_chunk(g):
                kind, i = CHUNKS[g % NCH]
                if g >= 2:
                    sp.wait_ge(chunk_lo, g - 1)
                slot = wraw[:, g % 2]
                if kind == "qa":
                    for half in range(2):
                        sp.dma_start(slot[:, :, half * HD:(half + 1) * HD],
                                     win_v[:, :, half * 256 + i * HD:half * 256 + (i + 1) * HD])\
                            .then_inc(chunk_loaded[g % 2], 16)
                else:
                    src, c0 = chunk_src[kind]
                    if kind == "wo":
                        half, pair = i // 4, i % 4
                        slot = by_pair(slot)
                        part = src[:, 2 * pair:2 * pair + 2, half * 512:(half + 1) * 512]
                    else:
                        part = src[:, :, c0 + i * P:c0 + (i + 1) * P]
                    sp.dma_start(slot, part).then_inc(chunk_loaded[g % 2], 16)

            def small_loads(stage):
                if stage == 1:
                    sp.dma_start(wr[:, :, :], w_router.rearrange("(k p) e -> p k e", p=P)).then_inc(small_loaded, 16)
                    sp.dma_start(gcol[:, :], grp_g).then_inc(small_loaded, 16)
                    sp.dma_start(sinkb[:, :], sink.partition_broadcast(P)).then_inc(small_loaded, 16)
                    sp.dma_start(rbb[:, :], router_bias.partition_broadcast(P)).then_inc(small_loaded, 16)
                    sp.wait_ge(setup_dve, 1)
                    sp.dma_start(o_sb[0:60, 0, 16:47], rpb.rearrange("h r c -> (h r) c")).then_inc(rpb_loaded, 16)
                elif stage == 2:
                    sp.wait_ge(rpb_loaded, 16)
                    sp.dma_start(pad_dram.rearrange("h r c -> (h r) c"), o_sb[0:60, 0, 0:64]).then_inc(pad_stored, 16)
                elif stage == 3:
                    sp.wait_ge(pad_stored, 16)
                    for h in range(B_HEADS):
                        for kind, delta in enumerate((0, -8, -16)):
                            src = bass.AP(pad_dram.tensor, h * 15 * 64 + 16 + delta, [[1, 16], [64, 15], [1, BW]])
                            sp.dma_start(biasb_dram[h * 3 + kind], src).then_inc(biasb_spread, 16)
                elif stage == 4:
                    sp.wait_ge(biasb_spread, 16 * 12)
                    for rr in range(ROWS):
                        sp.dma_start(biasB_rows[rr * 16:(rr + 1) * 16, :].rearrange("p (n c) -> p n c", c=256),
                                     biasb_dram[:, :, rr:rr + ROWS, :].rearrange("n i a b -> i n (a b)"))\
                            .then_inc(biasb_loaded, 16)
                elif stage == 8:
                    sp.dma_start(ln[:, 0, :], ln1_g.partition_broadcast(P)).then_inc(ln_loaded, 16)
                    sp.dma_start(ln[:, 1, :], ln1_b.partition_broadcast(P)).then_inc(ln_loaded, 16)

            for g in range(NSEQ * NCH):
                load_chunk(g)
                if g == 1:
                    for t in range(NT):
                        sp.dma_start(x_nat[:, t, :], x[0][t * P:(t + 1) * P, :]).then_inc(x_loaded[0][t], 16)
                small_loads(g)
                s, c = g // NCH, g % NCH
                if c == CHUNKS.index(("vb", 1)) + 2:
                    t_waits(sp, T_OF_VALUES[(s, "vb", 1)])
                    for w in range(4):
                        for odd in range(2):
                            p0 = odd * GRID_W + WIN0[w]
                            sp.dma_start(vbw_dram[s, w].rearrange("(t o) c d -> o c t d", o=2)[odd],
                                         vstg[p0:p0 + BW, :, :]).then_inc(vb_stored, 16)
                    sp.wait_ge(vb_stored, 16 * 8 * (s + 1))
                    sp.dma_start(vbw[:, :, :], vbw_dram[s].rearrange("w (h r) c d -> (r c) (w h) d", h=2))\
                        .then_inc(vbw_loaded, 16)

            def load_unit(e, w):
                if w < KD:
                    src = (w_gate, w_up)[w // 4][bass.ds(e, 1), (w % 4) * 2 * P:(w % 4 + 1) * 2 * P, :]
                    sp.dma_start(raw[:, w, :].rearrange("p (k c) -> p k c", k=2),
                                 src.rearrange("a (k p) c -> p (a k) c", p=P)).then_inc(raw_loaded[w], 16)
                else:
                    src = w_down[bass.ds(e, 1), (w - KD) * P:(w - KD + 1) * P, :]
                    sp.dma_start(raw[:, w, :], src.rearrange("a p c -> (a p) c")).then_inc(raw_loaded[w], 16)

            sp.wait_ge(biased, 2 * (32 + 16))
            for w in range(UNITS):
                if w == 6:
                    sp.wait_ge(chunk_lo, NSEQ * NCH)
                if w == KD:
                    sp.wait_ge(routed, 1)
                load_unit(0, w)
            with sp.Fori(1, NE) as e:
                for w in range(UNITS):
                    lo_sem, owned = (unit_lo_pool, POOL_LO) if w in POOL_LO else (unit_lo_dve, DVE_LO)
                    sp.wait_ge(lo_sem, e * len(owned) + owned.index(w) + 1)
                    load_unit(e, w)

            for t in range(TT):
                lo_sem, owned = (unit_lo_pool, POOL_LO) if t in POOL_LO else (unit_lo_dve, DVE_LO)
                sp.wait_ge(lo_sem, NE * len(owned) + owned.index(t) + 1)
                sp.dma_start(fin[t], x1_dram[t * P:(t + 1) * P, :]).then_inc(x1_back[t], 16)

            for t in range(TT):
                if t < TT - 1:
                    sp.wait_ge(fin_y, t + 1)
                else:
                    sp.wait_ge(fin_last, 1)
                sp.dma_start(out[t // NT][0, (t % NT) * P:(t % NT + 1) * P, :], fin[t]).then_inc(out_stored, 16)
            sp.wait_ge(out_stored, 16 * TT)

        @block.gpsimd
        def _(pool):
            n = [0]

            def link(i):
                n[0] += 1
                i.then_inc(pch, 1)
                pool.wait_ge(pch, n[0])

            link(nc.gpsimd.memset(ident[:, :], 0.0))
            link(nc.gpsimd.memset(anti[:, :], 0.0))
            link(nc.gpsimd.memset(izero[:, :], 0))
            nc.gpsimd.affine_select(out=ident[:, :], in_=ident[:, :], compare_op=ALU.not_equal, fill=1.0, base=0,
                                    pattern=[[-1, P]], channel_multiplier=1).then_inc(setup_pool, 1)
            nc.gpsimd.affine_select(out=anti[:, :], in_=anti[:, :], compare_op=ALU.not_equal, fill=1.0, base=-(P - 1),
                                    pattern=[[1, P]], channel_multiplier=1).then_inc(setup_pool, 1)
            nc.gpsimd.memset(ones_b[:, :], 1.0).then_inc(setup_pool, 1)
            pool.wait_ge(setup_pool, 3)
            nc.gpsimd.affine_select(out=tri_b[:, :], in_=ones_b[:, :], compare_op=ALU.is_gt, fill=0.0, base=0,
                                    pattern=[[1, P]], channel_multiplier=-1).then_inc(setup_pool, 1)
            nc.gpsimd.iota(dist, pattern=[[-1, 3 * P]], base=P, channel_multiplier=1,
                           allow_small_or_imprecise_dtypes=True).then_inc(setup_pool, 1)
            nc.gpsimd.iota(scol[:, 0:1], pattern=[[0, 1]], base=0, channel_multiplier=1).then_inc(setup_pool, 1)
            nc.gpsimd.iota(o_sb[:, 0, 64:96], pattern=[[1, BW]], base=0, channel_multiplier=0,
                           allow_small_or_imprecise_dtypes=True).then_inc(setup_pool, 1)
            nc.gpsimd.iota(riota[:, :], pattern=[[1, P]], base=0, channel_multiplier=0,
                           allow_small_or_imprecise_dtypes=True).then_inc(setup_pool, 1)
            nc.gpsimd.iota(tokf[:, :], pattern=[[P, TT]], base=0, channel_multiplier=1,
                           allow_small_or_imprecise_dtypes=True).then_inc(setup_pool, 1)

            def lo_chunk(g):
                kind, _ = CHUNKS[g % NCH]
                slot = g % 2
                if kind == "wo":
                    pool.wait_ge(chunk_loaded[slot], chunk_loads(g))
                    pool.wait_ge(small_loaded, 64)
                    pair = CHUNKS[g % NCH][1] % 4
                    w = by_pair(wraw[:, slot])
                    nc.gpsimd.tensor_tensor(w, w, gcol[:, 2 * pair:2 * pair + 2].unsqueeze(2).to_broadcast([P, 2, 512]),
                                            ALU.mult).then_inc(chunk_scaled, 1)
                pool.wait_ge(chunk_hi, g + 1)
                nc.gpsimd.tensor_tensor(wch[1][:, slot, :, :], wraw[:, slot], wch[0][:, slot, :, :].bitcast(F32),
                                        ALU.subtract).then_inc(chunk_lo, 1)

            def lo_first_expert():
                for w in range(KD):
                    pool.wait_ge(unit_hi, w + 1)
                    nc.gpsimd.tensor_tensor(wu[1][:, w, :], raw[:, w, :], wu[0][:, w, :].bitcast(F32),
                                            ALU.subtract).then_inc(unit_lo_pool if w in POOL_LO else unit_lo_dve, 1)

            for ev in EVENTS:
                what, s = ev[0], ev[1]
                if what == "C":
                    g = ev[3]
                    if g == 0:
                        lo_chunk(0)
                        lo_chunk(1)
                    if g + 2 < NSEQ * NCH:
                        lo_chunk(g + 2)
                elif what == "o" and s == 0 and ev[3] == 1:
                    t, u = ev[2], ev[4]
                    if t == 0:
                        for v in range(LAST_OA[0] - 1, LAST_OA[0] + 1):
                            pool.wait_ge(t_ready[v % 2], v // 2 + 1)
                        pool.wait_ge(pv_done, NU)
                        pool.dma_start(mem_nat, mem[1].rearrange("(t p) d -> p t d", p=P)).then_inc(mem_loaded[1], 16)
                    pool.wait_ge(t_ready[u % 2], u // 2 + 1)
                    pool.dma_start(o_sb[:, t, :], x[1][t * P:(t + 1) * P, :]).then_inc(x_loaded[1][t], 16)
                elif what == "LN":
                    t = ev[2]
                    pool.wait_ge(x1_ready, s * NT + t + 1)
                    pool.dma_start(x1_dram[(s * NT + t) * P:(s * NT + t + 1) * P, :], x_nat[:, t, :]).then_inc(x1_stored, 16)
                elif what == "R" and s == 0:
                    t = ev[2]
                    if t == 0:
                        pool.wait_ge(x1_stored, 16 * NT)
                    for u in R_UNITS[(0, t)]:
                        pool.wait_ge(t_ready[u % 2], u // 2 + 1)
                    pool.dma_start(x_nat[:, t, :], x[1][t * P:(t + 1) * P, :]).then_inc(x_again[t], 16)
            pool.dma_start(ln[:, 0, :], ln2_g.partition_broadcast(P)).then_inc(ln2_loaded, 16)
            pool.dma_start(ln[:, 1, :], ln2_b.partition_broadcast(P)).then_inc(ln2_loaded, 16)
            lo_first_expert()

            pool.wait_ge(routed, 1)

            def gather():
                nc.gpsimd.indirect_dma_start(xg, None, x1_dram, bass.IndirectOffsetOnAxis(idxc[:, 0:1], 0))\
                    .then_inc(xg_loaded, 16)

            def lo_units(e, ws):
                for w in ws:
                    pool.wait_ge(unit_hi, e * UNITS + w + 1)
                    nc.gpsimd.tensor_tensor(wu[1][:, w, :], raw[:, w, :], wu[0][:, w, :].bitcast(F32),
                                            ALU.subtract).then_inc(unit_lo_pool, 1)

            nc.gpsimd.tensor_copy(idxc[:, :], idx[:, 0:1]).then_inc(xg_idx, 1)
            pool.wait_ge(xg_idx, 1)
            gather()
            def next_gather(j):
                pool.wait_ge(xgT_psum, j + 1)
                nc.gpsimd.tensor_tensor(idxc[:, :], idx[:, bass.ds(j + 1, 1)], izero[:, :], ALU.add).then_inc(xg_idx, 1)
                pool.wait_ge(xg_idx, j + 2)
                nc.gpsimd.tensor_tensor(carry[:, 0:1], riota[0:1, 0:1], riota[0:1, 1:2], ALU.add)
                gather()

            def expert(e, last=False):
                lo = pool.value_load(tiles_cum[0:1, bass.ds(e, 1)], min_val=1, max_val=SLOTS - 2)
                hi = pool.value_load(tiles_cum[0:1, bass.ds(e + 1, 1)], min_val=1, max_val=SLOTS - 1)
                next_gather(lo)
                lo_units(e, late)
                with pool.If(lo + 1 < hi):
                    with pool.Fori(lo + 1, hi) as j:
                        next_gather(j)
                if not last:
                    lo_units(e + 1, early)

            early, late = [w for w in POOL_LO if w < 6], [w for w in POOL_LO if w >= 6]
            lo_units(0, late[1:])
            next_gather(0)
            first_hi = pool.value_load(tiles_cum[0:1, 1:2], min_val=1, max_val=SLOTS - 1)
            with pool.If(first_hi > 1):
                with pool.Fori(1, first_hi) as j:
                    next_gather(j)
            lo_units(1, early)
            with pool.Fori(1, NE - 1) as e:
                expert(e)
            expert(NE - 1, last=True)
            total = pool.value_load(tiles_cum[0:1, NE:NE + 1], min_val=1, max_val=SLOTS - 1)

            y_tiles = y_dram.rearrange("(j p) c -> j p c", p=P)
            with pool.Fori(total, SLOTS) as j:
                for half in range(2):
                    pool.dma_start(y_tiles[bass.ds(j, 1), :, half * 512:(half + 1) * 512].rearrange("a p c -> (a p) c"),
                                   zeros).then_inc(y_zeroed, 16)

            pool.wait_ge(xg_loaded, total * 16 + 16)
            nc.gpsimd.tensor_tensor(carry[:, 2:3], riota[0:1, 0:1], riota[0:1, 1:2], ALU.add)
            spare = pool.value_load(tiles_cum[0:1, NE + 1:NE + 2], min_val=1, max_val=SLOTS - NE)
            pool.wait_ge(y_zeroed, spare * 32)
            pool.wait_ge(y_stored, total * 16 + 16)
            nc.gpsimd.tensor_tensor(carry[:, 1:2], riota[0:1, 0:1], riota[0:1, 1:2], ALU.add)
            for t in range(TT):
                for c in range(2):
                    nc.gpsimd.indirect_dma_start(fin_rows[t][c], None, y_dram,
                                                 bass.IndirectOffsetOnAxis(slot_i[:, c, t:t + 1], 0))\
                        .then_inc(fin_loaded[t], 16)
            pool.wait_ge(ln2_loaded, 32)
            for t in range(TT - 1):
                pool.wait_ge(fin_rstd, t + 1)
                if t < FIN_ACT:
                    nc.gpsimd.tensor_tensor(fin[t], fin[t], ln[:, 0, :], ALU.mult).then_inc(fin_gain, 1)
                    pool.wait_ge(fin_gain, t + 1)
                nc.gpsimd.tensor_tensor(fin[t], fin[t], ln[:, 1, :], ALU.add).then_inc(fin_y, 1)

        @block.scalar
        def _(act):
            def hi_chunk(g):
                slot = g % 2
                kind, _ = CHUNKS[g % NCH]
                act.wait_ge(chunk_loaded[slot], chunk_loads(g))
                if kind == "wo":
                    act.wait_ge(chunk_scaled, (g // NCH) * 8 + CHUNKS[g % NCH][1] + 1)
                if g >= 2:
                    act.wait_ge(c_ready[slot], g // 2)
                nc.scalar.activation(wch[0][:, slot, :, :], wraw[:, slot], ACT.Copy).then_inc(chunk_hi, 1)

            def hi_units(cum_prev, e, ws):
                for w in ws:
                    act.wait_ge(raw_loaded[w], e * 16 + 16)
                    act.wait_ge(units_used, cum_prev * UNITS + w + 1)
                    nc.scalar.copy(wu[0][:, w, :], raw[:, w, :]).then_inc(unit_hi, 1)

            for ev in EVENTS:
                what, s = ev[0], ev[1]
                if what in ("x", "m", "o"):
                    t, b, u = ev[2], ev[3], ev[4]
                    act.wait_ge(t_ready[u % 2], u // 2 + 1)
                    src = Tb[u % 2][:, :].rearrange("p (k c) -> p k c", k=4)
                    if what == "o" and b == 1:
                        nc.scalar.activation(grid_view(xT[0], t), src[:, 0:2, :].rearrange("p k (r c) -> p k r c", r=ROWS),
                                             ACT.Copy)
                        nc.scalar.activation(xT[0][:, 6:8, t * P:(t + 1) * P], src[:, 2:4, :], ACT.Copy).then_inc(t_hi, 1)
                    else:
                        dst = (memT if what == "m" else xT)[0]
                        nc.scalar.activation(dst[:, 4 * b:4 * b + 4, t * P:(t + 1) * P], src, ACT.Copy).then_inc(t_hi, 1)
                elif what == "C":
                    c, cu = ev[2], ev[3]
                    kind, g = CHUNKS[c]
                    bnk = Cb[cu % 2]
                    if cu == 0:
                        hi_chunk(0)
                        hi_chunk(1)
                    if kind in VALUES:
                        width = MEM if kind == "mv" else S
                        act.wait_ge(c_ready[cu % 2], cu // 2 + 1)
                        done = s * len(V_UNITS) + V_UNITS.index(c)
                        if done:
                            u2 = V_TURNED[done - 1]
                            act.wait_ge(t_ready[u2 % 2], u2 // 2 + 1)
                        nc.scalar.activation(vT[:, 0:width // 256, :],
                                             bnk[:, 0:width].rearrange("p (a b) -> p a b", b=256), ACT.Copy)\
                            .then_inc(c_drained[cu % 2], 1)
                    if kind in split_C:
                        act.wait_ge(c_ready[cu % 2], cu // 2 + 1)
                        dst, width = c_dest(kind, g)
                        src = bnk[:, 0:width]
                        if kind == "qb":
                            dst, src = [by_block(dst[0])], by_row(src)
                        nc.scalar.activation(dst[0], src, ACT.Copy,
                                             scale=SCALE if kind[0] == "q" else 1.0).then_inc(c_hi, 1)
                    gg = s * NCH + c + 2
                    if gg < NSEQ * NCH:
                        hi_chunk(gg)
                elif what == "S":
                    i, a = ev[2], ev[3]
                    kind, tile, h = UNIT_LIST[i]
                    gi, hs = group_of(s, i)
                    if h == 0 and gi >= 2:
                        act.wait_ge(o_drained[gi % 2], gi // 2)
                    pr = probs[:, a % 2, :]
                    if kind == "M":
                        act.wait_ge(maxed, s * 16 + i + 1)
                        if a >= 2:
                            u2 = T_OF_UNIT[a - 2]
                            act.wait_ge(t_ready[u2 % 2], u2 // 2 + 1)
                        nc.scalar.activation(pr[:, 0:MEM], Sb[a % 2][:, 0:MEM], ACT.Exp, bias=negm[:, gi % 2, h:h + 1],
                                             accum_out=sums[:, gi % 2, h:h + 1]).then_inc(exped, 1)
                    else:
                        w = key_range(tile)[1] if kind == "A" else 256
                        act.wait_ge(biased, s * 48 + i - 16 + 1)
                        nc.scalar.activation(pr[:, 0:w], pr[:, 0:w], ACT.Exp, scale=-1.0,
                                             bias=negm[:, gi % 2, h:h + 1],
                                             accum_out=sums[:, gi % 2, h:h + 1]).then_inc(exped, 1)
                        if kind == "A" and h == A_HEADS - 1:
                            act.wait_ge(sink_in, s * NT + tile + 1)
                            nc.scalar.activation(es[:, gi % 2, :], es[:, gi % 2, :], ACT.Exp).then_inc(sink_exp, 1)
                elif what == "T":
                    i, a, u = ev[2], ev[3], ev[4]
                    if act_copies(i):
                        copy_probs(act, nc.scalar.copy, s, i, a, u)
                elif what == "r":
                    t, b, u = ev[2], ev[3], ev[4]
                    act.wait_ge(t_ready[u % 2], u // 2 + 1)
                    if t == 0 and b == 0:
                        act.wait_ge(vb_stored, 16 * 8 * (s + 1))
                    if s * NT + t >= 2:
                        act.wait_ge(route_psum, s * NT + t - 1)
                    nc.scalar.activation(x1T[t % 2][:, 4 * b:4 * b + 4, :], Tb[u % 2][:, :].rearrange("p (k c) -> p k c", k=4),
                                         ACT.Copy).then_inc(t_drained[u % 2], 1)
                elif what == "VAR" and s == NSEQ - 1:
                    for b in range(2):
                        act.wait_ge(c_ready[b], NSEQ * NCH // 2)
                    hi_units(0, 0, range(KD))
                elif what == "R" and ev[2] == NT - 1:
                    act.wait_ge(route_psum, (s + 1) * NT)
                    nc.scalar.activation(sc[:, s * NT:(s + 1) * NT, :],
                                         Ob[1][:, 0:NT * NE].rearrange("p (t e) -> p t e", t=NT),
                                         ACT.Sigmoid).then_inc(sig_done, 1)

            def xgT_his(j):
                act.wait_ge(xgT_psum, j + 1)
                for b in range(2):
                    ins = nc.scalar.copy(xgT[0][:, 4 * b:4 * b + 4, :], Tb[b][:, :].rearrange("p (k c) -> p k c", k=4))
                ins.then_inc(xgT_hi, 1)

            def tile_gate(n):
                act.wait_ge(units_used, n * UNITS + 4)
                act.wait_ge(h_mid, n * 2)
                nc.scalar.activation(sg, Cb[0][:, :], ACT.Silu).then_inc(silu_done, 1)

            def tile_hidden(n):
                for i in range(2):
                    act.wait_ge(hT_psum, n * 2 + i + 1)
                    dst, src = hT_part(0, i)
                    nc.scalar.copy(dst, src).then_inc(hT_hi, 1)
                xgT_his(n)

            def tile_last(n):
                act.wait_ge(units_used, n * UNITS + UNITS)
                act.wait_ge(y_stored, n * 16)
                for half in range(2):
                    nc.scalar.copy(y_sb[:, half * 512:(half + 1) * 512], Ob[half][:, :]).then_inc(y_half[half], 1)
                for half in range(2):
                    act.wait_ge(y_half[half], n + 1)
                act.dma_start(y_dram.rearrange("(j p) c -> j p c", p=P)[bass.ds(n - 1, 1)].rearrange("a p c -> (a p) c"),
                              y_sb).then_inc(y_stored, 16)

            def expert(e, first=False, last=False):
                lo = act.value_load(tiles_cum[0:1, bass.ds(e, 1)], min_val=0 if first else 1, max_val=SLOTS - 1)
                hi = act.value_load(tiles_cum[0:1, bass.ds(e + 1, 1)], min_val=1, max_val=SLOTS - 1)
                if not first:
                    hi_units(lo, e, range(6, UNITS))
                    tile_last(lo)
                if last:
                    with act.Fori(lo, hi) as j:
                        tile_gate(j + 1)
                        tile_hidden(j + 1)
                        tile_last(j + 1)
                    return
                with act.If(lo < hi - 1):
                    with act.Fori(lo, hi - 1) as j:
                        tile_gate(j + 1)
                        tile_hidden(j + 1)
                        tile_last(j + 1)
                hi_units(hi, e + 1, range(0, 4))
                tile_gate(hi)
                hi_units(hi, e + 1, range(4, 6))
                tile_hidden(hi)

            xgT_his(0)
            hi_units(0, 0, range(KD, UNITS))
            expert(0, first=True)
            with act.Fori(1, NE - 1) as e:
                expert(e)
            expert(NE - 1, last=True)

            for t in range(TT):
                act.wait_ge(x1_back[t], 16)
                nc.scalar.activation(fin[t], fin[t], ACT.Copy, scale=ALPHA).then_inc(fin_scaled, 1)
            for t in range(TT - 1):
                act.wait_ge(fin_norm, t + 1)
                if t < FIN_ACT:
                    nc.scalar.activation(fin[t], fin[t], ACT.Identity, bias=fin_bias[:, t:t + 1],
                                         scale=rstd[:, t:t + 1]).then_inc(fin_rstd, 1)
                    continue
                nc.scalar.activation(fin[t], fin[t], ACT.Copy, scale=rstd[:, t:t + 1]).then_inc(fin_rstd, 1)

        @block.vector
        def _(dve):
            n = [0]

            def link(i):
                n[0] += 1
                i.then_inc(dch, 1)
                dve.wait_ge(dch, n[0])

            def rsqrt(y, w):
                v, t = nv[:, 0:w], nt_[:, 0:w]
                link(nc.vector.tensor_scalar(t.bitcast(I32), v.bitcast(I32), 1, None, ALU.logical_shift_right))
                link(nc.vector.tensor_scalar(y.bitcast(I32), t.bitcast(I32), -1.0, float(0x5F3759DF), ALU.mult, ALU.add))
                for _ in range(3):
                    link(nc.vector.tensor_tensor(t, y, y, ALU.mult))
                    link(nc.vector.scalar_tensor_tensor(t, t, -0.5, v, ALU.mult, ALU.mult))
                    link(nc.vector.scalar_tensor_tensor(y, t, 1.5, y, ALU.add, ALU.mult))

            nc.vector.memset(o_sb[:, 0, 0:64], 0.0).then_inc(setup_dve, 1)
            for i, (sm, v) in enumerate(((units_used, UNITS), (unit_lo_dve, len(DVE_LO)), (unit_lo_pool, len(POOL_LO)),
                                         (h_mid, 2), (hT_psum, 2), (hT_hi, 2), (y_half[0], 1), (y_half[1], 1), (y_stored, 16))):
                nc.vector.memset(seed[:, i:i + 1], 0.0).then_inc(sm, v)
            dve.wait_ge(setup_pool, 9)
            link(nc.vector.scalar_tensor_tensor(dist, dist, -1.0, dist, ALU.mult, ALU.max))
            link(nc.vector.tensor_scalar(mask, dist, float(WINDOW), MASKED, ALU.is_gt, ALU.mult))
            link(nc.vector.tensor_scalar(scol[:, 1:2], scol[:, 0:1], 15, None, ALU.bitwise_and))
            link(nc.vector.tensor_copy(nv[:, 0:1], scol[:, 1:2]))
            d = o_sb[:, 0, 96:128]
            link(nc.vector.tensor_scalar(d, o_sb[:, 0, 64:96], nv[:, 0:1], None, ALU.subtract))
            gm = o_sb[:, 0, 128:224].rearrange("p (k c) -> p k c", k=3)
            link(nc.vector.tensor_scalar(gm[:, 0, 0:16], d[:, 0:16], -8.0, MASKED, ALU.is_lt, ALU.mult))
            link(nc.vector.tensor_scalar(gm[:, 0, 16:32], d[:, 16:32], 7.0, MASKED, ALU.is_gt, ALU.mult))
            link(nc.vector.tensor_scalar(gm[:, 1, :], d, 0.0, MASKED, ALU.is_lt, ALU.mult))
            link(nc.vector.tensor_scalar(o_sb[:, 0, 224:256], d, 15.0, MASKED, ALU.is_gt, ALU.mult))
            link(nc.vector.tensor_tensor(gm[:, 1, :], gm[:, 1, :], o_sb[:, 0, 224:256], ALU.add))
            link(nc.vector.tensor_scalar(gm[:, 2, 0:16], d[:, 0:16], 8.0, MASKED, ALU.is_lt, ALU.mult))
            link(nc.vector.tensor_scalar(gm[:, 2, 16:32], d[:, 16:32], 23.0, MASKED, ALU.is_gt, ALU.mult))

            def bias_b_tables():
                dve.wait_ge(small_loaded, 64)
                link(nc.vector.tensor_scalar(nsink[:, :], sinkb[:, :], -1.0, None, ALU.mult))
                for i in range(12):
                    kind = i % 3
                    bnk = Sb[(i // 2) % 2]
                    if i % 2 == 0:
                        dve.wait_ge(setup_pe, i // 2 + 1)
                    link(nc.vector.tensor_tensor(biasB[:, i, :].rearrange("p (r c) -> p r c", r=ROWS),
                                                 bnk[:, (i % 2) * 256:(i % 2 + 1) * 256].rearrange("p (r c) -> p r c", r=ROWS),
                                                 gm[:, kind, :].unsqueeze(1).to_broadcast([P, ROWS, BW]), ALU.add))
                    if i % 2 == 1:
                        nc.vector.memset(seed[:, 7:8], 0.0).then_inc(setup_dve, 1)
                        dve.wait_ge(setup_dve, 2 + i // 2)

            for ev in EVENTS:
                what, s = ev[0], ev[1]
                if what in ("x", "m", "o"):
                    t, b, u = ev[2], ev[3], ev[4]
                    dve.wait_ge(t_hi, T_HI[u])
                    src = Tb[u % 2][:, :].rearrange("p (k c) -> p k c", k=4)
                    if what == "o" and b == 1:
                        nc.vector.tensor_tensor(grid_view(xT[1], t), src[:, 0:2, :].rearrange("p k (r c) -> p k r c", r=ROWS),
                                                grid_view(xT[0], t).bitcast(F32), ALU.subtract)
                        nc.vector.tensor_tensor(xT[1][:, 6:8, t * P:(t + 1) * P], src[:, 2:4, :],
                                                xT[0][:, 6:8, t * P:(t + 1) * P].bitcast(F32), ALU.subtract)\
                            .then_inc(t_drained[u % 2], 1)
                    else:
                        tt = memT if what == "m" else xT
                        nc.vector.tensor_tensor(tt[1][:, 4 * b:4 * b + 4, t * P:(t + 1) * P], src,
                                                tt[0][:, 4 * b:4 * b + 4, t * P:(t + 1) * P].bitcast(F32),
                                                ALU.subtract).then_inc(t_drained[u % 2], 1)
                elif what == "BB":
                    bias_b_tables()
                elif what == "TA":
                    h = ev[2]
                    link(nc.vector.scalar_tensor_tensor(biasA[:, h, :], dist, -(2.0 ** -(h + 1)), mask, ALU.mult, ALU.add))
                elif what == "N":
                    normalise_groups(ev[2], link, rsqrt)
                elif what == "C":
                    c, cu = ev[2], ev[3]
                    kind, g = CHUNKS[c]
                    bnk = Cb[cu % 2]
                    if kind in split_C:
                        dst, width = c_dest(kind, g)
                        dve.wait_ge(c_hi, C_HI[cu])
                        if kind == "qb":
                            for blk in range(4):
                                ins = nc.vector.scalar_tensor_tensor(
                                    by_block(dst[1])[:, :, blk, :], by_row(bnk[:, :])[:, :, blk, :], SCALE,
                                    by_block(dst[0].bitcast(F32))[:, :, blk, :], ALU.mult, ALU.subtract)
                        else:
                            ins = nc.vector.scalar_tensor_tensor(dst[1], bnk[:, 0:width], SCALE if kind[0] == "q" else 1.0,
                                                                 dst[0].bitcast(F32), ALU.mult, ALU.subtract)
                        ins.then_inc(c_drained[cu % 2], 1)
                    elif kind == "wo" and g % 4 == 3:
                        half = g // 4
                        for t in range(NT):
                            if t < NT - 1:
                                dve.wait_ge(wo_ready, (s * 2 + half) * (NT - 1) + t + 1)
                            else:
                                dve.wait_ge(c_ready[cu % 2], cu // 2 + 1)
                            if s > 0:
                                dve.wait_ge(x_again[t], 16)
                            y = x_nat[:, t, half * 512:(half + 1) * 512]
                            nc.vector.scalar_tensor_tensor(y, y, ALPHA, wo_bank(half, t)[:, :], ALU.mult,
                                                           ALU.add).then_inc(wo_drained, 1)
                            dve.wait_ge(wo_drained, (s * 2 + half) * NT + t + 1)
                            link(nc.vector.bn_stats(stats[:, t, half, :], y))
                elif what == "v":
                    c, u = ev[2], ev[3]
                    kind, g = CHUNKS[c]
                    dve.wait_ge(t_ready[u % 2], u // 2 + 1)
                    if kind == "vb" and g == 0 and s > 0:
                        dve.wait_ge(vb_stored, 16 * 8)
                        dve.wait_ge(route_psum, NT)
                    width, dst = {"mv": (MEM, mv[:, :, g * P:(g + 1) * P]), "va": (S, va[:, :, :]),
                                  "vb": (S, vstg[:, :, g * P:(g + 1) * P])}[kind]
                    nc.vector.tensor_copy(dst, Tb[u % 2][:, 0:width].rearrange("p (t c) -> p t c", c=P))\
                        .then_inc(t_drained[u % 2], 1)
                elif what == "S":
                    i, a = ev[2], ev[3]
                    kind, tile, h = UNIT_LIST[i]
                    gi, _ = group_of(s, i)
                    dve.wait_ge(s_ready[a % 2], a // 2 + 1)
                    if kind == "M":
                        nc.vector.tensor_reduce(negm[:, gi % 2, h:h + 1], Sb[a % 2][:, 0:MEM], AX.X, ALU.max,
                                                negate=True).then_inc(maxed, 1)
                    else:
                        u2 = T_OF_UNIT[a - 2]
                        dve.wait_ge(t_ready[u2 % 2], u2 // 2 + 1)
                        if kind == "A":
                            head = (h // 2) + 4 * (h % 2)
                            k0, w = key_range(tile)
                            off = k0 - (tile - 1) * P
                            bias, start = biasA[:, head, off:off + w], nsink[:, head:head + 1]
                        else:
                            w = 256
                            bias, start = biasB[:, h * 3 + (0, 1, 1, 2)[tile], :], 3.0e38
                        nc.vector.tensor_tensor_reduce(out=probs[:, a % 2, 0:w], in0=Sb[a % 2][:, 0:w], in1=bias,
                                                       scale=-1.0, scalar=start, op0=ALU.add, op1=ALU.min,
                                                       accum_out=negm[:, gi % 2, h:h + 1]).then_inc(biased, 1)
                        if kind == "A" and h == A_HEADS - 1:
                            dve.wait_ge(biased, s * 48 + i - 16 + 1)
                            nc.vector.tensor_tensor(
                                es[:, gi % 2, :].rearrange("p (a b) -> p b a", b=2),
                                negm[:, gi % 2, :].rearrange("p (a b) -> p b a", b=2),
                                sinkb[:, :].rearrange("p (b a) -> p b a", b=2), ALU.add).then_inc(sink_in, 1)
                elif what == "T":
                    i, a, u = ev[2], ev[3], ev[4]
                    if not act_copies(i):
                        copy_probs(dve, nc.vector.tensor_copy, s, i, a, u)
                elif what == "PV":
                    i, a = ev[2], ev[3]
                    kind, tile, h = UNIT_LIST[i]
                    if h == HEADS[kind] - 1:
                        gi, _ = group_of(s, i)
                        nh = HEADS[kind]
                        den = sums[:, gi % 2, 0:nh]
                        dve.wait_ge(exped, a + 1)
                        if kind == "A":
                            dve.wait_ge(sink_exp, s * NT + tile + 1)
                            link(nc.vector.tensor_tensor(es[:, gi % 2, :], es[:, gi % 2, :], den, ALU.add))
                            den = es[:, gi % 2, :]
                        link(nc.vector.reciprocal(rden[:, gi % 2, 0:nh], den))
                        dve.wait_ge(pv_done, a + 1)
                        c0 = OCOL[kind]
                        dst = o_sb[:, tile, c0:c0 + nh * HD]
                        psv = Ob[gi % 2][:, 0:nh * HD]
                        rb = rden[:, gi % 2, 0:nh]
                        if kind == "A":
                            link(nc.vector.tensor_tensor(
                                dst.rearrange("p (b a d) -> p b a d", b=2, a=4),
                                psv.rearrange("p (a b d) -> p b a d", b=2, a=4),
                                rb.rearrange("p (a b) -> p b a", b=2).unsqueeze(3).to_broadcast([P, 2, 4, HD]),
                                ALU.mult))
                        else:
                            link(nc.vector.tensor_tensor(dst.rearrange("p (a d) -> p a d", a=nh),
                                                         psv.rearrange("p (a d) -> p a d", a=nh),
                                                         rb.unsqueeze(2).to_broadcast([P, nh, HD]), ALU.mult))
                        gl = gi % len(GROUPS)
                        nc.vector.bn_stats(stats[:, gl % TT, 0, :], dst).then_inc(o_drained[gi % 2], 1)
                        dve.wait_ge(o_drained[gi % 2], gi // 2 + 1)
                        link(nc.vector.bn_aggr(mvv[:, gl, :], stats[:, gl % TT, 0, :]))
                elif what == "VAR":
                    for t in range(NT):
                        link(nc.vector.bn_aggr(mvv[:, t, :], stats[:, t, :, :].rearrange("p a b -> p (a b)")))
                    link(nc.vector.tensor_scalar(nv[:, 0:NT], mvv[:, 0:NT, 1], EPS, None, ALU.add))
                    rsqrt(rstd[:, s * NT:(s + 1) * NT], NT)
                elif what == "LN":
                    t = ev[2]
                    if s == 0 and t == 0:
                        dve.wait_ge(ln_loaded, 32)
                    row = x_nat[:, t, :]
                    link(nc.vector.scalar_tensor_tensor(row, row, mvv[:, t, 0:1], ln[:, 0, :], ALU.subtract, ALU.mult))
                    nc.vector.scalar_tensor_tensor(row, row, rstd[:, s * NT + t:s * NT + t + 1], ln[:, 1, :],
                                                   ALU.mult, ALU.add).then_inc(x1_ready, 1)

            routing(dve, link)

            def lo_units(e, ws):
                for w in ws:
                    if w in POOL_LO:
                        continue
                    dve.wait_ge(unit_hi, e * UNITS + w + 1)
                    nc.vector.tensor_tensor(wu[1][:, w, :], raw[:, w, :], wu[0][:, w, :].bitcast(F32),
                                            ALU.subtract).then_inc(unit_lo_dve, 1)

            def xgT_los(j):
                dve.wait_ge(xgT_hi, j + 1)
                for b in range(2):
                    ins = nc.vector.tensor_tensor(xgT[1][:, 4 * b:4 * b + 4, :],
                                                  Tb[b][:, :].rearrange("p (k c) -> p k c", k=4),
                                                  xgT[0][:, 4 * b:4 * b + 4, :].bitcast(F32), ALU.subtract)
                ins.then_inc(xgT_lo, 1)

            def tile_first(n):
                dve.wait_ge(silu_done, n)
                dve.wait_ge(units_used, n * UNITS + KD)
                for i in range(2):
                    nc.vector.tensor_tensor(h_sb[:, i * 256:(i + 1) * 256], sg[:, i * 256:(i + 1) * 256],
                                            Cb[1][:, i * 256:(i + 1) * 256], ALU.mult).then_inc(h_mid, 1)
                for i in range(2):
                    dve.wait_ge(hT_hi, n * 2 + i + 1)
                    dst, src = hT_part(1, i)
                    nc.vector.tensor_tensor(dst, src, hT_part(0, i)[0].bitcast(F32), ALU.subtract).then_inc(hT_lo, 1)
                xgT_los(n)

            def expert(e, first=False, last=False):
                lo = dve.value_load(tiles_cum[0:1, bass.ds(e, 1)], min_val=0 if first else 1, max_val=SLOTS - 1)
                hi = dve.value_load(tiles_cum[0:1, bass.ds(e + 1, 1)], min_val=1, max_val=SLOTS - 1)
                if not first:
                    lo_units(e, range(5, UNITS))
                if last:
                    with dve.Fori(lo, hi) as j:
                        tile_first(j + 1)
                    return
                with dve.If(lo < hi - 1):
                    with dve.Fori(lo, hi - 1) as j:
                        tile_first(j + 1)
                lo_units(e + 1, range(0, 5))
                tile_first(hi)

            xgT_los(0)
            dve.wait_ge(unit_lo_dve, len(DVE_LO) + sum(w < KD for w in DVE_LO))
            lo_units(0, range(KD, UNITS))
            expert(0, first=True)
            with dve.Fori(1, NE - 1) as e:
                expert(e)
            expert(NE - 1, last=True)

            dve.wait_ge(ln2_loaded, 32)
            for t0 in range(0, TT, 2):
                for t in (t0, t0 + 1):
                    dve.wait_ge(fin_loaded[t], 32)
                    dve.wait_ge(fin_scaled, t + 1)
                    o = fin[t]
                    link(nc.vector.scalar_tensor_tensor(o, fin_rows[t][0], wts[:, 0, t:t + 1], o, ALU.mult, ALU.add))
                    nc.vector.scalar_tensor_tensor(o, fin_rows[t][1], wts[:, 1, t:t + 1], o, ALU.mult, ALU.add)\
                        .then_inc(fin_acc, 1)
                    dve.wait_ge(fin_acc, t + 1)
                    nc.vector.bn_stats(stats[:, t, 0, :], o[:, 0:512])
                    link(nc.vector.bn_stats(stats[:, t, 1, :], o[:, 512:1024]))
                    link(nc.vector.bn_aggr(mvv[:, t, :], stats[:, t, :, :].rearrange("p a b -> p (a b)")))
                link(nc.vector.tensor_scalar(nv[:, 0:2], mvv[:, t0:t0 + 2, 1], EPS, None, ALU.add))
                rsqrt(rstd[:, t0:t0 + 2], 2)
                if t0 < FIN_ACT:
                    nc.vector.scalar_tensor_tensor(fin_bias[:, t0:t0 + 2], mvv[:, t0:t0 + 2, 0], -1.0,
                                                   rstd[:, t0:t0 + 2], ALU.mult, ALU.mult).then_inc(fin_norm, 2)
                    continue
                for t in (t0, t0 + 1):
                    o = fin[t]
                    nc.vector.scalar_tensor_tensor(o, o, mvv[:, t, 0:1], ln[:, 0, :], ALU.subtract, ALU.mult)\
                        .then_inc(fin_norm, 1)
            dve.wait_ge(fin_norm, TT)
            nc.vector.scalar_tensor_tensor(fin[-1], fin[-1], rstd[:, TT - 1:TT], ln[:, 1, :], ALU.mult, ALU.add)\
                .then_inc(fin_last, 1)

        @block.tensor
        def _(pe):
            pe.wait_ge(setup_pool, 2)

            def three(out_ap, st, mvg, first, last, last_sem=None):
                ins = nc.tensor.matmul(out_ap, st[0], mvg[0], start=first, stop=False)
                ins = nc.tensor.matmul(out_ap, st[0], mvg[1], start=False, stop=False)
                ins = nc.tensor.matmul(out_ap, st[1], mvg[0], start=False, stop=last)
                return ins

            def bias_b_reverse():
                pe.wait_ge(biasb_loaded, 16 * ROWS)
                for i in range(6):
                    if i >= 2:
                        pe.wait_ge(setup_dve, i)
                    nc.tensor.matmul(Sb[i % 2][:, :], anti[:, :], biasB_rows[:, i * 512:(i + 1) * 512],
                                     start=True, stop=True).then_inc(setup_pe, 1)

            for ev in EVENTS:
                what, s = ev[0], ev[1]
                if what in ("x", "m", "o", "r"):
                    t, b, u = ev[2], ev[3], ev[4]
                    if u >= 2:
                        pe.wait_ge(t_drained[u % 2], u // 2)
                    if what == "x":
                        pe.wait_ge(x_loaded[s][t], 16)
                        src = (o_sb if s else x_nat)[:, t, :]
                    elif what == "m":
                        pe.wait_ge(mem_loaded[s], 16)
                        src = mem_nat[:, t, :]
                    elif what == "o":
                        pe.wait_ge(mixed_done, s * 3 + 2 + b)
                        src = o_sb[:, t, :]
                    else:
                        pe.wait_ge(x1_ready, s * NT + t + 1)
                        src = x_nat[:, t, :]
                    for k in range(4):
                        ins = nc.tensor.transpose(Tb[u % 2][:, k * P:(k + 1) * P],
                                                  src[:, (4 * b + k) * P:(4 * b + k + 1) * P], ident[:, :])
                    ins.then_inc(t_ready[u % 2], 1)
                elif what == "BB":
                    bias_b_reverse()
                elif what == "v":
                    c, u = ev[2], ev[3]
                    pe.wait_ge(t_drained[u % 2], u // 2)
                    pe.wait_ge(c_drained[c % 2], C_OUT[s * NCH + c])
                    for t in range((MEM if CHUNKS[c][0] == "mv" else S) // P):
                        ins = nc.tensor.transpose(Tb[u % 2][:, t * P:(t + 1) * P],
                                                  vT[:, t // 2, (t % 2) * P:(t % 2 + 1) * P], ident[:, :])
                    ins.then_inc(t_ready[u % 2], 1)
                elif what == "C":
                    c, cu = ev[2], ev[3]
                    kind, g = CHUNKS[c]
                    gg = s * NCH + c
                    sl = gg % 2
                    pe.wait_ge(chunk_lo, gg + 1)
                    if cu >= 2 and kind != "wo":
                        pe.wait_ge(c_drained[cu % 2], C_OUT[cu - 2])
                    if c == 0:
                        t_waits(pe, LAST_M[s])
                        if s > 0:
                            pe.wait_ge(wo_drained, s * 2 * NT)
                    if kind == "qm" and g == 0:
                        t_waits(pe, LAST_IN[s])
                    if kind == "wo" and g == 0:
                        t_waits(pe, LAST_OA[s])
                        pe.wait_ge(biased, (s + 1) * 48)
                        for b in range(2):
                            pe.wait_ge(o_drained[b], (s + 1) * len(GROUPS) // 2)
                    if kind == "wo" and g == 2:
                        t_waits(pe, LAST_O[s])
                    W = [wch[0][:, sl], wch[1][:, sl]]
                    bnk = Cb[cu % 2]
                    if kind == "wo":
                        half, pair = g // 4, g % 4
                        Wp = [by_pair(w_) for w_ in W]
                        for t in range(NT):
                            if pair == 0 and half == 0 and t == 0:
                                c_waits(pe, s * NCH + NCH - 9)
                            if pair == 0 and half == 1 and t >= 2:
                                pe.wait_ge(wo_drained, s * 2 * NT + t - 1)
                            for k in range(2):
                                kk = 2 * pair + k
                                ins = three(wo_bank(half, t)[:, :],
                                            [xT[0][:, kk, t * P:(t + 1) * P], xT[1][:, kk, t * P:(t + 1) * P]],
                                            [Wp[0][:, k, :], Wp[1][:, k, :]], kk == 0, kk == KD - 1)
                            if pair == 3 and t < NT - 1:
                                ins.then_inc(wo_ready, 1)
                    else:
                        src = memT if kind in ("mk", "mv") else xT
                        width = MEM if kind in ("mk", "mv") else S
                        for k in range(KD):
                            ins = three(bnk[:, 0:width], [W[0][:, k, :], W[1][:, k, :]],
                                        [src[0][:, k, :], src[1][:, k, :]], k == 0, k == KD - 1)
                    ins.then_inc(c_ready[cu % 2], 1)
                elif what == "S":
                    i, a = ev[2], ev[3]
                    kind, tile, h = UNIT_LIST[i]
                    if a == 0:
                        pe.wait_ge(setup_dve, 7)
                    if a >= 2:
                        s2, i2 = (a - 2) // NU, (a - 2) % NU
                        if UNIT_LIST[i2][0] == "M":
                            pe.wait_ge(exped, a - 1)
                        else:
                            pe.wait_ge(biased, s2 * 48 + i2 - 16 + 1)
                    if h == 0 and tile == 0:
                        c_waits(pe, s * NCH + {"M": 5, "A": 11, "B": 15}[kind])
                    bnk = Sb[a % 2]
                    if kind == "M":
                        lo_p = (h % 2) * HD
                        q = [t_[lo_p:lo_p + HD, h // 2, tile * P:(tile + 1) * P] for t_ in qmT]
                        kk = [t_[lo_p:lo_p + HD, h // 2, :] for t_ in mkT]
                        o = bnk[:, 0:MEM]
                    elif kind == "A":
                        lo_p = (h % 2) * HD
                        k0, w = key_range(tile)
                        q = [t_[lo_p:lo_p + HD, h // 2, tile * P:(tile + 1) * P] for t_ in qaT]
                        kk = [t_[lo_p:lo_p + HD, 0, k0:k0 + w] for t_ in kaT]
                        o = bnk[:, 0:w]
                    else:
                        lo_p = (h % 2) * HD
                        q = [t_[lo_p:lo_p + HD, h // 2, tile * P:(tile + 1) * P] for t_ in qbT]
                        kk = [t_[lo_p:lo_p + HD, h // 2, :].rearrange("p (r c) -> p r c", r=ROWS)
                              [:, :, WIN0[tile]:WIN0[tile] + BW] for t_ in kbT]
                        o = bnk[:, 0:256]
                    three(o, q, kk, True, True).then_inc(s_ready[a % 2], 1)
                elif what == "T":
                    i, a, u = ev[2], ev[3], ev[4]
                    kind, tile, h = UNIT_LIST[i]
                    w = key_range(tile)[1] if kind == "A" else 256
                    pe.wait_ge(exped, a + 1)
                    if u >= 2:
                        pe.wait_ge(t_drained[u % 2], u // 2)
                    for k in range(w // P):
                        ins = nc.tensor.transpose(Tb[u % 2][:, k * P:(k + 1) * P], probs[:, a % 2, k * P:(k + 1) * P],
                                                  ident[:, :])
                    ins.then_inc(t_ready[u % 2], 1)
                elif what == "PV":
                    i, a = ev[2], ev[3]
                    kind, tile, h = UNIT_LIST[i]
                    gi, _ = group_of(s, i)
                    u = T_OF_UNIT[a]
                    pe.wait_ge(t_drained[u % 2], u // 2 + 1)
                    if h == 0 and gi >= 2:
                        pe.wait_ge(o_drained[gi % 2], gi // 2)
                    if s == 1 and i == 0:
                        pe.wait_ge(sig_done, 1)
                    if kind == "M":
                        vs = [mv[:, k, h * HD:(h + 1) * HD] for k in range(2)]
                    elif kind == "A":
                        k0, w = key_range(tile)
                        vs = [va[:, k0 // P + k, (h % 2) * HD:(h % 2 + 1) * HD] for k in range(w // P)]
                    else:
                        if h == 0 and tile == 0:
                            pe.wait_ge(vbw_loaded, 16 * (s + 1))
                        vs = [vbw[:, 2 * tile + k, h * HD:(h + 1) * HD] for k in range(2)]
                    for k, v in enumerate(vs):
                        ins = nc.tensor.matmul(Ob[gi % 2][:, h * HD:(h + 1) * HD], probsT[:, a % 2, k * P:(k + 1) * P], v,
                                               start=(k == 0), stop=(k == len(vs) - 1))
                    ins.then_inc(pv_done, 1)
                elif what == "R":
                    t = ev[2]
                    for u in R_UNITS[(s, t)]:
                        pe.wait_ge(t_drained[u % 2], u // 2 + 1)
                    if t == 0:
                        pe.wait_ge(small_loaded, 64)
                        pe.wait_ge(o_drained[1], (s + 1) * len(GROUPS) // 2)
                    for k in range(KD):
                        ins = nc.tensor.matmul(Ob[1][:, t * NE:(t + 1) * NE], x1T[t % 2][:, k, :], wr[:, k, :],
                                               start=(k == 0), stop=(k == KD - 1))
                    ins.then_inc(route_psum, 1)

            pe.wait_ge(mask_ready, 1)
            m = mask_b[:, :].rearrange("p (t e) -> p t e", t=TT)
            for i in range(TT):
                for k in range(i):
                    nc.tensor.matmul(Ob[0][:, i * NE:(i + 1) * NE], ones_b[:, :], m[:, k, :], start=(k == 0), stop=False)
                nc.tensor.matmul(Ob[0][:, i * NE:(i + 1) * NE], tri_b[:, :], m[:, i, :], start=(i == 0), stop=True)
            for k in range(TT):
                ins = nc.tensor.matmul(Ob[0][:, TT * NE:TT * NE + NE], ones_b[:, :], m[:, k, :], start=(k == 0),
                                       stop=(k == TT - 1))
            ins.then_inc(rank_done, 1)
            pe.wait_ge(onehot_ready, 1)
            for i in range(2 * TT):
                ins = nc.tensor.matmul(Ob[1][:, 0:2 * SLOTS], rowoh[:, i, :], tileoh[:, i, :], start=(i == 0),
                                       stop=(i == 2 * TT - 1))
            ins.then_inc(idx_psum, 1)

            def transpose_rows(j):
                pe.wait_ge(xg_loaded, j * 16 + 16)
                for k in range(KD):
                    ins = nc.tensor.transpose(Tb[k // 4][:, (k % 4) * P:(k % 4 + 1) * P], xg[:, k * P:(k + 1) * P], ident[:, :])
                ins.then_inc(xgT_psum, 1)

            def unit_wait(e, w):
                lo_sem, owned = (unit_lo_pool, POOL_LO) if w in POOL_LO else (unit_lo_dve, DVE_LO)
                pe.wait_ge(lo_sem, e * len(owned) + len(owned) + owned.index(w) + 1)

            pe.wait_ge(routed, 1)
            transpose_rows(0)
            with pe.Fori(0, NE) as e:
                lo = pe.value_load(tiles_cum[0:1, bass.ds(e, 1)], min_val=0, max_val=SLOTS - 1)
                hi = pe.value_load(tiles_cum[0:1, bass.ds(e + 1, 1)], min_val=1, max_val=SLOTS - 1)
                with pe.Fori(lo, hi) as j:
                    pe.wait_ge(xgT_lo, j + 1)
                    for w in range(KD):
                        unit_wait(e, w)
                        for k in range(2 * (w % 4), 2 * (w % 4) + 2):
                            ins = three(Cb[w // 4][:, :], [xgT[0][:, k, :], xgT[1][:, k, :]],
                                        [wu[b_][:, w, (k % 2) * 512:(k % 2 + 1) * 512] for b_ in range(2)],
                                        k == 0, k == KD - 1)
                        ins.then_inc(units_used, 1)
                    transpose_rows(j + 1)
                    for i in range(2):
                        pe.wait_ge(h_mid, j * 2 + 2 + i + 1)
                        for f in range(2):
                            ins = nc.tensor.transpose(Sb[i][:, f * P:(f + 1) * P],
                                                      h_sb[:, (2 * i + f) * P:(2 * i + f + 1) * P], ident[:, :])
                        ins.then_inc(hT_psum, 1)
                    pe.wait_ge(y_half[0], j + 1)
                    pe.wait_ge(y_half[1], j + 1)
                    for f in range(KF):
                        unit_wait(e, KD + f)
                        pe.wait_ge(hT_lo, j * 2 + f // 2 + 1)
                        st = [hT[0][:, f, :], hT[1][:, f, :]]
                        for a_, b_ in ((0, 0), (0, 1), (1, 0)):
                            for half in range(2):
                                ins = nc.tensor.matmul(Ob[half][:, :], st[a_], wu[b_][:, KD + f, half * 512:(half + 1) * 512],
                                                       start=(f == 0 and a_ + b_ == 0), stop=(f == KF - 1 and a_ == 1))
                        ins.then_inc(units_used, 1)


_INS = ["x", "mem", "w_in", "w_mem_kv", "sink", "rpb", "grp_g", "w_out", "ln1_g", "ln1_b", "w_router", "router_bias",
        "w_gate", "w_up", "w_down", "ln2_g", "ln2_b"]


def kernel(x_prompt, x_sample, mem_prompt, mem_sample, w_in, w_mem_kv, sink_logits, rpb, grp_norm_g, w_out,
           ln1_g, ln1_b, w_router, router_bias, w_gate, w_up, w_down, ln2_g, ln2_b):
    import concourse.bacc as bacc
    import numpy as np
    from concourse.bass_utils import run_bass_kernel_spmd

    nc = bacc.Bacc("TRN2", target_bir_lowering=False, num_devices=1)
    given = {
        "x0": x_prompt, "x1": x_sample, "mem0": mem_prompt, "mem1": mem_sample, "w_in": w_in[0],
        "w_mem_kv": w_mem_kv[0], "sink": sink_logits[0], "rpb": rpb[0], "grp_g": np.asarray(grp_norm_g[0]).reshape(KD, P).T, "w_out": w_out[0],
        "ln1_g": ln1_g[0], "ln1_b": ln1_b[0], "w_router": w_router, "router_bias": router_bias,
        "w_gate": w_gate[0], "w_up": w_up[0], "w_down": w_down[0], "ln2_g": ln2_g[0], "ln2_b": ln2_b[0]}
    arrays, aps = {}, {}
    for name, a in given.items():
        a = np.ascontiguousarray(a)
        arrays[f"in_{name}"] = a
        aps[name] = nc.dram_tensor(f"in_{name}", a.shape, mybir.dt.from_np(a.dtype), kind="ExternalInput").ap()
    outs = [nc.dram_tensor(f"out_{s}", (1, S, D), F32, kind="ExternalOutput").ap() for s in range(NSEQ)]
    aps["x"] = [aps.pop("x0")[0], aps.pop("x1")[0]]
    aps["mem"] = [aps.pop("mem0")[0], aps.pop("mem1")[0]]
    build_kernel(nc, *[aps[n] for n in _INS], outs)
    r = run_bass_kernel_spmd(nc, [arrays], core_ids=[0]).results[0]
    return r["out_0"], r["out_1"]
```
